# Optimizing a Trainium2 kernel written in Bass

```python
import jax, jax.numpy as jnp
from jax import lax
import numpy as np
import math

D_MODEL = 1024
BATCH = 1
SEQ = 256
DEPTH = 1

D_MIX = D_MODEL
HEAD_DIM = 64
D_RWKV = D_MIX // 2
D_NSA = D_MIX - D_RWKV
RWKV_HEADS = D_RWKV // HEAD_DIM
NSA_Q_HEADS = D_NSA // HEAD_DIM
NSA_KV_HEADS = 2
NSA_GROUP = NSA_Q_HEADS // NSA_KV_HEADS
D_KV = NSA_KV_HEADS * HEAD_DIM
LORA_W = 64
LORA_A = 64
LORA_G = 128
RWKV_SIZES = (D_RWKV, D_RWKV, D_RWKV, LORA_W, LORA_A, LORA_G)
N_RWKV_COLS = sum(RWKV_SIZES)
CMP_BLOCK = 32
CMP_STRIDE = 16
CMP_HIDDEN = 256
SEL_BLOCK = 64
SEL_TOPK = 16
WINDOW = 512
Q_BLOCK = 128
NSA_SIZES = (D_NSA, D_KV, D_KV, D_KV, D_KV, D_KV, D_KV, 3 * NSA_Q_HEADS)
N_NSA_COLS = sum(NSA_SIZES)
N_IN = N_RWKV_COLS + N_NSA_COLS
D_FF = -(-8 * D_MODEL // (3 * 256)) * 256
NORM_EPS = 1e-6
GN_EPS = 64e-5
NEG = -1e30
BIG = 1e30


def _split(z, sizes):
    return jnp.split(z, [int(c) for c in np.cumsum(sizes)[:-1]], axis=-1)

def rms_norm(x, g):
    xf = x.astype(jnp.float32)
    y = xf * lax.rsqrt(jnp.mean(xf * xf, axis=-1, keepdims=True) + NORM_EPS)
    return (y * g).astype(x.dtype)

def alibi_slopes(n_heads):
    return 2.0 ** (-8.0 * jnp.arange(1, n_heads + 1, dtype=jnp.float32) / n_heads)

def swiglu(x, w_gate, w_up, w_down):
    return (jax.nn.silu(x @ w_gate) * (x @ w_up)) @ w_down

def rwkv7_time_mix(p, mu, w0, w2, a0, a2, g2, k_k, k_a, r_k, lnx_w, lnx_b):
    B, T, _ = p.shape
    H, N = RWKV_HEADS, HEAD_DIM
    p = p.astype(jnp.float32)
    p_prev = jnp.pad(p, ((0, 0), (1, 0), (0, 0)))[:, :-1]
    p = p + mu * (p_prev - p)
    r, k, v, dw, da, dg = _split(p, RWKV_SIZES)
    w_log = -jax.nn.softplus(-(w0 + jnp.tanh(dw) @ w2)) - 0.5
    decay = jnp.exp(-jnp.exp(w_log))
    a = jax.nn.sigmoid(a0 + da @ a2)
    g = jax.nn.sigmoid(dg) @ g2
    heads = lambda z: z.reshape(B, T, H, N)
    kk = heads(k * k_k)
    kk = kk / jnp.maximum(jnp.sqrt(jnp.sum(kk * kk, axis=-1, keepdims=True)), 1e-12)
    k = k * (1.0 + (a - 1.0) * k_a)
    r, k, v, decay, a = map(heads, (r, k, v, decay, a))
    xs = tuple(jnp.moveaxis(z, 1, 0) for z in (r, decay, k, v, -kk, kk * a))

    def step(S, inp):
        r_t, w_t, k_t, v_t, a_t, b_t = inp
        sa = jnp.einsum('bhvk,bhk->bhv', S, a_t)
        S = S * w_t[:, :, None, :] + sa[..., None] * b_t[:, :, None, :] + v_t[..., None] * k_t[:, :, None, :]
        return S, jnp.einsum('bhvk,bhk->bhv', S, r_t)

    S0 = jnp.zeros((B, H, N, N), jnp.float32)
    _, y = lax.scan(step, S0, xs)
    y = jnp.moveaxis(y, 0, 1)
    mean = jnp.mean(y, axis=-1, keepdims=True)
    var = jnp.mean(jnp.square(y - mean), axis=-1, keepdims=True)
    y = ((y - mean) * lax.rsqrt(var + GN_EPS)).reshape(B, T, D_RWKV) * lnx_w + lnx_b
    bonus = jnp.sum(r * k * r_k, axis=-1, keepdims=True) * v
    return (y + bonus.reshape(B, T, D_RWKV)) * g

def nsa_attention(p, pe_k, pe_v, ck1, ck2, cv1, cv2):
    B, T, _ = p.shape
    Hk, G, dk = NSA_KV_HEADS, NSA_GROUP, HEAD_DIM
    p = p.astype(jnp.float32)
    q, kc, vc, ks, vs, kw, vw, gl = _split(p, NSA_SIZES)
    q = q.reshape(B, T, Hk, G, dk) * (dk ** -0.5)
    gates = jax.nn.sigmoid(gl).reshape(B, T, Hk, G, 3)
    kv_heads = lambda z: z.reshape(B, T, Hk, dk)

    n_cmp = (T - CMP_BLOCK) // CMP_STRIDE + 1
    cmp_idx = np.arange(n_cmp)[:, None] * CMP_STRIDE + np.arange(CMP_BLOCK)[None, :]

    def compress(z, pe, w1, w2):
        blk = kv_heads(z)[:, cmp_idx] + pe[None, None, :, None, :]
        blk = jnp.transpose(blk, (0, 3, 1, 2, 4)).reshape(B, Hk, n_cmp, CMP_BLOCK * dk)
        return jax.nn.gelu(blk @ w1) @ w2

    k_cmp = compress(kc, pe_k, ck1, ck2)
    v_cmp = compress(vc, pe_v, cv1, cv2)
    cmp_start = np.arange(n_cmp) * CMP_STRIDE
    cmp_end = jnp.asarray(cmp_start + CMP_BLOCK - 1)

    n_sel = T // SEL_BLOCK
    top_k = min(SEL_TOPK, n_sel)
    sel_start = np.arange(n_sel) * SEL_BLOCK
    ov = np.clip(np.minimum(cmp_start[:, None] + CMP_BLOCK, sel_start[None, :] + SEL_BLOCK)
                 - np.maximum(cmp_start[:, None], sel_start[None, :]), 0, None) / CMP_STRIDE
    ov = jnp.asarray(ov, jnp.float32)
    k_sel = kv_heads(ks).reshape(B, n_sel, SEL_BLOCK, Hk, dk).transpose(0, 3, 1, 2, 4)
    v_sel = kv_heads(vs).reshape(B, n_sel, SEL_BLOCK, Hk, dk).transpose(0, 3, 1, 2, 4)

    pad = ((0, 0), (WINDOW, 0), (0, 0), (0, 0))
    k_win = jnp.pad(kv_heads(kw), pad)
    v_win = jnp.pad(kv_heads(vw), pad)

    slopes = alibi_slopes(NSA_Q_HEADS).reshape(Hk, G)
    b_ix = jnp.arange(B)[:, None, None, None]
    h_ix = jnp.arange(Hk)[None, :, None, None]
    blk_ids = jnp.arange(n_sel)

    def query_block(qi):
        q0 = qi * Q_BLOCK
        t = q0 + jnp.arange(Q_BLOCK)
        qb = lax.dynamic_slice_in_dim(q, q0, Q_BLOCK, 1)
        gb = lax.dynamic_slice_in_dim(gates, q0, Q_BLOCK, 1)

        s = jnp.einsum('bqhgd,bhcd->bhgqc', qb, k_cmp)
        s = s - slopes[None, :, :, None, None] * jnp.abs(t[:, None] - cmp_end[None, :])
        ok_c = cmp_end[None, :] <= t[:, None]
        p_c = jax.nn.softmax(jnp.where(ok_c, s, NEG), axis=-1) * jnp.any(ok_c, axis=-1)[:, None]
        o_c = jnp.einsum('bhgqc,bhcd->bqhgd', p_c, v_cmp)

        imp = jnp.einsum('bhgqc,cn->bhqn', p_c, ov)
        cur = t // SEL_BLOCK
        valid = blk_ids[None, :] <= cur[:, None]
        forced = (blk_ids[None, :] == 0) | (blk_ids[None, :] == cur[:, None]) | (blk_ids[None, :] == cur[:, None] - 1)
        imp = jnp.where(valid, jnp.where(forced, BIG, imp), NEG)
        top_v, top_i = lax.top_k(imp, top_k)
        kg = k_sel[b_ix, h_ix, top_i]
        vg = v_sel[b_ix, h_ix, top_i]
        pos = top_i[..., None] * SEL_BLOCK + jnp.arange(SEL_BLOCK)
        s = jnp.einsum('bqhgd,bhqnjd->bhgqnj', qb, kg)
        s = s - slopes[None, :, :, None, None, None] * jnp.abs(t[:, None, None] - pos)[:, :, None]
        ok_s = ((top_v > 0.5 * NEG)[..., None] & (pos <= t[:, None, None]))[:, :, None]
        s = jnp.where(ok_s, s, NEG).reshape(B, Hk, G, Q_BLOCK, top_k * SEL_BLOCK)
        p_s = jax.nn.softmax(s, axis=-1)
        o_s = jnp.einsum('bhgqm,bhqmd->bqhgd', p_s, vg.reshape(B, Hk, Q_BLOCK, top_k * SEL_BLOCK, dk))

        kwb = lax.dynamic_slice_in_dim(k_win, q0, Q_BLOCK + WINDOW, 1)
        vwb = lax.dynamic_slice_in_dim(v_win, q0, Q_BLOCK + WINDOW, 1)
        pos_w = q0 - WINDOW + jnp.arange(Q_BLOCK + WINDOW)
        dist = t[:, None] - pos_w[None, :]
        s = jnp.einsum('bqhgd,bkhd->bhgqk', qb, kwb) - slopes[None, :, :, None, None] * jnp.abs(dist)
        ok_w = (pos_w[None, :] >= 0) & (dist >= 0) & (dist < WINDOW)
        p_w = jax.nn.softmax(jnp.where(ok_w, s, NEG), axis=-1)
        o_w = jnp.einsum('bhgqk,bkhd->bqhgd', p_w, vwb)

        return gb[..., 0:1] * o_c + gb[..., 1:2] * o_s + gb[..., 2:3] * o_w

    out = lax.map(query_block, jnp.arange(T // Q_BLOCK))
    return jnp.moveaxis(out, 0, 1).reshape(B, T, D_NSA)

def first_inputs(seed: int = 0) -> dict:
    key = jax.random.key(seed)
    ks = jax.random.split(key, 26)
    f32 = jnp.float32
    L = DEPTH

    def nrm(k, shape, scale):
        return jax.random.normal(k, shape, f32) * scale

    def gain(k, shape):
        return 1.0 + 0.02 * jax.random.normal(k, shape, f32)

    return {
        'x': nrm(ks[0], (BATCH, SEQ, D_MODEL), 1.0),
        'norm1_g': gain(ks[1], (L, D_MODEL)),
        'w_in': nrm(ks[2], (L, D_MODEL, N_IN), D_MODEL ** -0.5),
        'mu_shift': jax.random.uniform(ks[3], (L, N_RWKV_COLS), f32),
        'rwkv_w0': jax.random.uniform(ks[4], (L, D_RWKV), f32, -4.0, 1.0),
        'rwkv_w2': nrm(ks[5], (L, LORA_W, D_RWKV), 0.1),
        'rwkv_a0': nrm(ks[6], (L, D_RWKV), 0.5),
        'rwkv_a2': nrm(ks[7], (L, LORA_A, D_RWKV), 0.1),
        'rwkv_g2': nrm(ks[8], (L, LORA_G, D_RWKV), LORA_G ** -0.5),
        'rwkv_k_k': 0.85 + 0.05 * jax.random.normal(ks[9], (L, D_RWKV), f32),
        'rwkv_k_a': gain(ks[10], (L, D_RWKV)),
        'rwkv_r_k': nrm(ks[11], (L, RWKV_HEADS, HEAD_DIM), 0.1),
        'rwkv_lnx_w': gain(ks[12], (L, D_RWKV)),
        'rwkv_lnx_b': nrm(ks[13], (L, D_RWKV), 0.01),
        'nsa_pe_k': nrm(ks[14], (L, CMP_BLOCK, HEAD_DIM), 0.1),
        'nsa_pe_v': nrm(ks[15], (L, CMP_BLOCK, HEAD_DIM), 0.1),
        'nsa_cmp_k_w1': nrm(ks[16], (L, CMP_BLOCK * HEAD_DIM, CMP_HIDDEN), (CMP_BLOCK * HEAD_DIM) ** -0.5),
        'nsa_cmp_k_w2': nrm(ks[17], (L, CMP_HIDDEN, HEAD_DIM), CMP_HIDDEN ** -0.5),
        'nsa_cmp_v_w1': nrm(ks[18], (L, CMP_BLOCK * HEAD_DIM, CMP_HIDDEN), (CMP_BLOCK * HEAD_DIM) ** -0.5),
        'nsa_cmp_v_w2': nrm(ks[19], (L, CMP_HIDDEN, HEAD_DIM), CMP_HIDDEN ** -0.5),
        'w_out': nrm(ks[20], (L, D_MIX, D_MODEL), D_MIX ** -0.5),
        'norm2_g': gain(ks[21], (L, D_MODEL)),
        'ffn_w_gate': nrm(ks[22], (L, D_MODEL, D_FF), D_MODEL ** -0.5),
        'ffn_w_up': nrm(ks[23], (L, D_MODEL, D_FF), D_MODEL ** -0.5),
        'ffn_w_down': nrm(ks[24], (L, D_FF, D_MODEL), D_FF ** -0.5),
        'norm_f_g': gain(ks[25], (D_MODEL,)),
    }

def first_block(x, norm1_g, w_in, mu_shift, rwkv_w0, rwkv_w2, rwkv_a0, rwkv_a2, rwkv_g2,
              rwkv_k_k, rwkv_k_a, rwkv_r_k, rwkv_lnx_w, rwkv_lnx_b, nsa_pe_k, nsa_pe_v,
              nsa_cmp_k_w1, nsa_cmp_k_w2, nsa_cmp_v_w1, nsa_cmp_v_w2, w_out, norm2_g,
              ffn_w_gate, ffn_w_up, ffn_w_down, norm_f_g):
    h = x
    for i in range(DEPTH):
        u = rms_norm(h, norm1_g[i])
        p_rwkv, p_nsa = jnp.split(u @ w_in[i], [N_RWKV_COLS], axis=-1)
        y_rwkv = rwkv7_time_mix(p_rwkv, mu_shift[i], rwkv_w0[i], rwkv_w2[i], rwkv_a0[i], rwkv_a2[i],
                                rwkv_g2[i], rwkv_k_k[i], rwkv_k_a[i], rwkv_r_k[i],
                                rwkv_lnx_w[i], rwkv_lnx_b[i])
        y_nsa = nsa_attention(p_nsa, nsa_pe_k[i], nsa_pe_v[i], nsa_cmp_k_w1[i], nsa_cmp_k_w2[i],
                              nsa_cmp_v_w1[i], nsa_cmp_v_w2[i])
        y = jnp.concatenate([y_rwkv, y_nsa], axis=-1).astype(h.dtype)
        h = h + y @ w_out[i]
        h = h + swiglu(rms_norm(h, norm2_g[i]), ffn_w_gate[i], ffn_w_up[i], ffn_w_down[i])
    return rms_norm(h, norm_f_g)


DEPTH_2 = 2

EPS = 1e-6
BLOCK_Q = 128
D_FF_2 = 2816
GLA_HEADS = 4
GLA_DK = 64
GLA_DV = 128
GLA_GATE_RANK = 16
GLA_GATE_NORMALIZER = 16.0
GLA_CHUNK = 64
FOX_HEADS = 8
FOX_DH = 64
DSA_HEADS = 16
DSA_DH = 64
DSA_LATENT = 256
IDX_HEADS = 8
IDX_DIM = 64
TOPK_MAX = 256
T5_BUCKETS = 32
T5_MAX_DIST = 128

N_EVEN = (DEPTH_2 + 1) // 2
N_ODD = DEPTH_2 // 2

EVEN_SIZES = (GLA_HEADS * GLA_DK, GLA_HEADS * GLA_DK, GLA_HEADS * GLA_DV, GLA_HEADS * GLA_DV, GLA_GATE_RANK,
              FOX_HEADS * FOX_DH, FOX_HEADS * FOX_DH, FOX_HEADS * FOX_DH, FOX_HEADS)
ODD_SIZES = (DSA_HEADS * DSA_DH, DSA_LATENT, IDX_HEADS * IDX_DIM, IDX_DIM, IDX_HEADS)
D_IN_EVEN = sum(EVEN_SIZES)
D_IN_ODD = sum(ODD_SIZES)
EVEN_SPLITS = tuple(int(v) for v in np.cumsum(EVEN_SIZES)[:-1])
ODD_SPLITS = tuple(int(v) for v in np.cumsum(ODD_SIZES)[:-1])
D_MIX_EVEN = GLA_HEADS * GLA_DV + FOX_HEADS * FOX_DH
D_MIX_ODD = DSA_HEADS * DSA_DH


def rmsnorm(x, g):
    xf = x.astype(jnp.float32)
    y = xf * lax.rsqrt(jnp.mean(xf * xf, axis=-1, keepdims=True) + EPS)
    return (y * g.astype(jnp.float32)).astype(x.dtype)

def swiglu_2(h, w_in, w_out):
    a, b = jnp.split(h @ w_in, 2, axis=-1)
    return (jax.nn.silu(a) * b) @ w_out

def to_blocks(t, nb):
    return t.reshape((t.shape[0], nb, BLOCK_Q) + t.shape[2:]).swapaxes(0, 1)

def gla_chunked(q, k, v, gk):
    B, S, H, dk = q.shape
    dv = v.shape[-1]
    C = GLA_CHUNK
    N = S // C

    def chunks(t):
        return t.astype(jnp.float32).reshape(B, N, C, H, t.shape[-1]).transpose(1, 0, 3, 2, 4)

    qc = chunks(q) * (dk ** -0.5)
    kc, vc, gc = chunks(k), chunks(v), chunks(gk)
    G = jnp.cumsum(gc, axis=-2)
    G_last = G[..., -1, :]
    q_dec = qc * jnp.exp(G)
    k_dec = kc * jnp.exp(-G)
    k_to_end = kc * jnp.exp(G_last[..., None, :] - G)
    causal = jnp.tril(jnp.ones((C, C), dtype=bool))
    A = jnp.where(causal, jnp.einsum('nbhid,nbhjd->nbhij', q_dec, k_dec), 0.0)
    o_intra = jnp.einsum('nbhij,nbhjv->nbhiv', A, vc)

    def step(state, inp):
        qd, ke, vv, gl = inp
        o = jnp.einsum('bhid,bhdv->bhiv', qd, state)
        state = jnp.exp(gl)[..., None] * state + jnp.einsum('bhjd,bhjv->bhdv', ke, vv)
        return state, o

    state0 = jnp.zeros((B, H, dk, dv), jnp.float32)
    _, o_inter = lax.scan(step, state0, (q_dec, k_to_end, vc, G_last))
    o = o_intra + o_inter
    return o.transpose(1, 0, 3, 2, 4).reshape(B, S, H, dv)

def fox_attention(q, k, v, log_f):
    B, S, H, dh = q.shape
    nb = S // BLOCK_Q
    F = jnp.cumsum(log_f, axis=1)
    F_keys = F.transpose(0, 2, 1)
    key_pos = jnp.arange(S)

    def one_block(args):
        i, qb, Fb = args
        q_pos = i * BLOCK_Q + jnp.arange(BLOCK_Q)
        s = jnp.einsum('bqhd,bkhd->bhqk', qb, k).astype(jnp.float32) * (dh ** -0.5)
        s = s + (Fb.transpose(0, 2, 1)[..., :, None] - F_keys[..., None, :])
        s = jnp.where(key_pos[None, :] <= q_pos[:, None], s, -jnp.inf)
        p = jax.nn.softmax(s, axis=-1)
        return jnp.einsum('bhqk,bkhd->bqhd', p.astype(v.dtype), v)

    o = lax.map(one_block, (jnp.arange(nb), to_blocks(q, nb), to_blocks(F, nb)))
    return o.swapaxes(0, 1).reshape(B, S, H, dh)

def t5_bucket(dist):
    max_exact = T5_BUCKETS // 2
    d = jnp.maximum(dist, 1).astype(jnp.float32)
    large = max_exact + (jnp.log(d / max_exact) / math.log(T5_MAX_DIST / max_exact)
                         * (T5_BUCKETS - max_exact)).astype(jnp.int32)
    large = jnp.minimum(large, T5_BUCKETS - 1)
    return jnp.where(dist < max_exact, dist, large)

def dsa_attention(q_lat, c, q_idx, k_idx, w_idx, t5_table):
    B, S, H, DL = q_lat.shape
    k_top = min(TOPK_MAX, S // 4)
    nb = S // BLOCK_Q
    key_pos = jnp.arange(S)
    w_scaled = w_idx.astype(jnp.float32) * (IDX_HEADS ** -0.5)
    gather = jax.vmap(lambda cb, ib: cb[ib])

    def one_block(args):
        i, qb, qib, wb = args
        q_pos = i * BLOCK_Q + jnp.arange(BLOCK_Q)
        logit_idx = jnp.einsum('bqhd,bkd->bqhk', qib, k_idx).astype(jnp.float32) * (IDX_DIM ** -0.5)
        score = jnp.einsum('bqh,bqhk->bqk', wb, jax.nn.relu(logit_idx))
        score = jnp.where((key_pos[None, :] <= q_pos[:, None])[None], score, -jnp.inf)
        _, idx = lax.top_k(score, k_top)
        c_sel = gather(c, idx)
        dist = q_pos[None, :, None] - idx
        bias = t5_table[t5_bucket(jnp.maximum(dist, 0))]
        s = jnp.einsum('bqhl,bqkl->bqhk', qb, c_sel).astype(jnp.float32) * (DSA_DH ** -0.5)
        s = s + bias.transpose(0, 1, 3, 2).astype(jnp.float32)
        s = jnp.where((dist >= 0)[:, :, None, :], s, -jnp.inf)
        p = jax.nn.softmax(s, axis=-1)
        return jnp.einsum('bqhk,bqkl->bqhl', p.astype(c.dtype), c_sel)

    o = lax.map(one_block, (jnp.arange(nb), to_blocks(q_lat, nb), to_blocks(q_idx, nb), to_blocks(w_scaled, nb)))
    return o.swapaxes(0, 1).reshape(B, S, H, DL)

def even_mixer(h, w_in, gla_w_gate, gla_b_gate, gla_norm_g, fox_b_f, w_out):
    B, S, _ = h.shape
    q_g, k_g, v_g, g_out, gk_low, q_f, k_f, v_f, f_logit = jnp.split(h @ w_in, EVEN_SPLITS, axis=-1)
    gk = jax.nn.log_sigmoid((gk_low @ gla_w_gate + gla_b_gate).astype(jnp.float32)) / GLA_GATE_NORMALIZER
    o_gla = gla_chunked(q_g.reshape(B, S, GLA_HEADS, GLA_DK), k_g.reshape(B, S, GLA_HEADS, GLA_DK),
                        v_g.reshape(B, S, GLA_HEADS, GLA_DV), gk.reshape(B, S, GLA_HEADS, GLA_DK)).astype(h.dtype)
    o_gla = rmsnorm(o_gla, gla_norm_g) * jax.nn.silu(g_out.reshape(B, S, GLA_HEADS, GLA_DV))
    log_f = jax.nn.log_sigmoid((f_logit + fox_b_f).astype(jnp.float32))
    o_fox = fox_attention(q_f.reshape(B, S, FOX_HEADS, FOX_DH), k_f.reshape(B, S, FOX_HEADS, FOX_DH),
                          v_f.reshape(B, S, FOX_HEADS, FOX_DH), log_f)
    o = jnp.concatenate([o_gla.reshape(B, S, -1), o_fox.reshape(B, S, -1)], axis=-1)
    return o @ w_out

def odd_mixer(h, w_in, kv_norm_g, w_uk, w_uv, w_out, t5_table):
    B, S, _ = h.shape
    q, ckv, q_idx, k_idx, w_idx = jnp.split(h @ w_in, ODD_SPLITS, axis=-1)
    c = rmsnorm(ckv, kv_norm_g)
    q_lat = jnp.einsum('bshd,hdl->bshl', q.reshape(B, S, DSA_HEADS, DSA_DH), w_uk)
    o_lat = dsa_attention(q_lat, c, q_idx.reshape(B, S, IDX_HEADS, IDX_DIM), k_idx, w_idx, t5_table)
    o = jnp.einsum('bshl,hld->bshd', o_lat, w_uv).reshape(B, S, D_MIX_ODD)
    return o @ w_out

def second_inputs(seed: int = 0) -> dict:
    key = jax.random.key(seed)
    ks = jax.random.split(key, 17)
    f32 = jnp.float32

    def nrm(k, shape, fan_in):
        return jax.random.normal(k, shape, f32) * (fan_in ** -0.5)

    def gain(k, shape):
        return 1.0 + 0.02 * jax.random.normal(k, shape, f32)

    return {
        "x": jax.random.normal(ks[0], (BATCH, SEQ, D_MODEL), f32),
        "norm_g": gain(ks[1], (DEPTH_2, 3, D_MODEL)),
        "ffn_w_in": nrm(ks[2], (DEPTH_2, 2, D_MODEL, 2 * D_FF_2), D_MODEL),
        "ffn_w_out": nrm(ks[3], (DEPTH_2, 2, D_FF_2, D_MODEL), D_FF_2),
        "even_w_in": nrm(ks[4], (N_EVEN, D_MODEL, D_IN_EVEN), D_MODEL),
        "gla_w_gate": nrm(ks[5], (N_EVEN, GLA_GATE_RANK, GLA_HEADS * GLA_DK), GLA_GATE_RANK),
        "gla_b_gate": 0.02 * jax.random.normal(ks[6], (N_EVEN, GLA_HEADS * GLA_DK), f32),
        "gla_norm_g": gain(ks[7], (N_EVEN, GLA_DV)),
        "fox_b_f": 2.0 + 0.5 * jax.random.normal(ks[8], (N_EVEN, FOX_HEADS), f32),
        "even_w_out": nrm(ks[9], (N_EVEN, D_MIX_EVEN, D_MODEL), D_MIX_EVEN),
        "odd_w_in": nrm(ks[10], (N_ODD, D_MODEL, D_IN_ODD), D_MODEL),
        "mla_kv_norm_g": gain(ks[11], (N_ODD, DSA_LATENT)),
        "mla_w_uk": nrm(ks[12], (N_ODD, DSA_HEADS, DSA_DH, DSA_LATENT), DSA_LATENT),
        "mla_w_uv": nrm(ks[13], (N_ODD, DSA_HEADS, DSA_LATENT, DSA_DH), DSA_LATENT),
        "odd_w_out": nrm(ks[14], (N_ODD, D_MIX_ODD, D_MODEL), D_MIX_ODD),
        "t5_table": 0.5 * jax.random.normal(ks[15], (T5_BUCKETS, DSA_HEADS), f32),
        "final_norm_g": gain(ks[16], (D_MODEL,)),
    }

def second_block(x, norm_g, ffn_w_in, ffn_w_out, even_w_in, gla_w_gate, gla_b_gate, gla_norm_g, fox_b_f,
              even_w_out, odd_w_in, mla_kv_norm_g, mla_w_uk, mla_w_uv, odd_w_out, t5_table, final_norm_g):
    for layer in range(DEPTH_2):
        g = norm_g[layer]
        x = x + 0.5 * swiglu_2(rmsnorm(x, g[0]), ffn_w_in[layer, 0], ffn_w_out[layer, 0])
        h = rmsnorm(x, g[1])
        j = layer // 2
        if layer % 2 == 0:
            x = x + even_mixer(h, even_w_in[j], gla_w_gate[j], gla_b_gate[j], gla_norm_g[j], fox_b_f[j], even_w_out[j])
        else:
            x = x + odd_mixer(h, odd_w_in[j], mla_kv_norm_g[j], mla_w_uk[j], mla_w_uv[j], odd_w_out[j], t5_table)
        x = x + 0.5 * swiglu_2(rmsnorm(x, g[2]), ffn_w_in[layer, 1], ffn_w_out[layer, 1])
    return rmsnorm(x, final_norm_g)


def setup_inputs(seed=0):
    out = dict(first_inputs(seed))
    for name, value in second_inputs(seed + 1).items():
        if name != "x":
            out[name + "_2"] = value
    return out


def reference(
    x, norm1_g, w_in, mu_shift, rwkv_w0, rwkv_w2, rwkv_a0, rwkv_a2, rwkv_g2, rwkv_k_k, rwkv_k_a,
    rwkv_r_k, rwkv_lnx_w, rwkv_lnx_b, nsa_pe_k, nsa_pe_v, nsa_cmp_k_w1, nsa_cmp_k_w2,
    nsa_cmp_v_w1, nsa_cmp_v_w2, w_out, norm2_g, ffn_w_gate, ffn_w_up, ffn_w_down, norm_f_g,
    norm_g_2, ffn_w_in_2, ffn_w_out_2, even_w_in_2, gla_w_gate_2, gla_b_gate_2, gla_norm_g_2,
    fox_b_f_2, even_w_out_2, odd_w_in_2, mla_kv_norm_g_2, mla_w_uk_2, mla_w_uv_2, odd_w_out_2,
    t5_table_2, final_norm_g_2,
):
    x = first_block(
        x, norm1_g, w_in, mu_shift, rwkv_w0, rwkv_w2, rwkv_a0, rwkv_a2, rwkv_g2, rwkv_k_k,
        rwkv_k_a, rwkv_r_k, rwkv_lnx_w, rwkv_lnx_b, nsa_pe_k, nsa_pe_v, nsa_cmp_k_w1,
        nsa_cmp_k_w2, nsa_cmp_v_w1, nsa_cmp_v_w2, w_out, norm2_g, ffn_w_gate, ffn_w_up,
        ffn_w_down, norm_f_g,
    )
    return second_block(
        x, norm_g_2, ffn_w_in_2, ffn_w_out_2, even_w_in_2, gla_w_gate_2, gla_b_gate_2,
        gla_norm_g_2, fox_b_f_2, even_w_out_2, odd_w_in_2, mla_kv_norm_g_2, mla_w_uk_2,
        mla_w_uv_2, odd_w_out_2, t5_table_2, final_norm_g_2,
    )


_drawn_inputs = setup_inputs


def setup_inputs(seed=0):
    import zlib

    import numpy as np

    out = dict(_drawn_inputs(seed))
    spreads = {}
    factors = {'rwkv_k_k': 2.725,
     'rwkv_lnx_w': 2.933,
     'rwkv_lnx_b': 4.095,
     'nsa_pe_k': 5.528,
     'gla_b_gate_2': 5.475,
     'gla_norm_g_2': 3.893,
     'mla_kv_norm_g_2': 8.0,
     'final_norm_g_2': 2.73}
    for name, (base, spread) in spreads.items():
        noise = np.random.default_rng([zlib.crc32(name.encode()), seed]).standard_normal(out[name].shape)
        drawn = base * np.exp(spread * noise) if base else spread * noise
        out[name] = __import__('jax').numpy.asarray(drawn.astype(out[name].dtype))
    for name, factor in factors.items():
        out[name] = (out[name] * factor).astype(out[name].dtype)
    return out
```

```python
from contextlib import ExitStack

import numpy as np

import concourse.bass as bass
from concourse import mybir

F32 = mybir.dt.float32
F32R = mybir.dt.float32r
U8 = mybir.dt.uint8
ALU = mybir.AluOpType
ACT = mybir.ActivationFunctionType
AX = mybir.AxisListType

P = 128
T, D = 256, 1024
TT, KC = T // P, D // P
F = 2816
FC = F // P
HD = 64
SLOT = 3 * 1024
RING = 4
NC_CMP, CMP_STRIDE = 15, 16
LEVELS = 7
DECAY = float(np.exp(-0.5))
NEG = -1e30
TOPK = 64

SLOTS = [("w_in", 8), ("cmp_w1", 3), ("w_out", 3), ("ffn0", FC), ("ffn1", FC), ("even_in", 8), ("even_out", 3),
         ("ffn2", FC), ("ffn3", FC), ("odd_in", 5), ("uk_uv", 2), ("odd_out", 3), ("ffn4", FC)]
BASE = {}
NSLOTS = 0
for _name, _n in SLOTS:
    BASE[_name] = NSLOTS
    NSLOTS += _n

CONSTS = [("ident", P), ("reverse", P), ("pair_ones", P), ("ones", P), ("w2", 512), ("a2", 512), ("g2", 512), ("gate_w", KC * 24),
          ("even_small", KC * 24), ("odd_small", KC * 8), ("gla_gate", 256), ("ck2", 256), ("cv2", 128),
          ("pe_k", 16), ("pe_v", 16), ("t5", 16), ("t5_onehot", 384), ("alibi", 256), ("alibi_cmp", 2 * 16),
          ("any_ok", 2), ("causal", 256), ("neg_half", 2 * 16),
          ("mu", 14), ("w0", 4), ("a0", 4), ("k_k", 4), ("k_a", 4), ("r_k", 4), ("lnx_w", 4), ("lnx_b", 4),
          ("gla_b", 2), ("gla_norm", 1), ("fox_b", 1), ("kv_norm", 2)]
COL = {}
NCONST = 0
for _name, _n in CONSTS:
    COL[_name] = (NCONST, _n)
    NCONST += _n

MASKS = 512 + 2 * LEVELS * P

IN_ITEMS = ([("col", 0), ("col", 1)] + [("col", b) for b in range(2, 6)] + [("zw", j) for j in range(4)]
            + [("za", j) for j in range(4)] + [("g", j) for j in range(4)] + [("col", b) for b in range(6, 22)]
            + [("tok", 0), ("tok", 1), ("gate", 0)])
EVEN_ITEMS = ([("small", 0)] + [("col", b) for b in range(4)] + [("gz", 0), ("gz", 1)]
              + [("col", b) for b in range(4, 16)]
              + [("tok", t, n) for n in range(3) for t in range(TT)])
ODD_ITEMS = ([("col", b) for b in range(13)] + [("ckv", t) for t in range(TT)] + [("small", t) for t in range(TT)])
UKV_ITEMS = [("kh", j) for j in range(8)] + [("vh", t, n) for t in range(TT) for n in range(2)]

RWKV_UNITS = 8


def build(nc, x_in, wstream, gains, consts_in, masks_in, scratch, out):
    ctx = ExitStack()
    with ctx:
        at = {}

        def sb(name, shape, dt=F32):
            at[name] = nc.sbuf_base
            return ctx.enter_context(nc.sbuf_tensor(name, shape, dt))

        def over(name, shape, under, skip=0):
            return nc.alloc_sbuf_tensor_at(name, shape, F32R, offset=at[under] + 4 * skip)

        names = ("x_loaded consts_loaded masks_loaded masks_ready gain0 gain1 land0 land1 land2 land3 free0 free1 free2 free3 "
                 "a_step v_step g_step ss_ready rstd_ready xn_ready x_done xT_ps uT_a uT_v "
                 "gu_ps silu_ready h_mul h_hi h_ready gu_done down_done hi_a hi_b lo_a lo_b uT_hi uT_lo mix_ready op_acc item_ps item_ev "
                 "shift_ready lora_in raw_free kk_sq n2_ps kk_clamped kk_sqrt kk_n2_read rk_ready bon_ps "
                 "bonus_read csm_ready e_ready scan_in ab_ready tok_ps tok_ev id_ready A_ps A_read "
                 "P_ps P_ev dM_ps M_ready rhs_ps rhs_ev sa_ps sa_ev y_ps s_ps y_ev s_ev var_ready grs_ready yn_ready "
                 "ynT_ps ynT_ev cmp_z cmp_h cmp_hact cmp_kv cmp_ready gates_ready gates_ps gate_tok "
                 "S_ps max_ready p_ready pT_ps pT_ev o_ps o_ready oT_ps oT_ev "
                 "gk_in gk_ab gk_min gk_ls gk_cs fox_cs fox_ps fox_tok gla_k gla_ready "
                 "c_ss c_rs c_n c_ps c_ev idx_ps idx_relu idx_acc sel_ready t5_ps t5_sb t5_out t5_in "
                 "stored").split()
        s = {n: ctx.enter_context(nc.semaphore(n)) for n in names}

        x = sb("x", [P, TT, D])
        xn = sb("xn", [P, TT, D])
        uT = sb("uT", [P, KC, T])
        yT = sb("yT", [P, KC, T])
        gb = sb("gb", [P, 2, D])
        ring = sb("ring", [P, RING, SLOT])
        ffb = sb("ffb", [P, 4, T])
        cst = sb("cst", [P, NCONST])
        msk = sb("msk", [P, MASKS], U8)
        small = sb("small", [P, 256])
        WK = 20480
        wk = sb("wk", [P, WK])
        ps = [ctx.enter_context(nc.psum_tensor(f"ps{i}", [P, 512], F32)) for i in range(8)]

        def C(name, lo=0, hi=None):
            o, n = COL[name]
            return cst[:, o + lo:o + (n if hi is None else hi)]

        def W(off, *shape):
            n = int(np.prod(shape))
            a = wk[:, off:off + n]
            if len(shape) == 2:
                a = a.rearrange("p (a b) -> p a b", b=shape[1])
            if len(shape) == 3:
                a = a.rearrange("p (a b c) -> p a b c", b=shape[1], c=shape[2])
            return a

        ident = C("ident")
        w_gu = over("w_gu", [P, 2, 2, 2 * D], "wk")
        w_dn = over("w_dn", [P, 2, 2, D], "wk", 8 * D)
        h_r = over("h_r", [P, 2, 2, T], "ffb")
        uT_r = [over("uT_h", [P, KC, T], "uT"), over("uT_l", [P, KC, T], "yT")]
        sg = wk[:, 12 * D:12 * D + 2 * T].rearrange("p (a b) -> p a b", a=2)
        ss, rstd = small[:, 0:2], small[:, 2:4]
        den, nmax, rden, coef = small[:, 4:12], small[:, 12:16], small[:, 16:17], small[:, 17:18]

        pr, pk, pv = W(0, 4, T), W(1024, 4, T), W(2048, 4, T)
        gg, kk, kp = W(3072, 4, T), W(4096, 4, T), W(1024, 4, T)
        sgm, agm = xn[:, 0, :].rearrange("p (a b) -> p a b", b=T), xn[:, 1, :].rearrange("p (a b) -> p a b", b=T)
        ytok = W(5120, TT, 512)
        tmp = W(5120, 4, T)
        arT = W(6144, 4, TT, 2 * P)
        bT, kT_ = W(8192, 4, TT * P), W(9216, 4, TT * P)
        AA = W(10240, RWKV_UNITS, 512)
        E1, E2, E3, cs = W(10240, 4, T), W(11264, 4, T), W(12288, 4, T), W(13312, 4, T)
        Mm, Mt = W(14336, RWKV_UNITS, P), W(15360, RWKV_UNITS, P)
        raw = W(14336, 4, 257)
        Pb = W(16384, 2, 512)
        csp = W(16384, 4, T)
        lora = W(17408, 2, T)
        td = W(17920, T)
        tg = W(18176, T)
        qT, ksT, kwT = W(18432, 4, T), W(19456, T), W(19712, T)
        vtok = yT[:, 0:4, :].rearrange("p (t c) n -> p t (c n)", t=2)
        bktok = yT[:, 4:8, :].rearrange("p (w c) n -> p w (c n)", w=2)
        Sst = ffb[:, 0, :].rearrange("p (c n) -> p c n", c=2)
        RH, SA = ffb[:, 1, :], ffb[:, 2, :]
        glT = ffb[:, 3, :]

        zk = sb("zk", [P, 3, P])
        zv = sb("zv", [P, 3, P])
        vsw = sb("vsw", [P, TT, 256])
        hid = sb("hid", [P, 2, 2, 48])
        kcT = sb("kcT", [P, 16])
        vc = sb("vc", [16, 2, HD])
        gtok = sb("gtok", [P, TT, 24])
        SS, Pp, PT = W(10240, 3, T), W(11008, 3, T), W(11776, 2, 2 * P)
        onsa = W(0, TT, 512)

        block = ctx.enter_context(nc.Block())

        def mask(i, n=1):
            return msk[:, 512 + i * P:512 + (i + n) * P]

        def att_units(kind):
            units = []
            if kind == "nsa":
                for t in range(TT):
                    K = P * (t + 1)
                    for h in range(8):
                        j, r = h % 4, HD * (h // 4)
                        q = qT[r:r + HD, j, t * P:(t + 1) * P]
                        slope = 2.0 ** -(h + 1)
                        out_ = onsa[:, t, h * HD:(h + 1) * HD]
                        for b in range(3):
                            u = dict(q=q, slope=slope, out=out_, add=b > 0, gate=gtok[:, t, 3 * h + b:3 * h + b + 1])
                            if b == 0:
                                u.update(k=kcT[r:r + HD, 0:NC_CMP], K=NC_CMP, v=[vc[0:NC_CMP, h // 4, :]],
                                         dist=C("alibi_cmp", 16 * t, 16 * t + NC_CMP))
                            else:
                                kx = ksT if b == 1 else kwT
                                o = (b - 1) * P + r
                                u.update(k=kx[r:r + HD, 0:K], K=K, v=[vsw[:, kt, o:o + HD] for kt in range(t + 1)],
                                         dist=C("alibi", P * (1 - t), P * (1 - t) + K))
                            units.append(u)
            if kind == "fox":
                for t in range(TT):
                    K = P * (t + 1)
                    for h in range(8):
                        c, r = h // 2, HD * (h % 2)
                        units.append(dict(q=fqT[r:r + HD, c, t * P:(t + 1) * P], k=fkT[r:r + HD, c, 0:K], K=K,
                                          v=[evtok[:, kt, 512 + h * HD:512 + (h + 1) * HD] for kt in range(t + 1)],
                                          row=ftok[:, t, h:h + 1], head=h, fneg=fneg[0:8, 0:K],
                                          dist=C("causal", P * (1 - t), P * (1 - t) + K),
                                          out=ofox[:, t, h * HD:(h + 1) * HD], add=False, gate=None))
            if kind == "dsa":
                for t in range(TT):
                    K = P * (t + 1)
                    for h in range(16):
                        c, r = h // 2, HD * (h % 2)
                        units.append(dict(q=oqT[r:r + HD, c, t * P:(t + 1) * P], k=khT[r:r + HD, c, 0:K], K=K,
                                          v=[vh[:, kt, h * HD:(h + 1) * HD] for kt in range(t + 1)],
                                          t5=bias16[:, h, P * (1 - t):P * (1 - t) + K], dist=selm[:, t, 0:K], out=odsa[:, t, h * HD:(h + 1) * HD], add=False, gate=None))
            return units

        gqT, gkT = W(0, 2, T), W(512, 2, T)
        goT = W(1024, 4, T)
        fqT, fkT = W(2048, 4, T), W(3072, 4, T)
        evtok = W(4096, TT, 1024)
        gsm = W(6144, T)
        gz, gab, gmn, gcs = W(6400, 2, T), W(6912, 2, T), W(7424, 2, T), W(7936, 2, T)
        fz, fab, fmn, fneg = W(8448, T), W(8704, T), W(8960, T), W(9216, T)
        fsum = W(9472, T)
        ftok = small[:, 192:208].rearrange("p (t h) -> p t h", t=2)
        gqd, gkd = W(14336, 2, T), W(14848, 2, T)
        gE1, gE2 = W(15360, 2, T), W(15872, 2, T)
        gkt = W(16384, 2, P)
        gA = W(16640, 4, P)
        gS = W(17152, 2, 256)
        ogla = W(17664, TT, 512)
        gsq = W(18688, 512)
        ofox = W(19200, 1, 1024)[:, 0, :].rearrange("p (t n) -> p t n", t=2)
        oqT, khT = W(0, 8, T), W(2048, 8, T)
        vh = W(4096, TT, 1024)
        odsa = W(6144, TT, 1024)
        qiT = W(8192, 4, T)
        kiT = W(9216, T)
        idxs = W(9472, 2, T)
        wtok = small[:, 208:224].rearrange("p (t h) -> p t h", t=2)
        selm = W(13568, 2, T)
        ckv = W(14080, 2, 256)
        cT = W(14592, 2, T)
        score = W(15104, T)
        bias16 = W(15360, 16, T)
        csc = W(9984, T)

        UN = {k: att_units(k) for k in ("nsa", "fox", "dsa")}
        UB = {"nsa": 0, "fox": len(UN["nsa"]), "dsa": len(UN["nsa"]) + len(UN["fox"])}
        IB, n = {}, 0
        for k, items in (("in", IN_ITEMS), ("even", EVEN_ITEMS), ("odd", ODD_ITEMS), ("ukv", UKV_ITEMS)):
            IB[k] = n
            n += len(items)
        TN = {n: i for i, n in enumerate([0, 1, 3, 4, 5, 6, 7, 8])}
        MIX_OF = {0: 0, 4: 1, 7: 2}
        FFN_OF = {1: 0, 3: 1, 5: 2, 6: 3, 8: 4}
        LOOPS = (FC - 6) // 4

        @block.sync
        def _(sp):
            sp.dma_start(x[:], x_in.rearrange("(t p) d -> p t d", p=P)).then_inc(s["x_loaded"], 16)
            for i in range(RING):
                sp.dma_start(ring[:, i, :], wstream[i]).then_inc(s[f"land{i}"], 16)
            NS = NSLOTS
            rounds = (NS - RING) // RING
            with sp.Fori(0, rounds) as r:
                for j in range(RING):
                    sp.wait_ge(s[f"free{j}"], r + 1)
                    sp.dma_start(ring[:, j, :],
                                 wstream[bass.ds(r * RING + (RING + j), 1)].rearrange("a p n -> p (a n)")
                                 ).then_inc(s[f"land{j}"], 16)
            for i in range(RING * (rounds + 1), NS):
                sp.wait_ge(s[f"free{i % RING}"], i // RING)
                sp.dma_start(ring[:, i % RING, :], wstream[i]).then_inc(s[f"land{i % RING}"], 16)
            sp.wait_ge(s["xn_ready"], 2 * 10)
            sp.dma_start(out.rearrange("(t p) d -> p t d", p=P), x[:]).then_inc(s["stored"], 16)
            sp.wait_ge(s["stored"], 16)

        def slot(i):
            return ring[:, i % RING, :]

        @block.tensor
        def _(pe):
            def land(i):
                pe.wait_ge(s[f"land{i % RING}"], 16 * (i // RING + 1))

            def mm(o, l, r, start=True, stop=True):
                return pe.matmul(o, l, r, start=start, stop=stop, skip_group_check=True)

            def norm_T(n):
                k = TN[n]
                for t in range(TT):
                    pe.wait_ge(s["xn_ready"], 2 * n + t + 1)
                    for half in range(2):
                        for c in range(4):
                            last = pe.transpose(ps[4 + 2 * t + half][:, c * P:(c + 1) * P],
                                                xn[:, t, (4 * half + c) * P:(4 * half + c + 1) * P], ident)
                        last.then_inc(s["xT_ps"], 1)
                if n in FFN_OF:
                    pe.wait_ge(s["uT_lo"], 4 * (FFN_OF[n] + 1))
                else:
                    pe.wait_ge(s["uT_a"], 2 * (MIX_OF[n] + 1))
                    pe.wait_ge(s["uT_v"], 2 * (MIX_OF[n] + 1))

            PASSES = [(0, 0), (1, 0), (0, 1)]

            def gate_up(j):
                for m in range(2):
                    for k in range(KC):
                        for n, (a, b) in enumerate(PASSES):
                            w = w_gu[:, j % 2, a, (m * KC + k) * P:(m * KC + k + 1) * P]
                            last = mm(ps[4 + j % 2][:, m * T:(m + 1) * T], w, uT_r[b][:, k, :],
                                      k == 0 and n == 0, k == KC - 1 and n == 2)
                last.then_inc(s["gu_ps"], 1)

            def down(j, start, stop):
                for t in range(TT):
                    for half in range(2):
                        for n, (a, b) in enumerate(PASSES):
                            last = mm(ps[2 * t + half][:, :], h_r[:, j % 2, a, t * P:(t + 1) * P],
                                      w_dn[:, j % 2, b, half * 512:(half + 1) * 512],
                                      start and n == 0, stop and n == 2)
                last.then_inc(s["down_done"], 1)

            def ffn(f):
                q = FC * f

                def step(c, r=0):
                    pe.wait_ge(s["lo_a"], r + (q + c + 1))
                    if q + c >= 2:
                        pe.wait_ge(s["h_ready"], r + (q + c - 1))
                    gate_up(c)
                    if c:
                        pe.wait_ge(s["lo_b"], r + (q + c))
                        pe.wait_ge(s["h_ready"], r + (q + c))
                        down(c - 1, c == 1, False)
                step(0)
                step(1)
                with pe.Fori(0, 4 * LOOPS, 4) as r:
                    for j in range(4):
                        step(2 + j, r)
                for c in range(2 + 4 * LOOPS, FC):
                    step(c)
                pe.wait_ge(s["lo_b"], q + FC)
                pe.wait_ge(s["h_ready"], q + FC)
                down(FC - 1, False, True)

            def out_proj(o, b):
                pe.wait_ge(s["mix_ready"], o + 1)
                for i in range(3):
                    land(b + i)
                    for c in range(3 * i, min(3 * i + 3, KC)):
                        w = slot(b + i)[:, (c % 3) * D:(c % 3 + 1) * D]
                        for t in range(TT):
                            for half in range(2):
                                last = mm(ps[2 * t + half][:, :], yT[:, c, t * P:(t + 1) * P],
                                          w[:, half * 512:(half + 1) * 512], c == 0, c == KC - 1)
                    last.then_inc(s[f"free{(b + i) % RING}"], 1)
                pe.wait_ge(s[f"free{(b + 2) % RING}"], (b + 2) // RING + 1)
                pe.sem_inc(s["op_acc"], 1)

            def item(q):
                if q >= 4:
                    pe.wait_ge(s["item_ev"], q - 3)
                return ps[4 + q % 4]

            def col_block(bank, b, blk):
                i = b + blk // 3
                if blk % 3 == 0:
                    land(i)
                w = slot(i).rearrange("p (k f) -> p k f", k=KC)
                for k in range(KC):
                    last = mm(bank[:, 0:T], w[:, k, (blk % 3) * P:(blk % 3 + 1) * P], uT[:, k, :], k == 0, k == KC - 1)
                return last

            def tok_block(bank, i, t, lo, hi):
                w = slot(i).rearrange("p (k f) -> p k f", k=KC)
                for k in range(KC):
                    last = mm(bank[:, 0:hi - lo], uT[:, k, t * P:(t + 1) * P], w[:, k, lo:hi], k == 0, k == KC - 1)
                return last

            def freed(n, i):
                pe.wait_ge(s["item_ps"], n)
                pe.sem_inc(s[f"free{i % RING}"], 1)

            def w_in():
                b = BASE["w_in"]
                for n, it in enumerate(IN_ITEMS):
                    q = IB["in"] + n
                    bank = item(q)
                    if it[0] == "col":
                        last = col_block(bank, b, it[1])
                    elif it[0] in ("zw", "za", "g"):
                        if it == ("zw", 0):
                            pe.wait_ge(s["lora_in"], 3)
                        src = {"zw": "w2", "za": "a2", "g": "g2"}[it[0]]
                        last = mm(bank[:, 0:T], C(src, it[1] * P, (it[1] + 1) * P), tg if it[0] == "g" else td)
                    elif it[0] == "tok":
                        last = tok_block(bank, b + 7, it[1], P, 3 * P)
                    else:
                        w = C("gate_w").rearrange("p (k n) -> p k n", k=KC)
                        for k in range(KC):
                            last = mm(bank[0:24, 0:T], w[:, k, :], uT[:, k, :], k == 0, k == KC - 1)
                    last.then_inc(s["item_ps"], 1)
                    if (it[0] == "col" and it[1] % 3 == 2) or it == ("tok", 1):
                        freed(q + 1, b + 7 if it[0] == "tok" else b + it[1] // 3)
                pe.wait_ge(s["kk_sq"], 1)
                for c in range(4):
                    last = mm(ps[c // 2][:, (c % 2) * T:(c % 2 + 1) * T], C("pair_ones"), tmp[:, c, :])
                last.then_inc(s["n2_ps"], 1)
                pe.wait_ge(s["rk_ready"], 1)
                for c in range(4):
                    last = mm(ps[2 + c // 2][:, (c % 2) * T:(c % 2 + 1) * T], C("pair_ones"), tmp[:, c, :])
                last.then_inc(s["bon_ps"], 1)

            def rwkv_tok():
                pe.wait_ge(s["ab_ready"], 1)
                pe.wait_ge(s["item_ev"], IB["in"] + len(IN_ITEMS))
                srcs = [(pv, t) for t in range(TT)] + [(bT, 0), (kT_, 0)]
                for n, (src, t) in enumerate(srcs):
                    for c in range(4):
                        last = pe.transpose(ps[4 + n][:, c * P:(c + 1) * P], src[:, c, t * P:(t + 1) * P], ident)
                    last.then_inc(s["tok_ps"], 1)
                pe.wait_ge(s["tok_ev"], 4)

            def rwkv_group(g):
                def unit(u):
                    t, h = u // 4, 4 * g + u % 4
                    return t, h // 2, HD * (h % 2)
                pe.wait_ge(s["bonus_read"], 1)
                for u in range(RWKV_UNITS):
                    t, c, r = unit(u)
                    uu = RWKV_UNITS * g + u
                    if uu >= 4:
                        pe.wait_ge(s["A_read"], uu - 3)
                    bank = ps[u % 4]
                    ar = arT[r:r + HD, c, t, :]
                    tk = slice(t * P, (t + 1) * P)
                    mm(ps[4 + 2 * t + u % 2][:, (u % 4) // 2 * P:((u % 4) // 2 + 1) * P],
                       arT[r:r + HD, c, t, 0:P], bT[r:r + HD, c, tk])
                    mm(bank[:, 0:256], bT[r:r + HD, c, tk], ar)
                    mm(bank[:, 256:512], kT_[r:r + HD, c, tk], ar).then_inc(s["A_ps"], 1)
                pe.wait_ge(s["M_ready"], 2 * LEVELS * g + 2)
                for lv in range(1, LEVELS):
                    e = (LEVELS - 1) * g + lv - 1
                    for half in range(2):
                        pe.wait_ge(s["M_ready"], 2 * (e + g) + half + 1)
                        for u in range(4 * half, 4 * half + 4):
                            last = mm(ps[half][:, (u % 4) * P:(u % 4 + 1) * P], AA[:, u, 0:P], Mm[:, u, :])
                        last.then_inc(s["P_ps"], 1)
                    for half in range(2):
                        pe.wait_ge(s["P_ev"], 2 * e + half + 1)
                        for u in range(4 * half, 4 * half + 4):
                            pu = Pb[:, half, (u % 4) * P:(u % 4 + 1) * P]
                            last = mm(ps[4 + half][:, (u % 4) * P:(u % 4 + 1) * P], pu, Mt[:, u, :])
                            if lv < LEVELS - 1:
                                last = mm(ps[2 + half][:, (u % 4) * P:(u % 4 + 1) * P], Mt[:, u, :], pu)
                        last.then_inc(s["dM_ps"], 1)
                pe.wait_ge(s["M_ready"], 2 * LEVELS * (g + 1))
                for t in range(TT):
                    n = 2 * g + t
                    if t:
                        pe.wait_ge(s["s_ev"], g + 1)
                    for c in range(2):
                        o = ps[6][:, c * P:(c + 1) * P]
                        if t:
                            mm(o, arT[:, 2 * g + c, 1, 0:P], Sst[:, c, :], True, False)
                        for hh in range(2):
                            u = 4 * t + 2 * c + hh
                            last = mm(o[:, hh * HD:(hh + 1) * HD], AA[:, u, 256:384],
                                      vtok[:, t, (4 * g + 2 * c + hh) * HD:(4 * g + 2 * c + hh + 1) * HD],
                                      not t, True)
                    last.then_inc(s["rhs_ps"], 1)
                    pe.wait_ge(s["rhs_ev"], n + 1)
                    for h in range(4):
                        last = mm(ps[7][:, h * HD:(h + 1) * HD], Mt[:, 4 * t + h, :], RH[:, h * HD:(h + 1) * HD])
                    last.then_inc(s["sa_ps"], 1)
                    pe.wait_ge(s["sa_ev"], n + 1)
                    for c in range(2):
                        o = ps[6][:, 256 + c * P:256 + (c + 1) * P]
                        if t:
                            mm(o, arT[:, 2 * g + c, 1, P:2 * P], Sst[:, c, :], True, False)
                        for hh in range(2):
                            u = 4 * t + 2 * c + hh
                            oh, hc = o[:, hh * HD:(hh + 1) * HD], (2 * c + hh) * HD
                            mm(oh, AA[:, u, 128:256], SA[:, hc:hc + HD], not t, False)
                            last = mm(oh, AA[:, u, 384:512], vtok[:, t, 4 * g * HD + hc:4 * g * HD + hc + HD],
                                      False, True)
                    last.then_inc(s["y_ps"], 1)
                    if not t:
                        for c in range(2):
                            cc = 2 * g + c
                            o = ps[7][:, 256 + c * P:256 + (c + 1) * P]
                            mm(o, bktok[:, 0, cc * P:(cc + 1) * P], SA[:, c * P:(c + 1) * P], True, False)
                            last = mm(o, bktok[:, 1, cc * P:(cc + 1) * P], vtok[:, 0, cc * P:(cc + 1) * P], False, True)
                        last.then_inc(s["s_ps"], 1)
                    pe.wait_ge(s["y_ev"], n + 1)

            def tok_T(src, n0, chunks=4):
                for t in range(TT):
                    pe.wait_ge(s["yn_ready"], n0 + t + 1)
                    for c in range(chunks):
                        last = pe.transpose(ps[t][:, c * P:(c + 1) * P], src[:, t, c * P:(c + 1) * P], ident)
                    last.then_inc(s["ynT_ps"], 1)

            def compress():
                b = BASE["cmp_w1"]
                pe.wait_ge(s["cmp_z"], 2)
                for n in range(2):
                    z = (zk, zv)[n]
                    for half in range(2):
                        for m in range(16):
                            piece = 16 * n + m
                            i = b + piece // 12
                            if half == 0 and (m == 0 or piece % 12 == 0):
                                land(i)
                            w = slot(i)[:, (piece % 12) * 256 + half * P:(piece % 12) * 256 + (half + 1) * P]
                            rhs = z[:, :, m:m + 8 * 14 + 1:8]
                            last = mm(ps[4 + n][:, half * 48:half * 48 + 45].rearrange("p (a c) -> p a c", a=3),
                                      w, rhs, m == 0, m == 15)
                    last.then_inc(s["cmp_h"], 1)
                pe.wait_ge(s["cmp_h"], 2)
                for i in range(3):
                    pe.sem_inc(s[f"free{(b + i) % RING}"], 1)
                pe.wait_ge(s["cmp_hact"], 1)
                for half in range(2):
                    mm(ps[6][:, 0:30], C("ck2", half * P, (half + 1) * P), hid[:, 0, half, 0:30], half == 0, half == 1)
                for g in range(2):
                    for half in range(2):
                        last = mm(ps[6][0:NC_CMP, 64 + g * HD:64 + (g + 1) * HD],
                                  hid[:, 1, half, 15 * g:15 * g + 15], C("cv2", half * HD, (half + 1) * HD),
                                  half == 0, half == 1)
                last.then_inc(s["cmp_kv"], 1)
                pe.wait_ge(s["gates_ready"], 1)
                for t in range(TT):
                    last = pe.transpose(ps[7][:, t * 24:(t + 1) * 24], glT[0:24, t * P:(t + 1) * P], ident[0:24, 0:24])
                last.then_inc(s["gates_ps"], 1)

            def attention(kind, go, value):
                units, b = UN[kind], UB[kind]
                n = len(units)
                if kind == "dsa":
                    pe.wait_ge(s["t5_in"], 16)
                pe.wait_ge(s[go], value)
                for i in range(n + 3):
                    if i < n:
                        u, a = b + i, units[i]
                        if u >= 3:
                            pe.wait_ge(s["max_ready"], u - 2)
                        o = ps[u % 3][:, 0:a["K"]]
                        if "head" in a:
                            h = a["head"]
                            mm(o, ident[0:8, h:h + 1].to_broadcast([8, P]), a["fneg"], True, False)
                        if "t5" in a:
                            mm(o, C("reverse"), a["t5"], True, False)
                        mm(o, a["q"], a["k"], "slope" in a, True).then_inc(s["S_ps"], 1)
                    if 2 <= i < n + 2:
                        u, a = b + i - 2, units[i - 2]
                        pe.wait_ge(s["p_ready"], u + 1)
                        if u >= 2:
                            pe.wait_ge(s["pT_ev"], u - 1)
                        for k in range(0, a["K"], P):
                            w = min(P, a["K"] - k)
                            last = pe.transpose(ps[3 + u % 2][0:w, k:k + P], Pp[:, u % 3, k:k + w], ident)
                        last.then_inc(s["pT_ps"], 1)
                    if i >= 3:
                        u, a = b + i - 3, units[i - 3]
                        pe.wait_ge(s["pT_ev"], u + 1)
                        if u >= 2:
                            pe.wait_ge(s["o_ready"], u - 1)
                        for k in range(0, a["K"], P):
                            w = min(P, a["K"] - k)
                            last = mm(ps[5 + u % 2][:, 0:HD], PT[0:w, u % 2, k:k + P], a["v"][k // P],
                                      k == 0, k + P >= a["K"])
                        last.then_inc(s["o_ps"], 1)

            def even_in():
                b = BASE["even_in"]
                for n, it in enumerate(EVEN_ITEMS):
                    q = IB["even"] + n
                    bank = item(q)
                    if it[0] == "small":
                        w = C("even_small").rearrange("p (k n) -> p k n", k=KC)
                        for k in range(KC):
                            mm(bank[0:16, 0:T], w[:, k, 0:16], uT[:, k, :], k == 0, k == KC - 1)
                        for k in range(KC):
                            last = mm(bank[0:8, T:2 * T], w[:, k, 16:24], uT[:, k, :], k == 0, k == KC - 1)
                    elif it[0] == "gz":
                        if it[1] == 0:
                            pe.wait_ge(s["item_ev"], IB["even"] + 1)
                        last = mm(bank[:, 0:T], C("gla_gate", it[1] * P, (it[1] + 1) * P)[0:16, :], gsm[0:16, :])
                    elif it[0] == "col":
                        last = col_block(bank, b, it[1])
                    else:
                        _, t, w = it
                        if t == 0 and w:
                            land(b + 5 + w)
                        last = tok_block(bank, b + 5 + w, t, 0 if w else P, 3 * P)
                    last.then_inc(s["item_ps"], 1)
                    if (it[0] == "col" and it[1] % 3 == 2) or (it[0] == "tok" and it[1] == 1):
                        freed(q + 1, b + 5 + it[2] if it[0] == "tok" else b + it[1] // 3)

            def gla():
                pe.wait_ge(s["fox_cs"], 1)
                for t in range(TT):
                    last = pe.transpose(ps[3][:, t * 8:(t + 1) * 8], fsum[0:8, t * P:(t + 1) * P], ident[0:8, 0:8])
                last.then_inc(s["fox_ps"], 1)
                pe.wait_ge(s["gla_k"], 1)
                for c in range(2):
                    last = pe.transpose(ps[2][:, c * P:(c + 1) * P], gkd[:, c, 0:P], ident)
                last.then_inc(s["tok_ps"], 1)
                for t in range(TT):
                    tk = slice(t * P, (t + 1) * P)
                    if t:
                        pe.wait_ge(s["A_read"], 2 * RWKV_UNITS + 1)
                    for h in range(4):
                        c, r = h // 2, HD * (h % 2)
                        last = mm(ps[4 + h % 2][:, c * P:(c + 1) * P], gkd[r:r + HD, c, tk], gqd[r:r + HD, c, tk])
                    last.then_inc(s["A_ps"], 1)
                    pe.wait_ge(s["A_read"], 2 * RWKV_UNITS + t + 1)
                    if t:
                        pe.wait_ge(s["s_ev"], 3)
                        pe.wait_ge(s["y_ev"], 5)
                    for h in range(4):
                        o = ps[1][:, h * P:(h + 1) * P]
                        if t:
                            r = HD * (h % 2)
                            mm(o, gqd[:, h // 2, tk], gS[:, h // 2, (h % 2) * P:(h % 2 + 1) * P], True, False)
                        last = mm(o, gA[:, h, :], evtok[:, t, h * P:(h + 1) * P], not t, True)
                    last.then_inc(s["y_ps"], 1)
                    if not t:
                        pe.wait_ge(s["tok_ev"], 5)
                        for c in range(2):
                            last = mm(ps[6][:, c * 256:(c + 1) * 256], gkt[:, c, :],
                                      evtok[:, 0, c * 256:(c + 1) * 256])
                        last.then_inc(s["s_ps"], 1)

            def odd_in():
                b = BASE["odd_in"]
                for n, it in enumerate(ODD_ITEMS):
                    q = IB["odd"] + n
                    bank = item(q)
                    if it[0] == "col":
                        last = col_block(bank, b, it[1])
                    elif it[0] == "ckv":
                        last = tok_block(bank, b + 4, it[1], P, 3 * P)
                    else:
                        w = C("odd_small").rearrange("p (k n) -> p k n", k=KC)
                        for k in range(KC):
                            last = mm(bank[:, 0:8], uT[:, k, it[1] * P:(it[1] + 1) * P], w[:, k, :],
                                      k == 0, k == KC - 1)
                    last.then_inc(s["item_ps"], 1)
                    if (it[0] == "col" and it[1] % 3 == 2) or it == ("ckv", 1):
                        freed(q + 1, b + 4 if it[0] == "ckv" else b + it[1] // 3)
                pe.wait_ge(s["c_n"], 1)
                for c in range(2):
                    for t in range(TT):
                        last = pe.transpose(ps[3][:, c * T + t * P:c * T + (t + 1) * P],
                                            ckv[:, t, c * P:(c + 1) * P], ident)
                last.then_inc(s["c_ps"], 1)
                pe.wait_ge(s["c_ev"], 1)
                b = BASE["uk_uv"]
                for n, it in enumerate(UKV_ITEMS):
                    q = IB["ukv"] + n
                    bank = item(q)
                    if it[0] == "kh":
                        if it[1] == 0:
                            land(b)
                        w = slot(b).rearrange("p (c n) -> p c n", c=3)
                        for c in range(2):
                            last = mm(bank[:, 0:T], w[:, c, it[1] * P:(it[1] + 1) * P], cT[:, c, :], c == 0, c == 1)
                    else:
                        _, t, half = it
                        if t == 0 and half == 0:
                            land(b + 1)
                        w = slot(b + 1).rearrange("p (c n) -> p c n", c=3)
                        for c in range(2):
                            last = mm(bank[:, :], cT[:, c, t * P:(t + 1) * P], w[:, c, half * 512:(half + 1) * 512],
                                      c == 0, c == 1)
                    last.then_inc(s["item_ps"], 1)
                    if it == ("kh", 7) or it == ("vh", 1, 1):
                        freed(q + 1, b if it[0] == "kh" else b + 1)
                for n in range(16):
                    t, h = n // 8, n % 8
                    r = HD * (h % 2)
                    if n >= 2:
                        pe.wait_ge(s["idx_relu"], n - 1)
                    mm(ps[n % 2][:, 0:P * (t + 1)], qiT[r:r + HD, h // 2, t * P:(t + 1) * P],
                       kiT[r:r + HD, 0:P * (t + 1)]).then_inc(s["idx_ps"], 1)

            def odd_oT():
                for t in range(TT):
                    pe.wait_ge(s["o_ready"], UB["dsa"] + 16 * (t + 1))
                    for half in range(2):
                        for c in range(4):
                            last = pe.transpose(ps[4 * t * 0 + 2 * t + half][:, c * P:(c + 1) * P],
                                                odsa[:, t, (4 * half + c) * P:(4 * half + c + 1) * P], ident)
                        last.then_inc(s["oT_ps"], 1)

            pe.wait_ge(s["consts_loaded"], 16)
            norm_T(0)
            w_in()
            rwkv_tok()
            rwkv_group(0)
            rwkv_group(1)
            tok_T(ytok, 0)
            compress()
            attention("nsa", "cmp_ready", 2)
            for t in range(TT):
                pe.wait_ge(s["o_ready"], UB["fox"] - (24 if t == 0 else 0))
                for c in range(4):
                    last = pe.transpose(ps[2 + t][:, c * P:(c + 1) * P], onsa[:, t, c * P:(c + 1) * P], ident)
                last.then_inc(s["oT_ps"], 1)
            out_proj(0, BASE["w_out"])
            norm_T(1)
            ffn(0)
            norm_T(3)
            ffn(1)
            norm_T(4)
            mm(ps[7][0:16, 0:384], C("t5")[0:32, :], C("t5_onehot")[0:32, :]).then_inc(s["t5_ps"], 1)
            pe.wait_ge(s["t5_sb"], 1)
            even_in()
            gla()
            tok_T(ogla, 2)
            attention("fox", "gla_ready", 2)
            for t in range(TT):
                pe.wait_ge(s["o_ready"], UB["fox"] + 8 * (t + 1))
                for c in range(4):
                    last = pe.transpose(ps[2 + t][:, c * P:(c + 1) * P], ofox[:, t, c * P:(c + 1) * P], ident)
                last.then_inc(s["oT_ps"], 1)
            out_proj(1, BASE["even_out"])
            norm_T(5)
            ffn(2)
            norm_T(6)
            ffn(3)
            norm_T(7)
            odd_in()
            attention("dsa", "idx_relu", 16)
            odd_oT()
            out_proj(2, BASE["odd_out"])
            norm_T(8)
            ffn(4)

        @block.scalar
        def _(act):
            cnt = {}
            ready = dict.fromkeys(names, 0)

            def A(ins, name="a_step", n=1):
                cnt[name] = cnt.get(name, 0) + n
                ins.then_inc(s[name], n)
                act.wait_ge(s[name], cnt[name])

            def gain(n):
                if n >= 2:
                    act.wait_ge(s["xn_ready"], 2 * (n - 1))
                act.dma_start(gb[:, n % 2, :], gains[:, n * D:(n + 1) * D]).then_inc(s[f"gain{n % 2}"], 16)

            def norm(n):
                if n:
                    act.wait_ge(s["x_done"], n)
                else:
                    act.wait_ge(s["x_loaded"], 16)
                for t in range(TT):
                    A(act.activation(xn[:, t, :], x[:, t, :], ACT.Square, accum_out=ss[:, t:t + 1]), "ss_ready")
                if 1 <= n <= 8:
                    gain(n + 1)
                if n in MIX_OF:
                    k = TN[n]
                    for t in range(TT):
                        act.wait_ge(s["xT_ps"], 4 * k + 2 * t + 1)
                        A(act.copy(uT[:, 0:4, t * P:(t + 1) * P],
                                   ps[4 + 2 * t][:, :].rearrange("p (c n) -> p c n", c=4)), "uT_a")
                if n in FFN_OF:
                    f, k = FFN_OF[n], TN[n]
                    hi_a(f, 0)
                    for i in range(4):
                        act.wait_ge(s["xT_ps"], 4 * k + i + 1)
                        c0, t = 4 * (i % 2), i // 2
                        act.copy(uT_r[0][:, c0:c0 + 4, t * P:(t + 1) * P],
                                 ps[4 + i][:, :].rearrange("p (c n) -> p c n", c=4)).then_inc(s["uT_hi"], 1)

            def hi_a(f, c, r=0, rr=0):
                q, i = FC * f, BASE[f"ffn{f}"] + c
                act.wait_ge(s[f"land{i % RING}"], rr + 16 * (i // RING + 1))
                if q + c >= 2:
                    act.wait_ge(s["gu_ps"], r + (q + c - 1))
                act.copy(w_gu[:, c % 2, 0, :], slot(i)[:, 0:2 * D]).then_inc(s["hi_a"], 1)

            def hi_b(f, c, r=0):
                q, i = FC * f, BASE[f"ffn{f}"] + c
                if q + c >= 2:
                    act.wait_ge(s["down_done"], r + (q + c - 1))
                act.copy(w_dn[:, c % 2, 0, :], slot(i)[:, 2 * D:3 * D]).then_inc(s["hi_b"], 1)

            def ffn(f):
                q = FC * f

                def step(c, r=0, rr=0):
                    act.wait_ge(s["gu_ps"], r + (q + c + 1))
                    if q + c >= 2:
                        act.wait_ge(s["h_ready"], r + (q + c - 1))
                    act.activation(sg[:, c % 2, :], ps[4 + c % 2][:, 0:T], ACT.Silu).then_inc(s["silu_ready"], 1)
                    if c + 2 < FC:
                        hi_a(f, c + 2, r, rr)
                    if c + 1 < FC:
                        hi_b(f, c + 1, r)
                hi_b(f, 0)
                hi_a(f, 1)
                step(0)
                step(1)
                with act.Fori(0, 4 * LOOPS, 4) as r:
                    for j in range(4):
                        step(2 + j, r, r * 4)
                for c in range(2 + 4 * LOOPS, FC):
                    step(c)

            def w_in():
                for n, it in enumerate(IN_ITEMS):
                    q = IB["in"] + n
                    act.wait_ge(s["item_ps"], q + 1)
                    bank = ps[4 + q % 4][:, 0:T]
                    name, j = it
                    if name == "col" and j < 14:
                        if j >= 4:
                            act.wait_ge(s["raw_free"], j - 3)
                        A(act.copy(raw[:, j % 4, 1:257], bank), "item_ev")
                        if j == 1:
                            act.wait_ge(s["shift_ready"], 2)
                            A(act.activation(td[0:64, :], lora[0:64, 0, :], ACT.Tanh), "lora_in")
                            A(act.copy(td[64:128, :], lora[64:128, 0, :]), "lora_in")
                            A(act.activation(tg, lora[:, 1, :], ACT.Sigmoid), "lora_in")
                    elif name == "zw":
                        A(act.activation(sgm[:, j, :], bank, ACT.Sigmoid, bias=C("w0", j, j + 1)), "item_ev")
                    elif name == "za":
                        A(act.activation(agm[:, j, :], bank, ACT.Sigmoid, bias=C("a0", j, j + 1)), "item_ev")
                    elif name == "g":
                        A(act.copy(gg[:, j, :], bank), "item_ev")
                    elif name == "col" and j < 18:
                        A(act.mul(qT[:, j - 14, :], bank, HD ** -0.5), "item_ev")
                    elif name == "col" and j in (18, 19):
                        z = (zk, zv)[j - 18]
                        for g in range(2):
                            for par in range(2):
                                ins = act.copy(z[par * HD:(par + 1) * HD, g, :], bank[g * HD:(g + 1) * HD, par:T:2])
                                A(ins, "item_ev" if (g, par) == (1, 1) else "a_step")
                        act.copy(z[:, 2, 0:16], C(("pe_k", "pe_v")[j - 18])).then_inc(s["cmp_z"], 1)
                    elif name == "col" and j in (20, 21):
                        A(act.copy((ksT, kwT)[j - 20], bank), "item_ev")
                    elif name == "tok":
                        A(act.copy(vsw[:, j, :], bank), "item_ev")
                    else:
                        A(act.copy(glT[0:24, :], bank[0:24, :]), "item_ev")
                A(act.activation(glT[0:24, :], glT[0:24, :], ACT.Sigmoid), "gates_ready")
                act.wait_ge(s["kk_clamped"], 1)
                A(act.activation(tmp, tmp, ACT.Sqrt), "kk_sqrt")
                act.wait_ge(s["csm_ready"], 1)
                cm = small[:, 32:40]
                for c in range(4):
                    for t in range(TT):
                        tk = slice(t * P, (t + 1) * P)
                        i = 2 * c + t
                        for o, src, sc, b0 in ((E1, cs, -DECAY, 32), (E2, cs, DECAY, 40), (E3, csp, -DECAY, 32)):
                            act.activation(o[:, c, tk], src[:, c, tk], ACT.Exp, scale=sc,
                                           bias=small[:, b0 + i:b0 + i + 1]).then_inc(s["e_ready"], 1)
                act.activation(small[:, 48:52], small[:, 52:56], ACT.Exp, scale=-DECAY).then_inc(s["e_ready"], 1)

            def rwkv():
                dsts = [vtok[:, 0, :], vtok[:, 1, :], bktok[:, 0, :], bktok[:, 1, :]]
                for n in range(4):
                    act.wait_ge(s["tok_ps"], n + 1)
                    A(act.copy(dsts[n], ps[4 + n][:, :]), "tok_ev")
                for g in range(2):
                    for lv in range(1, LEVELS):
                        e = (LEVELS - 1) * g + lv - 1
                        for half in range(2):
                            act.wait_ge(s["P_ps"], 2 * e + half + 1)
                            A(act.copy(Pb[:, half, :], ps[half][:, :]), "P_ev")
                    for t in range(TT):
                        n = 2 * g + t
                        act.wait_ge(s["rhs_ps"], n + 1)
                        A(act.copy(RH, ps[6][:, 0:256]), "rhs_ev")
                        act.wait_ge(s["sa_ps"], n + 1)
                        A(act.copy(SA, ps[7][:, 0:256]), "sa_ev")
                        act.wait_ge(s["y_ps"], n + 1)
                        A(act.copy(ytok[:, t, g * 256:(g + 1) * 256], ps[6][:, 256:512]), "y_ev")

            def compress():
                act.wait_ge(s["cmp_h"], 2)
                for n in range(2):
                    for half in range(2):
                        A(act.copy(small[:, 56:57], ps[4 + n][:, half * 48 + 30:half * 48 + 31]))
                        A(act.activation(hid[:, n, half, 0:30], ps[4 + n][:, half * 48:half * 48 + 30],
                                         ACT.Gelu_apprx_tanh, bias=small[:, 56:57]),
                          "cmp_hact" if (n, half) == (1, 1) else "a_step")
                act.wait_ge(s["cmp_kv"], 1)
                A(act.copy(kcT[0:64, 0:15], ps[6][0:64, 0:15]))
                A(act.copy(kcT[64:128, 0:15], ps[6][64:128, 15:30]))
                A(act.copy(vc[0:15, :, :], ps[6][0:15, 64:192].rearrange("p (g d) -> p g d", g=2)), "gate_tok")
                act.wait_ge(s["gates_ps"], 1)
                A(act.copy(gtok[:, :, :], ps[7][:, 0:48].rearrange("p (t n) -> p t n", t=2)), "gate_tok")

            def attention(kind):
                units, b = UN[kind], UB[kind]
                n = len(units)
                for i in range(n + 2):
                    if i < n:
                        u, a = b + i, units[i]
                        act.wait_ge(s["max_ready"], u + 1)
                        if u >= 3:
                            act.wait_ge(s["pT_ps"], u - 2)
                        act.activation(Pp[:, u % 3, 0:a["K"]], SS[:, u % 3, 0:a["K"]], ACT.Exp,
                                       bias=nmax[:, u % 4:u % 4 + 1],
                                       accum_out=den[:, u % 8:u % 8 + 1]).then_inc(s["p_ready"], 1)
                    if i >= 2:
                        u, a = b + i - 2, units[i - 2]
                        act.wait_ge(s["pT_ps"], u + 1)
                        if u >= 2:
                            act.wait_ge(s["o_ps"], u - 1)
                        w = min(P, a["K"])
                        nn = P * -(-a["K"] // P)
                        act.copy(PT[0:w, u % 2, 0:nn], ps[3 + u % 2][0:w, 0:nn]).then_inc(s["pT_ev"], 1)

            def even_in():
                for n, it in enumerate(EVEN_ITEMS):
                    q = IB["even"] + n
                    act.wait_ge(s["item_ps"], q + 1)
                    bk = ps[4 + q % 4]
                    bank = bk[:, 0:T]
                    if it[0] == "small":
                        A(act.copy(gsm[0:16, :], bk[0:16, 0:T]))
                        A(act.add(fz[0:8, :], bk[0:8, T:2 * T], C("fox_b")[0:8, :])
                          if False else act.activation(fz[0:8, :], bk[0:8, T:2 * T], ACT.Identity,
                                                       bias=C("fox_b")[0:8, :]), "item_ev")
                    elif it[0] == "gz":
                        A(act.activation(gz[:, it[1], :], bank, ACT.Identity, bias=C("gla_b", it[1], it[1] + 1)),
                          "item_ev")
                    elif it[0] == "col":
                        j = it[1]
                        if j < 2:
                            A(act.mul(gqT[:, j, :], bank, HD ** -0.5), "item_ev")
                        elif j < 4:
                            A(act.copy(gkT[:, j - 2, :], bank), "item_ev")
                        elif j < 8:
                            A(act.activation(goT[:, j - 4, :], bank, ACT.Silu), "item_ev")
                        elif j < 12:
                            A(act.mul(fqT[:, j - 8, :], bank, HD ** -0.5), "item_ev")
                        else:
                            A(act.copy(fkT[:, j - 12, :], bank), "item_ev")
                    else:
                        _, t, w = it
                        lo, nn = (0, 256) if w == 0 else (256 + 384 * (w - 1), 384)
                        A(act.copy(evtok[:, t, lo:lo + nn], bk[:, 0:nn]), "item_ev")
                A(act.activation(gab, gz, ACT.Abs))
                A(act.activation(fab[0:8, :], fz[0:8, :], ACT.Abs))
                A(act.activation(gab, gab, ACT.Exp, scale=-1.0))
                A(act.activation(fab[0:8, :], fab[0:8, :], ACT.Exp, scale=-1.0))
                A(act.activation(gab, gab, ACT.Ln, bias=1.0))
                A(act.activation(fab[0:8, :], fab[0:8, :], ACT.Ln, bias=1.0), "gk_ab")
                act.wait_ge(s["gk_cs"], 1)
                for c in range(2):
                    for t in range(TT):
                        tk = slice(t * P, (t + 1) * P)
                        i = 2 * c + t
                        act.activation(gE1[:, c, tk], gcs[:, c, tk], ACT.Exp, scale=1 / 16.0,
                                       bias=small[:, 64 + i:65 + i]).then_inc(s["e_ready"], 1)
                        act.activation(gE2[:, c, tk], gcs[:, c, tk], ACT.Exp, scale=-1 / 16.0,
                                       bias=small[:, 72 + i:73 + i]).then_inc(s["e_ready"], 1)
                act.activation(small[:, 80:82], small[:, 84:86], ACT.Exp, scale=1 / 16.0).then_inc(s["e_ready"], 1)

            def gla():
                act.wait_ge(s["fox_ps"], 1)
                A(act.copy(ftok, ps[3][:, 0:16].rearrange("p (t h) -> p t h", t=2)), "fox_tok")
                act.wait_ge(s["tok_ps"], 5)
                A(act.copy(gkt, ps[2][:, 0:256].rearrange("p (c n) -> p c n", c=2)), "tok_ev")
                for t in range(TT):
                    act.wait_ge(s["y_ps"], 4 + t + 1)
                    A(act.copy(ogla[:, t, :], ps[1][:, :]), "y_ev")

            def odd_in():
                for n, it in enumerate(ODD_ITEMS):
                    q = IB["odd"] + n
                    act.wait_ge(s["item_ps"], q + 1)
                    bk = ps[4 + q % 4]
                    bank = bk[:, 0:T]
                    j = it[1]
                    if it[0] == "col" and j < 8:
                        A(act.mul(oqT[:, j, :], bank, HD ** -0.5), "item_ev")
                    elif it[0] == "col" and j < 12:
                        A(act.mul(qiT[:, j - 8, :], bank, HD ** -0.5), "item_ev")
                    elif it[0] == "col":
                        A(act.copy(kiT, bank), "item_ev")
                    elif it[0] == "ckv":
                        A(act.copy(ckv[:, j, :], bank), "item_ev")
                    else:
                        A(act.mul(wtok[:, j, :], bk[:, 0:8], 8 ** -0.5), "item_ev")
                for t in range(TT):
                    A(act.activation(csc, ckv[:, t, :], ACT.Square, accum_out=small[:, 88 + t:89 + t]), "c_ss")
                act.wait_ge(s["c_ps"], 1)
                for c in range(2):
                    A(act.mul(cT[:, c, :], ps[3][:, c * T:(c + 1) * T], C("kv_norm", c, c + 1)),
                      "c_ev" if c else "a_step")
                for n, it in enumerate(UKV_ITEMS):
                    q = IB["ukv"] + n
                    act.wait_ge(s["item_ps"], q + 1)
                    bk = ps[4 + q % 4]
                    if it[0] == "kh":
                        A(act.copy(khT[:, it[1], :], bk[:, 0:T]), "item_ev")
                    else:
                        A(act.copy(vh[:, it[1], it[2] * 512:(it[2] + 1) * 512], bk[:, :]), "item_ev")
                for n in range(16):
                    K = P * (n // 8 + 1)
                    act.wait_ge(s["idx_ps"], n + 1)
                    if n >= 2:
                        act.wait_ge(s["idx_acc"], n - 1)
                    act.activation(idxs[:, n % 2, 0:K], ps[n % 2][:, 0:K], ACT.Relu).then_inc(s["idx_relu"], 1)

            act.dma_start(cst[:], consts_in).then_inc(s["consts_loaded"], 16)
            gain(0)
            gain(1)
            act.dma_start(W(5120, MASKS), masks_in).then_inc(s["masks_loaded"], 16)
            act.wait_ge(s["consts_loaded"], 16)
            norm(0)
            w_in()
            rwkv()
            compress()
            attention("nsa")
            norm(1)
            ffn(0)
            norm(2)
            norm(3)
            ffn(1)
            norm(4)
            act.wait_ge(s["t5_ps"], 1)
            A(act.copy(ffb[0:16, 0:2, :].rearrange("p a b -> p (a b)")[:, 0:384], ps[7][0:16, 0:384]), "t5_sb")
            act.dma_start(scratch, ffb[0:16, 0:2, :].rearrange("p a b -> p (a b)")[:, 0:384]).then_inc(s["t5_out"], 16)
            even_in()
            gla()
            attention("fox")
            act.wait_ge(s["t5_out"], 16)
            norm(5)
            ffn(2)
            norm(6)
            ffn(3)
            norm(7)
            act.dma_start(bias16, bass.AP(scratch.tensor, 0, [[1, P], [384, 16], [1, T]])).then_inc(s["t5_in"], 16)
            odd_in()
            attention("dsa")
            norm(8)
            ffn(4)
            norm(9)

        @block.gpsimd
        def _(gp):
            cnt = {}

            def G(ins, name="g_step"):
                cnt[name] = cnt.get(name, 0) + 1
                ins.then_inc(s[name], 1)
                gp.wait_ge(s[name], cnt[name])

            def rsqrt(o, i, scale, eps, name):
                n = i.shape[1]
                G(gp.tensor_scalar(o, i, scale, eps, ALU.mult, ALU.add))
                G(gp.tensor_tensor(o, o, C("neg_half", 0, n), ALU.pow), name)

            def norm(n):
                gp.wait_ge(s["ss_ready"], 2 * (n + 1))
                rsqrt(rstd, ss, 1.0 / D, 1e-6, "rstd_ready")

            def identities():
                for M in (Mm, Mt):
                    G(gp.tensor_copy(M, ident.unsqueeze(1).to_broadcast([P, RWKV_UNITS, P])), "id_ready")

            gp.wait_ge(s["consts_loaded"], 16)
            gp.wait_ge(s["masks_loaded"], 16)
            G(gp.tensor_copy(msk[:], W(5120, MASKS)), "masks_ready")
            G(gp.memset(raw[:, :, 0:1], 0.0), "scan_in")
            G(gp.memset(zk[:, 2, :], 0.0), "scan_in")
            G(gp.memset(zv[:, 2, :], 0.0), "scan_in")
            norm(0)
            gp.wait_ge(s["ab_ready"], 1)
            G(gp.memset(AA, 0.0), "id_ready")
            G(gp.memset(Sst, 0.0), "id_ready")
            for g in range(2):
                if g:
                    gp.wait_ge(s["y_ps"], 2)
                identities()
            for t in range(TT):
                gp.wait_ge(s["var_ready"], t + 1)
                rsqrt(small[:, 96 + 8 * t:104 + 8 * t], small[:, 112 + 8 * t:120 + 8 * t], 1.0 / HD, 64e-5, "grs_ready")
            norm(1)
            norm(2)
            norm(3)
            norm(4)
            gp.wait_ge(s["gla_k"], 1)
            G(gp.memset(gA, 0.0), "id_ready")
            G(gp.memset(gS, 0.0), "id_ready")
            for t in range(TT):
                gp.wait_ge(s["var_ready"], 2 + t + 1)
                rsqrt(small[:, 128 + 4 * t:132 + 4 * t], small[:, 136 + 4 * t:140 + 4 * t], 1.0 / P, 1e-6, "grs_ready")
            norm(5)
            norm(6)
            norm(7)
            gp.wait_ge(s["c_ss"], 2)
            rsqrt(small[:, 90:92], small[:, 88:90], 1.0 / 256, 1e-6, "c_rs")
            norm(8)
            norm(9)

        @block.vector
        def _(v):
            cnt = {}

            def V(ins, name="v_step"):
                cnt[name] = cnt.get(name, 0) + 1
                ins.then_inc(s[name], 1)
                v.wait_ge(s[name], cnt[name])

            def norm(n, dst=None):
                v.wait_ge(s[f"gain{n % 2}"], 16 * (n // 2 + 1))
                v.wait_ge(s["rstd_ready"], n + 1)
                for t in range(TT):
                    V(v.scalar_tensor_tensor((xn if dst is None else dst)[:, t, :], x[:, t, :], rstd[:, t:t + 1],
                                             gb[:, n % 2, :], ALU.mult, ALU.mult), "xn_ready")
                if n in MIX_OF:
                    k = TN[n]
                    for t in range(TT):
                        v.wait_ge(s["xT_ps"], 4 * k + 2 * t + 2)
                        V(v.tensor_copy(uT[:, 4:8, t * P:(t + 1) * P],
                                        ps[5 + 2 * t][:, :].rearrange("p (c n) -> p c n", c=4)), "uT_v")
                if n in FFN_OF:
                    f = FFN_OF[n]
                    lo_a(f, 0)
                    for i in range(4):
                        v.wait_ge(s["uT_hi"], 4 * f + i + 1)
                        c0, t = 4 * (i % 2), i // 2
                        v.tensor_tensor(uT_r[1][:, c0:c0 + 4, t * P:(t + 1) * P],
                                        ps[4 + i][:, :].rearrange("p (c n) -> p c n", c=4),
                                        uT_r[0][:, c0:c0 + 4, t * P:(t + 1) * P].bitcast(F32),
                                        ALU.subtract).then_inc(s["uT_lo"], 1)

            def lo_a(f, c, r=0):
                q, i = FC * f, BASE[f"ffn{f}"] + c
                v.wait_ge(s["hi_a"], r + (q + c + 1))
                v.tensor_tensor(w_gu[:, c % 2, 1, :], slot(i)[:, 0:2 * D], w_gu[:, c % 2, 0, :].bitcast(F32),
                                ALU.subtract).then_inc(s["lo_a"], 1)

            def lo_b(f, c, r=0):
                q, i = FC * f, BASE[f"ffn{f}"] + c
                v.wait_ge(s["hi_b"], r + (q + c + 1))
                v.tensor_tensor(w_dn[:, c % 2, 1, :], slot(i)[:, 2 * D:3 * D], w_dn[:, c % 2, 0, :].bitcast(F32),
                                ALU.subtract).then_inc(s["lo_b"], 1)
                v.wait_ge(s["lo_b"], r + (q + c + 1))
                v.sem_inc(s[f"free{i % RING}"], 1)

            def residual(scale):
                for t in range(TT):
                    for half in range(2):
                        xs = x[:, t, half * 512:(half + 1) * 512]
                        V(v.scalar_tensor_tensor(xs, ps[2 * t + half][:, :], scale, xs, ALU.mult, ALU.add),
                          "x_done" if (t, half) == (1, 1) else "v_step")

            def ffn(f, scale):
                q = FC * f

                def step(c, r=0):
                    n = q + c
                    v.wait_ge(s["silu_ready"], r + (n + 1))
                    h, hr = sg[:, c % 2, :], h_r[:, c % 2, :, :]
                    v.tensor_tensor(h, h, ps[4 + c % 2][:, T:2 * T], ALU.mult).then_inc(s["h_mul"], 1)
                    v.wait_ge(s["h_mul"], r + (n + 1))
                    if n >= 2:
                        v.wait_ge(s["down_done"], r + (n - 1))
                    v.tensor_copy(hr[:, 0, :], h).then_inc(s["h_hi"], 1)
                    v.wait_ge(s["h_hi"], r + (n + 1))
                    v.tensor_tensor(hr[:, 1, :], h, hr[:, 0, :].bitcast(F32), ALU.subtract).then_inc(s["h_ready"], 1)
                    if c + 2 < FC:
                        lo_a(f, c + 2, r)
                    if c + 1 < FC:
                        lo_b(f, c + 1, r)
                lo_b(f, 0)
                lo_a(f, 1)
                step(0)
                step(1)
                with v.Fori(0, 4 * LOOPS, 4) as r:
                    for j in range(4):
                        step(2 + j, r)
                for c in range(2 + 4 * LOOPS, FC):
                    step(c)
                v.wait_ge(s["down_done"], q + FC)
                residual(scale)

            def w_in():
                v.wait_ge(s["scan_in"], 3)
                order = {j: n for n, it in enumerate(IN_ITEMS) if it[0] == "col" for j in [it[1]]}
                dst = [lora[:, 0, :], lora[:, 1, :]] + [m[:, j, :] for m in (pk, pr, pv) for j in range(4)]
                for j in range(14):
                    v.wait_ge(s["item_ev"], IB["in"] + order[j] + 1)
                    V(v.tensor_tensor(dst[j], raw[:, j % 4, 0:256], raw[:, j % 4, 1:257], ALU.subtract))
                    V(v.scalar_tensor_tensor(dst[j], dst[j], C("mu", j, j + 1), raw[:, j % 4, 1:257],
                                             ALU.mult, ALU.add), "shift_ready")
                    v.sem_inc(s["raw_free"], 1)
                    if j == 1:
                        continue
                for c in range(4):
                    V(v.tensor_scalar(kk[:, c, :], pk[:, c, :], C("k_k", c, c + 1), None, ALU.mult))
                v.wait_ge(s["masks_ready"], 1)
                V(v.tensor_tensor(tmp, kk, kk, ALU.mult), "kk_sq")
                v.wait_ge(s["n2_ps"], 1)
                for c in range(2):
                    V(v.tensor_scalar(tmp[:, 2 * c:2 * c + 2, :], ps[c][:, :].rearrange("p (a b) -> p a b", a=2),
                                      1e-24, None, ALU.max), "kk_clamped" if c else "v_step")
                v.wait_ge(s["kk_sqrt"], 1)
                V(v.reciprocal(tmp, tmp))
                V(v.tensor_tensor(kk, kk, tmp, ALU.mult))
                for c in range(4):
                    V(v.tensor_scalar(tmp[:, c, :], agm[:, c, :], -1.0, C("k_a", c, c + 1), ALU.add, ALU.mult))
                V(v.scalar_tensor_tensor(kp, tmp, 1.0, pk, ALU.add, ALU.mult))
                for c in range(4):
                    V(v.scalar_tensor_tensor(tmp[:, c, :], pr[:, c, :], C("r_k", c, c + 1), kp[:, c, :],
                                             ALU.mult, ALU.mult), "rk_ready" if c == 3 else "v_step")
                for c in range(4):
                    for t in range(TT):
                        tk = slice(t * P, (t + 1) * P)
                        V(v.tensor_tensor_scan(cs[:, c, tk], C("ones"), sgm[:, c, tk], 0.0, ALU.mult, ALU.add))
                V(v.tensor_tensor(csp, cs, sgm, ALU.subtract))
                mid = cs.rearrange("p c (t n) -> p (c t) n", t=2)
                V(v.tensor_scalar(small[:, 32:40], mid[:, :, 63], DECAY, None, ALU.mult))
                V(v.tensor_scalar(small[:, 40:48], mid[:, :, 63], -DECAY, None, ALU.mult))
                V(v.tensor_tensor(small[:, 52:56], cs[:, :, 127], cs[:, :, 63], ALU.subtract))
                V(v.tensor_tensor(small[:, 52:56], small[:, 52:56], cs[:, :, 191], ALU.add), "csm_ready")
                v.wait_ge(s["e_ready"], 25)
                arv = arT.rearrange("p c t (w n) -> p c t w n", w=2)
                for c in range(4):
                    re = lambda a: a[:, c, :].rearrange("p (t n) -> p t n", t=2)
                    V(v.scalar_tensor_tensor(arv[:, c, :, 0, :], re(kk), -1.0, re(E3), ALU.mult, ALU.mult))
                    V(v.tensor_tensor(arv[:, c, :, 1, :], re(pr), re(E1), ALU.mult))
                V(v.tensor_tensor(bT, kk, agm, ALU.mult))
                V(v.tensor_tensor(bT, bT, E2, ALU.mult))
                V(v.tensor_tensor(kT_, kp, E2, ALU.mult), "ab_ready")

            def rwkv():
                v.wait_ge(s["bon_ps"], 1)
                v.wait_ge(s["tok_ps"], 2)
                for c in range(2):
                    V(v.tensor_tensor(pv[:, 2 * c:2 * c + 2, :], ps[2 + c][:, :].rearrange("p (a b) -> p a b", a=2),
                                      pv[:, 2 * c:2 * c + 2, :], ALU.mult), "bonus_read" if c else "v_step")
                for g in range(2):
                    v.wait_ge(s["id_ready"], 2 + 2 * (g + 1))
                    for u in range(RWKV_UNITS):
                        uu = RWKV_UNITS * g + u
                        v.wait_ge(s["A_ps"], uu + 1)
                        V(v.copy_predicated(Mt[:, u, :], mask(LEVELS), ps[u % 4][:, 0:P]))
                        if g:
                            pass
                        V(v.copy_predicated(AA[:, u, :], msk[:, 0:512], ps[u % 4][:, :]), "A_read")
                        if u % 4 == 3:
                            h = u // 4
                            for par in range(2):
                                V(v.copy_predicated(Mm[:, 4 * h + par:4 * h + 4:2, :],
                                                    mask(0).unsqueeze(1).to_broadcast([P, 2, P]),
                                                    ps[4 + 2 * h + par][:, 0:256].rearrange("p (u n) -> p u n", u=2)),
                                  "M_ready" if par else "v_step")
                    for lv in range(1, LEVELS):
                        e = (LEVELS - 1) * g + lv - 1
                        for half in range(2):
                            v.wait_ge(s["dM_ps"], 2 * e + half + 1)
                            hs = slice(4 * half, 4 * half + 4)
                            if lv < LEVELS - 1:
                                V(v.copy_predicated(Mm[:, hs, :], mask(lv).unsqueeze(1).to_broadcast([P, 4, P]),
                                                    ps[2 + half][:, :].rearrange("p (u n) -> p u n", u=4)))
                            V(v.copy_predicated(Mt[:, hs, :],
                                                mask(LEVELS + lv).unsqueeze(1).to_broadcast([P, 4, P]),
                                                ps[4 + half][:, :].rearrange("p (u n) -> p u n", u=4)), "M_ready")
                    v.wait_ge(s["s_ps"], g + 1)
                    for hh in range(2):
                        r = slice(hh * HD, (hh + 1) * HD)
                        for c in range(2):
                            V(v.tensor_scalar(Sst[r, c, hh * HD:(hh + 1) * HD],
                                              ps[7][r, 256 + c * P + hh * HD:256 + c * P + (hh + 1) * HD],
                                              small[r, 48 + 2 * g + c:49 + 2 * g + c], None, ALU.mult),
                              "s_ev" if (hh, c) == (1, 1) else "v_step")
                for t in range(TT):
                    v.wait_ge(s["y_ev"], 3 + t)
                    yv = ytok[:, t, :].rearrange("p (h n) -> p h n", h=8)
                    sq = AA[:, 0, :].rearrange("p (h n) -> p h n", h=8)
                    mean = small[:, 144:152]
                    if t == 0:
                        v.wait_ge(s["y_ps"], 4)
                    V(v.tensor_reduce(mean, yv, AX.X, ALU.add))
                    V(v.tensor_scalar(mean, mean, 1.0 / HD, None, ALU.mult))
                    V(v.tensor_tensor(yv, yv, mean.unsqueeze(2).to_broadcast([P, 8, HD]), ALU.subtract))
                    V(v.tensor_tensor(sq, yv, yv, ALU.mult))
                    V(v.tensor_reduce(small[:, 112 + 8 * t:120 + 8 * t], sq, AX.X, ALU.add), "var_ready")
                    v.wait_ge(s["grs_ready"], t + 1)
                    V(v.tensor_tensor(yv, yv, small[:, 96 + 8 * t:104 + 8 * t].unsqueeze(2).to_broadcast([P, 8, HD]),
                                      ALU.mult), "yn_ready")
                for t in range(TT):
                    v.wait_ge(s["ynT_ps"], t + 1)
                    tk = slice(t * P, (t + 1) * P)
                    for c in range(4):
                        V(v.tensor_scalar(yT[:, c, tk], ps[t][:, c * P:(c + 1) * P], C("lnx_w", c, c + 1),
                                          C("lnx_b", c, c + 1), ALU.mult, ALU.add))
                    V(v.tensor_tensor(yT[:, 0:4, tk], yT[:, 0:4, tk], pv[:, :, tk], ALU.add))
                    V(v.tensor_tensor(yT[:, 0:4, tk], yT[:, 0:4, tk], gg[:, :, tk], ALU.mult))

            def compress():
                v.wait_ge(s["gate_tok"], 2)
                for t in range(TT):
                    gv = gtok[:, t, :].rearrange("p (h b) -> p h b", b=3)[:, :, 0]
                    V(v.tensor_scalar(gv, gv, C("any_ok", t, t + 1), None, ALU.mult), "cmp_ready")

            def attention(kind):
                units, b = UN[kind], UB[kind]
                n = len(units)

                def result(i):
                    u, a = b + i, units[i]
                    v.wait_ge(s["o_ps"], u + 1)
                    V(v.reciprocal(rden, den[:, u % 8:u % 8 + 1]))
                    o = ps[5 + u % 2][:, 0:HD]
                    if a["gate"] is not None:
                        V(v.tensor_tensor(rden, rden, a["gate"], ALU.mult))
                    if a["add"]:
                        V(v.scalar_tensor_tensor(a["out"], o, rden, a["out"], ALU.mult, ALU.add), "o_ready")
                    else:
                        V(v.tensor_scalar(a["out"], o, rden, None, ALU.mult), "o_ready")

                for i in range(n):
                    u, a = b + i, units[i]
                    K = a["K"]
                    v.wait_ge(s["S_ps"], u + 1)
                    if u >= 3:
                        v.wait_ge(s["p_ready"], u - 2)
                    sc, o = ps[u % 3][:, 0:K], SS[:, u % 3, 0:K]
                    if "slope" in a:
                        V(v.scalar_tensor_tensor(o, a["dist"], a["slope"], sc, ALU.mult, ALU.add))
                    elif "row" in a:
                        V(v.scalar_tensor_tensor(o, sc, a["row"], a["dist"], ALU.add, ALU.add))
                    else:
                        V(v.tensor_tensor(o, sc, a["dist"], ALU.add))
                    V(v.tensor_reduce(nmax[:, u % 4:u % 4 + 1], o, AX.X, ALU.max, negate=True), "max_ready")
                    if i >= 4:
                        result(i - 4)
                for i in range(n - 4, n):
                    result(i)

            def mix_T(n0, c0):
                for t in range(TT):
                    v.wait_ge(s["oT_ps"], n0 + t + 1)
                    V(v.tensor_copy(yT[:, c0:c0 + 4, t * P:(t + 1) * P],
                                    ps[2 + t][:, :].rearrange("p (c n) -> p c n", c=4)),
                      "mix_ready" if t else "v_step")

            def even_in():
                v.wait_ge(s["item_ev"], IB["even"] + len(EVEN_ITEMS))
                V(v.tensor_scalar(gmn, gz, 0.0, None, ALU.min))
                V(v.tensor_scalar(fmn[0:8, :], fz[0:8, :], 0.0, None, ALU.min))
                v.wait_ge(s["gk_ab"], 1)
                V(v.tensor_tensor(gmn, gmn, gab, ALU.subtract))
                V(v.tensor_tensor(fmn[0:8, :], fmn[0:8, :], fab[0:8, :], ALU.subtract))
                for t in range(TT):
                    V(v.tensor_tensor_scan(fsum[0:8, t * P:(t + 1) * P], C("ones")[0:8, :],
                                           fmn[0:8, t * P:(t + 1) * P],
                                           fsum[0:8, t * P - 1:t * P] if t else 0.0, ALU.mult, ALU.add),
                      "fox_cs" if t else "v_step")
                V(v.tensor_scalar(fneg[0:8, :], fsum[0:8, :], -1.0, None, ALU.mult))
                for c in range(2):
                    for t in range(TT):
                        tk = slice(t * P, (t + 1) * P)
                        V(v.tensor_tensor_scan(gcs[:, c, tk], C("ones"), gmn[:, c, tk], 0.0, ALU.mult, ALU.add))
                mid = gcs.rearrange("p c (t n) -> p (c t) n", t=2)
                V(v.tensor_scalar(small[:, 64:68], mid[:, :, 63], -1 / 16.0, None, ALU.mult))
                V(v.tensor_scalar(small[:, 72:76], mid[:, :, 63], 1 / 16.0, None, ALU.mult))
                V(v.tensor_tensor(small[:, 84:86], gcs[:, :, 127], gcs[:, :, 63], ALU.subtract))
                V(v.tensor_tensor(small[:, 84:86], small[:, 84:86], gcs[:, :, 191], ALU.add), "gk_cs")
                v.wait_ge(s["e_ready"], 25 + 9)
                V(v.tensor_tensor(gqd, gqT, gE1, ALU.mult))
                V(v.tensor_tensor(gkd, gkT, gE2, ALU.mult), "gla_k")

            def gla():
                v.wait_ge(s["id_ready"], 8)
                for t in range(TT):
                    v.wait_ge(s["A_ps"], 2 * RWKV_UNITS + t + 1)
                    if t:
                        v.wait_ge(s["y_ps"], 5)
                    for par in range(2):
                        V(v.copy_predicated(gA[:, par:4:2, :], msk[:, P:2 * P].unsqueeze(1).to_broadcast([P, 2, P]),
                                            ps[4 + par][:, 0:256].rearrange("p (h n) -> p h n", h=2)),
                          "A_read" if par else "v_step")
                    if not t:
                        v.wait_ge(s["s_ps"], 3)
                        for hh in range(2):
                            r = slice(hh * HD, (hh + 1) * HD)
                            for c in range(2):
                                V(v.tensor_scalar(gS[r, c, hh * P:(hh + 1) * P],
                                                  ps[6][r, c * 256 + hh * P:c * 256 + (hh + 1) * P],
                                                  small[r, 80 + c:81 + c], None, ALU.mult),
                                  "s_ev" if (hh, c) == (1, 1) else "v_step")
                for t in range(TT):
                    v.wait_ge(s["y_ev"], 5 + t)
                    yv = ogla[:, t, :].rearrange("p (h n) -> p h n", h=4)
                    sq = gsq.rearrange("p (h n) -> p h n", h=4)
                    V(v.tensor_tensor(sq, yv, yv, ALU.mult))
                    V(v.tensor_reduce(small[:, 136 + 4 * t:140 + 4 * t], sq, AX.X, ALU.add), "var_ready")
                    v.wait_ge(s["grs_ready"], 3 + t)
                    V(v.tensor_tensor(yv, yv, small[:, 128 + 4 * t:132 + 4 * t].unsqueeze(2).to_broadcast([P, 4, P]),
                                      ALU.mult), "yn_ready")
                for t in range(TT):
                    v.wait_ge(s["ynT_ps"], 3 + t)
                    tk = slice(t * P, (t + 1) * P)
                    V(v.scalar_tensor_tensor(yT[:, 0:4, tk], ps[t][:, :].rearrange("p (c n) -> p c n", c=4),
                                             C("gla_norm"), goT[:, :, tk], ALU.mult, ALU.mult), "gla_ready")

            def odd_in():
                v.wait_ge(s["c_rs"], 1)
                for t in range(TT):
                    V(v.tensor_scalar(ckv[:, t, :], ckv[:, t, :], small[:, 90 + t:91 + t], None, ALU.mult),
                      "c_n" if t else "v_step")
                for t in range(TT):
                    K = P * (t + 1)
                    for h in range(8):
                        n = 8 * t + h
                        v.wait_ge(s["idx_relu"], n + 1)
                        rl, sc = idxs[:, n % 2, 0:K], score[:, 0:K]
                        if h:
                            V(v.scalar_tensor_tensor(sc, rl, wtok[:, t, h:h + 1], sc, ALU.mult, ALU.add), "idx_acc")
                        else:
                            V(v.tensor_scalar(sc, rl, wtok[:, t, h:h + 1], None, ALU.mult), "idx_acc")
                    causal = C("causal", P * (1 - t), P * (1 - t) + K)
                    V(v.tensor_tensor(sc, sc, causal, ALU.add))
                    for r in range(TOPK // 8):
                        V(v.max(small[:, 152:160], sc))
                        V(v.match_replace(sc, small[:, 152:160], sc, -3e38))
                    V(v.tensor_scalar(sc, sc, -2e38, NEG, ALU.is_gt, ALU.mult))
                    V(v.tensor_tensor(selm[:, t, 0:K], sc, causal, ALU.add), "sel_ready")

            norm(0)
            w_in()
            rwkv()
            compress()
            attention("nsa")
            mix_T(0, 4)
            v.wait_ge(s["op_acc"], 1)
            residual(1.0)
            norm(1)
            ffn(0, 1.0)
            norm(2, x)
            V(v.tensor_copy(small[:, 160:161], small[:, 0:1]), "x_done")
            norm(3)
            ffn(1, 0.5)
            norm(4)
            even_in()
            gla()
            v.wait_ge(s["fox_tok"], 1)
            attention("fox")
            mix_T(2, 4)
            v.wait_ge(s["op_acc"], 2)
            residual(1.0)
            norm(5)
            ffn(2, 0.5)
            norm(6)
            ffn(3, 0.5)
            norm(7)
            odd_in()
            attention("dsa")
            for t in range(TT):
                for half in range(2):
                    v.wait_ge(s["oT_ps"], 4 + 2 * t + half + 1)
                    V(v.tensor_copy(yT[:, 4 * half:4 * half + 4, t * P:(t + 1) * P],
                                    ps[2 * t + half][:, :].rearrange("p (c n) -> p c n", c=4)),
                      "mix_ready" if (t, half) == (1, 1) else "v_step")
            v.wait_ge(s["op_acc"], 3)
            residual(1.0)
            norm(8)
            ffn(4, 0.5)
            norm(9, x)


def column_blocks(w, cols, width=3 * P):
    cols = np.concatenate([cols, np.full((-len(cols)) % width, -1)])
    w = np.concatenate([w, np.zeros((w.shape[0], 1), w.dtype)], axis=1)[:, cols]
    return [np.ascontiguousarray(w[:, i:i + width].reshape(KC, P, width).transpose(1, 0, 2)).reshape(P, SLOT)
            for i in range(0, len(cols), width)]


def row_blocks(w):
    w = np.concatenate([w, np.zeros((P, D), w.dtype)]).reshape(3, 3, P, D)
    return [np.ascontiguousarray(w[i].transpose(1, 0, 2)).reshape(P, SLOT) for i in range(3)]


def ffn_slots(gate, up, down):
    g, u = (m.reshape(KC, P, FC, P).transpose(2, 1, 0, 3).reshape(FC, P, D) for m in (gate, up))
    return list(np.concatenate([g, u, down.reshape(FC, P, D)], axis=2))


def padded(a, n=SLOT):
    return np.concatenate([a, np.zeros((P, n - a.shape[1]), a.dtype)], axis=1)


def rows(a):
    return np.concatenate([a, np.zeros((P - a.shape[0], a.shape[1]), a.dtype)])


def columns(vec):
    return np.ascontiguousarray(vec.reshape(-1, P).T)


def lay_out(i):
    r = np.arange
    w_in, od, ev = i["w_in"][0], i["odd_w_in_2"][0], i["even_w_in_2"][0]
    q0 = 1792
    rwkv = np.concatenate([r(1536, 1792), r(512, 1024), r(0, 512), r(1024, 1536)])
    q = np.concatenate([q0 + h * HD + r(HD) for j in range(4) for h in (j, j + 4)])
    kv = q0 + 512
    in_cols = np.concatenate([rwkv, q, kv + r(256), kv + 256 + r(128), kv + 512 + r(128), kv + 384 + r(128),
                              kv + 640 + r(128)])
    slots = column_blocks(w_in, in_cols)
    pieces = np.concatenate([i["nsa_cmp_k_w1"][0], i["nsa_cmp_v_w1"][0]]).reshape(32, P, 256)
    for a in range(0, 32, 12):
        slots.append(padded(pieces[a:a + 12].transpose(1, 0, 2).reshape(P, -1)))
    slots += row_blocks(i["w_out"][0])
    slots += ffn_slots(i["ffn_w_gate"][0], i["ffn_w_up"][0], i["ffn_w_down"][0])
    f_in, f_out = i["ffn_w_in_2"], i["ffn_w_out_2"]

    def ffn2(layer, n):
        return ffn_slots(f_in[layer, n][:, :F], f_in[layer, n][:, F:], f_out[layer, n])
    slots += ffn2(0, 0)
    e_cols = np.concatenate([r(0, 512), 1024 + r(512), 1552 + r(1024), 512 + r(512), 2576 + r(512)])
    slots += column_blocks(ev, e_cols)
    slots += row_blocks(i["even_w_out_2"][0])
    slots += ffn2(0, 1) + ffn2(1, 0)
    o_cols = np.concatenate([r(1024), 1280 + r(512), 1792 + r(64), 1792 + r(64), 1024 + r(256)])
    slots += column_blocks(od, o_cols)
    uk = i["mla_w_uk_2"][0].transpose(2, 0, 1).reshape(2, P, D).transpose(1, 0, 2).reshape(P, 2 * D)
    uv = i["mla_w_uv_2"][0].transpose(1, 0, 2).reshape(2, P, D).transpose(1, 0, 2).reshape(P, 2 * D)
    slots += [padded(uk), padded(uv)]
    slots += row_blocks(i["odd_w_out_2"][0])
    slots += ffn2(1, 1)
    wstream = np.stack(slots)
    assert wstream.shape == (NSLOTS, P, SLOT)

    gains = [i["norm1_g"][0], i["norm2_g"][0], i["norm_f_g"]] + [i["norm_g_2"][a, b] for a in range(2) for b in range(3)]
    gains = np.concatenate(gains + [i["final_norm_g_2"]])
    gains = np.ascontiguousarray(np.broadcast_to(gains, (P, gains.size)))

    def small_w(w, cols):
        return w[:, cols].reshape(KC, P, len(cols)).transpose(1, 0, 2).reshape(P, -1)

    z64 = np.zeros((64, 512), np.float32)
    ck2 = i["nsa_cmp_k_w2"][0].reshape(2, P, HD).transpose(1, 0, 2)
    cv2 = i["nsa_cmp_v_w2"][0].reshape(2, P, HD).transpose(1, 0, 2).reshape(P, P)
    p_, c_ = np.arange(P)[:, None], np.arange(T)[None, :]
    dist = P + p_ - c_
    causal = np.where(dist >= 0, 0.0, NEG)
    end = np.arange(16)[None, :] * CMP_STRIDE + 31
    cmp_d = np.concatenate([np.where(end <= t * P + p_, -np.abs(t * P + p_ - end).astype(np.float64), NEG)
                            for t in range(TT)], axis=1)
    d = np.maximum(255 - np.arange(384), 0)
    large = 16 + (np.log(np.maximum(d, 1) / 16) / np.log(8.0) * 16 + 1e-9).astype(np.int64)
    bucket = np.where(d < 16, d, np.minimum(large, 31))
    c = {
        "ident": np.eye(P), "reverse": np.eye(P)[::-1], "pair_ones": np.kron(np.eye(2), np.ones((HD, HD))), "ones": np.ones((P, P)),
        "w2": np.concatenate([i["rwkv_w2"][0], z64]), "a2": np.concatenate([z64, i["rwkv_a2"][0]]),
        "g2": i["rwkv_g2"][0], "gate_w": small_w(w_in, q0 + 1280 + r(24)),
        "even_small": small_w(ev, np.concatenate([1536 + r(16), 3088 + r(8)])), "odd_small": small_w(od, 1856 + r(8)),
        "gla_gate": rows(i["gla_w_gate_2"][0]), "ck2": np.concatenate([ck2, ck2], axis=2).reshape(P, 256), "cv2": cv2,
        "pe_k": i["nsa_pe_k"][0].reshape(16, P).T, "pe_v": i["nsa_pe_v"][0].reshape(16, P).T,
        "t5": rows(i["t5_table_2"]), "t5_onehot": rows((bucket[None, :] == np.arange(32)[:, None]).astype(np.float32)),
        "alibi": np.where(dist >= 0, -dist, NEG), "alibi_cmp": cmp_d,
        "any_ok": np.concatenate([(p_ + t * P >= 31).astype(np.float32) for t in range(TT)], axis=1),
        "causal": causal, "neg_half": np.full((P, 32), -0.5),
        "mu": columns(i["mu_shift"][0][rwkv]), "w0": columns(i["rwkv_w0"][0]), "a0": columns(i["rwkv_a0"][0]),
        "k_k": columns(i["rwkv_k_k"][0]), "k_a": columns(i["rwkv_k_a"][0]), "r_k": columns(i["rwkv_r_k"][0].reshape(-1)),
        "lnx_w": columns(i["rwkv_lnx_w"][0]), "lnx_b": columns(i["rwkv_lnx_b"][0]), "gla_b": columns(i["gla_b_gate_2"][0]),
        "gla_norm": columns(i["gla_norm_g_2"][0]), "fox_b": rows(i["fox_b_f_2"][0][:, None]),
        "kv_norm": columns(i["mla_kv_norm_g_2"][0]),
    }
    for name, n in CONSTS:
        assert c[name].shape == (P, n), (name, c[name].shape)
    consts = np.concatenate([c[name].astype(np.float32) for name, _ in CONSTS], axis=1)
    strict, incl = (p_ < p_.T), (p_ <= p_.T)
    below = [((p_ // b) % 2 == 1) & (p_.T // b == p_ // b - 1) for b in (1 << lv for lv in range(LEVELS))]
    masks = np.concatenate([strict, incl, strict, incl] + below + [m.T for m in below], axis=1).astype(np.float32)
    return {"x_in": np.ascontiguousarray(i["x"][0]), "wstream": wstream, "gains": gains, "consts_in": consts,
            "masks_in": masks}


def kernel(**inputs):
    import concourse.bacc as bacc
    from concourse.bass_utils import run_bass_kernel_spmd
    arrays = lay_out({k: np.asarray(v) for k, v in inputs.items()})
    nc = bacc.Bacc("TRN2", target_bir_lowering=False, num_devices=1)
    args = {n: nc.dram_tensor(n, a.shape, F32, kind="ExternalInput").ap() for n, a in arrays.items()}
    scratch = nc.dram_tensor("t5_row", (16, 384), F32, kind="Internal").ap()
    out = nc.dram_tensor("out_dram", (T, D), F32, kind="ExternalOutput").ap()
    build(nc, **args, scratch=scratch, out=out)
    r = run_bass_kernel_spmd(nc, [arrays], core_ids=[0])
    return r.results[0]["out_dram"].reshape(1, T, D)
```

```python
from contextlib import ExitStack

import numpy as np

import concourse.bass as bass
from concourse import mybir

F32 = mybir.dt.float32
F32R = mybir.dt.float32r
U8 = mybir.dt.uint8
ALU = mybir.AluOpType
ACT = mybir.ActivationFunctionType
AX = mybir.AxisListType

P = 128
T, D = 256, 1024
TT, KC = T // P, D // P
F = 2816
FC = F // P
HD = 64
SLOT = 3 * 1024
RING = 4
NC_CMP, CMP_STRIDE = 15, 16
LEVELS = 7
DECAY = float(np.exp(-0.5))
NEG = -1e30
TOPK = 64

SLOTS = [("w_in", 8), ("cmp_w1", 3), ("w_out", 3), ("ffn0", FC), ("ffn1", FC), ("even_in", 8), ("even_out", 3),
         ("ffn2", FC), ("ffn3", FC), ("odd_in", 5), ("uk_uv", 2), ("odd_out", 3), ("ffn4", FC)]
BASE = {}
NSLOTS = 0
for _name, _n in SLOTS:
    BASE[_name] = NSLOTS
    NSLOTS += _n

CONSTS = [("ident", P), ("neg_half", 2 * 16),
          ("mu", 14), ("w0", 4), ("a0", 4), ("k_k", 4), ("k_a", 4), ("r_k", 4), ("lnx_w", 4), ("lnx_b", 4),
          ("gla_b", 2), ("gla_norm", 1), ("fox_b", 1), ("kv_norm", 2), ("q_scale", 4),
          ("reverse", P), ("pair_ones", P), ("ones", P), ("w2", 512), ("a2", 512), ("g2", 512), ("gate_w", KC * 24),
          ("even_small", KC * 40), ("odd_small", KC * 8), ("gla_gate", 256), ("ck2", 256), ("cv2", 128),
          ("pe_k", 16), ("pe_v", 16), ("t5", 16), ("t5_onehot", 384), ("alibi", 256), ("alibi_cmp", 2 * 16),
          ("any_ok", 2), ("causal", 256)]
COL = {}
NCONST = 0
for _name, _n in CONSTS:
    COL[_name] = (NCONST, _n)
    NCONST += _n

MASKS = 512 + 2 * LEVELS * P

IN_ITEMS = ([("col", 0), ("col", 1)] + [("col", b) for b in range(2, 6)] + [("zw", j) for j in range(4)]
            + [("za", j) for j in range(4)] + [("g", j) for j in range(4)] + [("col", b) for b in range(6, 22)]
            + [("tok", 0), ("tok", 1), ("gate", 0)])
EVEN_ITEMS = ([("small", 0)] + [("col", b) for b in range(4)] + [("gz", 0), ("gz", 1)]
              + [("col", b) for b in range(4, 16)]
              + [("tok", t, n) for n in range(3) for t in range(TT)])
ODD_ITEMS = ([("ki", 0)] + [("ckv", t) for t in range(TT)] + [("small", t) for t in range(TT)]
             + [("qi", j) for j in range(4)] + [("q", j) for j in range(8)])
UKV_ITEMS = [("kh", j) for j in range(8)] + [("vh", t, n) for t in range(TT) for n in range(2)]

FIRST = COL["reverse"][0]
RWKV_UNITS = 16
QUADS = RWKV_UNITS // 4


def build(nc, x_in, wstream, gains, consts_in, masks_in, scratch, out):
    ctx = ExitStack()
    with ctx:
        at = {}

        def sb(name, shape, dt=F32):
            at[name] = nc.sbuf_base
            return ctx.enter_context(nc.sbuf_tensor(name, shape, dt))

        def over(name, shape, under, skip=0):
            return nc.alloc_sbuf_tensor_at(name, shape, F32R, offset=at[under] + 4 * skip)

        names = ("x0_loaded x1_loaded first_loaded consts_loaded masks_loaded masks_ready gain0 gain1 land0 land1 land2 land3 free0 free1 free2 free3 "
                 "a_step v_step g_step ss_ready rstd_ready xn_ready x_done xT_ps uT_a uT_v "
                 "acc0_done gu_ps silu_ready h_mul h_hi h_ready gu_done down_done hi_a hi_b lo_a lo_b hi_blk lo_blk small_hi small_lo uT_hi uT_lo mix_ready op_acc item_ps item_ev "
                 "shift_ready lora_in raw_free kk_sq n2_ps kk_clamped kk_sqrt kk_n2_read rk_ready bon_ps "
                 "bonus_read pads_ready eye_ready csm_ready e_ready scan_in ab_ready tok_ps tok_ev id_ready A_ps A_read "
                 "P_ps P_ev dM_ps M_ready rhs_ps rhs_ev sa_ps sa_ev y_ps s_ps y_ev s_ev var_ready grs_ready yn_ready "
                 "ynT_ps ynT_ev cmp_z cmp_h cmp_row cmp_hT cmp_hact cmp_kv cmp_ready gates_ready gates_ps gate_tok "
                 "S_ps max_ready p_ready pT_ps pT_ev o_ps o_ready oT_ps oT_ev "
                 "gk_in gk_ab gk_min gk_ls gk_cs fox_cs fox_ps fox_tok gla_k gla_ready "
                 "c_ss c_rs c_n c_ps c_ev idx_ps idx_relu idx_acc sel_ready t5_ps t5_sb t5_out t5_in "
                 "stored").split()
        s = {n: ctx.enter_context(nc.semaphore(n)) for n in names}

        x = sb("x", [P, TT, D])
        xn = sb("xn", [P, TT, D])
        uT = sb("uT", [P, KC, T])
        yT = sb("yT", [P, KC, T])
        gb = sb("gb", [P, 2, D])
        ring = sb("ring", [P, RING, SLOT])
        ffb = sb("ffb", [P, 4, T])
        cst = sb("cst", [P, NCONST])
        msk = sb("msk", [P, MASKS], U8)
        small = sb("small", [P, 256])
        WK = 20480
        wk = sb("wk", [P, WK])
        ps = [ctx.enter_context(nc.psum_tensor(f"ps{i}", [P, 512], F32)) for i in range(8)]

        def C(name, lo=0, hi=None):
            o, n = COL[name]
            return cst[:, o + lo:o + (n if hi is None else hi)]

        def W(off, *shape):
            n = int(np.prod(shape))
            a = wk[:, off:off + n]
            if len(shape) == 2:
                a = a.rearrange("p (a b) -> p a b", b=shape[1])
            if len(shape) == 3:
                a = a.rearrange("p (a b c) -> p a b c", b=shape[1], c=shape[2])
            return a

        ident = C("ident")
        w_gu = over("w_gu", [P, 2, 2, 2 * D], "wk")
        w_dn = over("w_dn", [P, 2, 2, D], "wk", 8 * D)
        h_r = over("h_r", [P, 2, 2, T], "ffb")
        ring_r = over("ring_r", [P, RING, SLOT], "ring")
        w_h = {"even": [over(f"even_h{i}", [P, KC, 3 * P], "wk", o) for i, o in enumerate((9728, 17408))],
               "odd": [over(f"odd_h{i}", [P, KC, 3 * P], "wk", o) for i, o in enumerate((4096, 9216))]}
        w_small = [over(f"even_small{i}", [P, KC * 40], "wk", 14336 + KC * 40 * i) for i in range(2)]
        uT_r = [over("uT_h", [P, KC, T], "uT"), over("uT_l", [P, KC, T], "yT")]
        sg = wk[:, 12 * D:12 * D + 2 * T].rearrange("p (a b) -> p a b", a=2)
        ss, rstd = small[:, 0:2], small[:, 2:4]
        den, nmax, rden = small[:, 160:176], small[:, 12:16], small[:, 16:24]

        pr, pk, pv = W(0, 4, T), W(1024, 4, T), W(2048, 4, T)
        gg, kk, kp = W(3072, 4, T), W(4096, 4, T), W(1024, 4, T)
        sgm, agm = xn[:, 0, :].rearrange("p (a b) -> p a b", b=T), xn[:, 1, :].rearrange("p (a b) -> p a b", b=T)
        ytok = W(5120, TT, 512)
        tmp = W(5120, 4, T)
        arT = W(6144, 4, TT, 2 * P)
        bT, kT_ = W(8192, 4, TT * P), W(9216, 4, TT * P)
        AA4 = [W(10240, 4, 512), W(12288, 4, 512), xn[:].rearrange("p t (u n) -> p (t u) n", n=512),
               uT[:].rearrange("p (u c) n -> p u (c n)", u=4)]
        E1, E2, E3, cs = W(10240, 4, T), W(11264, 4, T), W(12288, 4, T), W(13312, 4, T)
        Mm, Mt = W(14336, RWKV_UNITS, P), W(0, RWKV_UNITS, P)
        raw = W(14336, 4, 257)
        Pb = W(16384, 2, 512)
        csp = W(16384, 4, T)
        lora = W(17408, 2, T)
        td = W(17920, T)
        tg = W(18176, T)
        hrow = W(17408, 2, T)
        qT = W(18432, 4, T)
        ksT, kwT = W(19456, 2, T), W(19968, 2, T)
        vtok = yT[:, 0:4, :].rearrange("p (t c) n -> p t (c n)", t=2)
        bktok = yT[:, 4:8, :].rearrange("p (w c) n -> p w (c n)", w=2)
        Sst = ffb[:, 0:2, :].rearrange("p a (c n) -> p (a c) n", c=2)
        RH, SA = ffb[:, 2:4, :].rearrange("p a n -> p (a n)"), Pb[:, 0, :]
        glT = ffb[:, 3, :]

        zk = sb("zk", [P, 3, P])
        zv = sb("zv", [P, 3, P])
        vsw = sb("vsw", [P, TT, 256])
        hid = sb("hid", [P, 2, 2, 48])
        kcT = sb("kcT", [P, 2, 16])
        vc = sb("vc", [16, 2, HD])
        gtok = sb("gtok", [P, TT, 24])
        SS, Pp, PT = W(10240, 3, T), W(11008, 3, T), W(11776, 2, 2 * P)
        obr = W(12288, 512).rearrange("p (h n) -> p h n", h=8)
        onsa = W(0, TT, 512)

        block = ctx.enter_context(nc.Block())

        def mask(i, n=1):
            return msk[:, 512 + i * P:512 + (i + n) * P]

        def att_units(kind):
            units = []
            for t in range(TT):
                K, tk = P * (t + 1), slice(t * P, (t + 1) * P)
                if kind == "nsa":
                    for b in range(3):
                        for h in range(8):
                            g, slope = h // 4, 2.0 ** -(h + 1)
                            u = dict(q=qT[:, h % 4, tk], scale=slope)
                            if b == 0:
                                u.update(k=kcT[:, g, 0:NC_CMP], K=NC_CMP, v=[vc[0:NC_CMP, g, :]],
                                         dist=C("alibi_cmp", 16 * t, 16 * t + NC_CMP))
                            else:
                                kx, o = (ksT, kwT)[b - 1], (b - 1) * P + g * HD
                                u.update(k=kx[:, g, 0:K], K=K, v=[vsw[:, kt, o:o + HD] for kt in range(t + 1)],
                                         dist=C("alibi", P * (1 - t), P * (1 - t) + K))
                            units.append(u)
                if kind == "fox":
                    for h in range(8):
                        units.append(dict(q=fqT[:, h // 2, tk], k=fkT[h // 4][:, h // 2 % 2, h % 2, 0:K], K=K, scale=1.0,
                                          v=[evtok[:, kt, 512 + h * HD:512 + (h + 1) * HD] for kt in range(t + 1)],
                                          head=h, tk=tk, dist=C("causal", P * (1 - t), P * (1 - t) + K)))
                if kind == "dsa":
                    for h in range(16):
                        units.append(dict(q=oqT[:, h // 2, tk], k=khT[h % 2][:, h // 2, 0:K], K=K, scale=1.0,
                                          v=[vh[:, kt, h * HD:(h + 1) * HD] for kt in range(t + 1)],
                                          t5=bias16[:, h, P * (1 - t):P * (1 - t) + K], dist=selm[:, t, 0:K]))
            return units

        gqT, gkT = W(0, 2, T), W(512, 2, T)
        goT = W(1024, 4, T)
        fqT, fkT = W(2048, 4, T), [W(12800, 2, 2, T), W(16384, 2, 2, T)]
        evtok = W(4096, TT, 1024)
        gsm = W(6144, T)
        gz, gab, gmn, gcs = W(6400, 2, T), W(6912, 2, T), W(7424, 2, T), W(7936, 2, T)
        fz, fab, fmn, fneg = W(8448, T), W(8704, T), W(8960, T), W(9216, T)
        fsum = W(9472, T)
        gqd, gkd = W(14336, 2, T), W(14848, 2, T)
        gE1, gE2 = W(15360, 2, T), W(15872, 2, T)
        gkt = W(12288, 2, P)
        gA = W(9728, 4, P)
        gS = W(13824, 2, 256)
        ogla = W(17664, TT, 512)
        gsq = W(18688, 512)
        ofox = W(19200, 1, 1024)[:, 0, :].rearrange("p (t n) -> p t n", t=2)
        oqT = W(0, 8, T)
        khT = [W(2048, 8, T), xn[:].rearrange("p t (c n) -> p (t c) n", n=T)]
        vh = W(4096, TT, 1024)
        odsa = W(6144, TT, 1024)
        qiT = W(8192, 4, T)
        kiT = W(12288, 2, T)
        idxs = W(7168, 2, T)
        wtok = small[:, 208:224].rearrange("p (t h) -> p t h", t=2)
        selm = W(13568, 2, T)
        ckv = W(14080, 2, 256)
        cT = W(14592, 2, T)
        score = W(15104, T)
        bias16 = W(15360, 16, T)
        csc = W(7680, T)

        USED = {"even": [[] for _ in EVEN_ITEMS], "odd": [[] for _ in ODD_ITEMS]}
        for n, it in enumerate(EVEN_ITEMS):
            if it[0] == "col":
                USED["even"][n] = [it[1]]
            if it[0] == "tok" and it[1] == 1:
                USED["even"][n] = [[16, 17], [18, 19, 20], [21, 22, 23]][it[2]]
        for n, it in enumerate(ODD_ITEMS):
            USED["odd"][n] = {"ki": [0], "ckv": [1, 2] if it[1] else [], "qi": [3 + it[1]], "q": [7 + it[1]]}.get(it[0], [])
        BLOCKS = {k: sum(len(b) for b in u) for k, u in USED.items()}
        PB = {"even": 0, "odd": BLOCKS["even"]}

        UN = {k: att_units(k) for k in ("nsa", "fox", "dsa")}
        UB = {"nsa": 0, "fox": len(UN["nsa"]), "dsa": len(UN["nsa"]) + len(UN["fox"])}
        IB, n = {}, 0
        for k, items in (("in", IN_ITEMS), ("even", EVEN_ITEMS), ("odd", ODD_ITEMS), ("ukv", UKV_ITEMS)):
            IB[k] = n
            n += len(items)
        TN = {n: i for i, n in enumerate([0, 1, 3, 4, 5, 6, 7, 8])}
        SPLIT_OF = {n: i for i, n in enumerate([1, 3, 4, 5, 6, 7, 8])}
        PROJ_OF = {4: "even", 7: "odd"}
        FFN_OF = {1: 0, 3: 1, 5: 2, 6: 3, 8: 4}
        LOOPS = (FC - 6) // 4

        @block.sync
        def _(sp):
            for t in range(TT):
                sp.dma_start(x[:, t, :], x_in[t * P:(t + 1) * P, :]).then_inc(s[f"x{t}_loaded"], 16)
            for i in range(RING):
                if i == 1:
                    sp.wait_ge(s["consts_loaded"], 16)
                sp.dma_start(ring[:, i, :], wstream[i]).then_inc(s[f"land{i}"], 16)
            NS = NSLOTS
            rounds = (NS - RING) // RING
            with sp.Fori(0, rounds) as r:
                for j in range(RING):
                    sp.wait_ge(s[f"free{j}"], r + 1)
                    sp.dma_start(ring[:, j, :],
                                 wstream[bass.ds(r * RING + (RING + j), 1)].rearrange("a p n -> p (a n)")
                                 ).then_inc(s[f"land{j}"], 16)
            for i in range(RING * (rounds + 1), NS):
                sp.wait_ge(s[f"free{i % RING}"], i // RING)
                sp.dma_start(ring[:, i % RING, :], wstream[i]).then_inc(s[f"land{i % RING}"], 16)
            for t in range(TT):
                sp.wait_ge(s["xn_ready"], 2 * 9 + t + 1)
                sp.dma_start(out[t * P:(t + 1) * P, :], x[:, t, :]).then_inc(s["stored"], 16)
            sp.wait_ge(s["stored"], 16 * TT)

        def slot(i):
            return ring[:, i % RING, :]

        @block.tensor
        def _(pe):
            def land(i):
                pe.wait_ge(s[f"land{i % RING}"], 16 * (i // RING + 1))

            def mm(o, l, r, start=True, stop=True):
                return pe.matmul(o, l, r, start=start, stop=stop, skip_group_check=True)

            def norm_T(n):
                k = TN[n]
                for t in range(TT):
                    pe.wait_ge(s["xn_ready"], 2 * n + t + 1)
                    for half in range(2):
                        for c in range(4):
                            last = pe.transpose(ps[4 + 2 * t + half][:, c * P:(c + 1) * P],
                                                xn[:, t, (4 * half + c) * P:(4 * half + c + 1) * P], ident)
                        last.then_inc(s["xT_ps"], 1)
                if n:
                    pe.wait_ge(s["uT_lo"], 4 * (SPLIT_OF[n] + 1))
                else:
                    pe.wait_ge(s["uT_a"], 2)
                    pe.wait_ge(s["uT_v"], 2)

            PASSES = [(0, 0), (1, 0), (0, 1)]

            def gate_up(j):
                for m in range(2):
                    for k in range(KC):
                        for n, (a, b) in enumerate(PASSES):
                            w = w_gu[:, j % 2, a, (m * KC + k) * P:(m * KC + k + 1) * P]
                            last = mm(ps[4 + j % 2][:, m * T:(m + 1) * T], w, uT_r[b][:, k, :],
                                      k == 0 and n == 0, k == KC - 1 and n == 2)
                last.then_inc(s["gu_ps"], 1)

            def down(j, start, stop):
                for t in range(TT):
                    for half in range(2):
                        for n, (a, b) in enumerate(PASSES):
                            last = mm(ps[2 * t + half][:, :], h_r[:, j % 2, a, t * P:(t + 1) * P],
                                      w_dn[:, j % 2, b, half * 512:(half + 1) * 512],
                                      start and n == 0, stop and n == 2)
                    if stop and t == 0:
                        last.then_inc(s["acc0_done"], 1)
                last.then_inc(s["down_done"], 1)

            def ffn(f):
                q = FC * f

                def step(c, r=0):
                    pe.wait_ge(s["lo_a"], r + (q + c + 1))
                    if q + c >= 2:
                        pe.wait_ge(s["h_ready"], r + (q + c - 1))
                    gate_up(c)
                    if c:
                        pe.wait_ge(s["lo_b"], r + (q + c))
                        pe.wait_ge(s["h_ready"], r + (q + c))
                        down(c - 1, c == 1, False)
                step(0)
                step(1)
                with pe.Fori(0, 4 * LOOPS, 4) as r:
                    for j in range(4):
                        step(2 + j, r)
                for c in range(2 + 4 * LOOPS, FC):
                    step(c)
                pe.wait_ge(s["lo_b"], q + FC)
                pe.wait_ge(s["h_ready"], q + FC)
                down(FC - 1, False, True)

            def out_proj(o, b):
                pe.wait_ge(s["mix_ready"], o + 1)
                for i in range(3):
                    land(b + i)
                    for c in range(3 * i, min(3 * i + 3, KC)):
                        w = slot(b + i)[:, (c % 3) * D:(c % 3 + 1) * D]
                        for t in range(TT):
                            for half in range(2):
                                last = mm(ps[2 * t + half][:, :], yT[:, c, t * P:(t + 1) * P],
                                          w[:, half * 512:(half + 1) * 512], c == 0, c == KC - 1)
                            if c == KC - 1 and t == 0:
                                last.then_inc(s["op_acc"], 1)
                    last.then_inc(s[f"free{(b + i) % RING}"], 1)
                pe.wait_ge(s[f"free{(b + 2) % RING}"], (b + 2) // RING + 1)
                pe.sem_inc(s["op_acc"], 1)

            def item(q):
                if q >= 4:
                    pe.wait_ge(s["item_ev"], q - 3)
                return ps[4 + q % 4]

            def col_block(bank, b, blk):
                i = b + blk // 3
                if blk % 3 == 0:
                    land(i)
                w = slot(i).rearrange("p (k f) -> p k f", k=KC)
                for k in range(KC):
                    last = mm(bank[:, 0:T], w[:, k, (blk % 3) * P:(blk % 3 + 1) * P], uT[:, k, :], k == 0, k == KC - 1)
                return last

            def tok_block(bank, i, t, lo, hi):
                w = slot(i).rearrange("p (k f) -> p k f", k=KC)
                for k in range(KC):
                    last = mm(bank[:, 0:hi - lo], uT[:, k, t * P:(t + 1) * P], w[:, k, lo:hi], k == 0, k == KC - 1)
                return last

            def parts(kind, blk):
                pe.wait_ge(s["lo_blk"], PB[kind] + blk + 1)
                i = (BASE[kind + "_in"] + blk // 3) % RING
                return w_h[kind][blk // 3 % 2], ring_r[:, i, :].rearrange("p (k f) -> p k f", k=KC)

            def col_split(kind, bank, blk):
                w, f = parts(kind, blk), blk % 3 * P
                for k in range(KC):
                    for n, (a, b) in enumerate(PASSES):
                        last = mm(bank[:, 0:T], w[a][:, k, f:f + P], uT_r[b][:, k, :],
                                  k == 0 and n == 0, k == KC - 1 and n == 2)
                return last

            def tok_split(kind, bank, blk, t, lo, hi):
                w = parts(kind, blk)
                for k in range(KC):
                    for n, (a, b) in enumerate(PASSES):
                        last = mm(bank[:, 0:hi - lo], uT_r[b][:, k, t * P:(t + 1) * P], w[a][:, k, lo:hi],
                                  k == 0 and n == 0, k == KC - 1 and n == 2)
                return last

            def small_item(o, l, r, n=2):
                for k in range(KC):
                    for part in range(2):
                        last = mm(o, l(k, part), r(k, part), k == 0 and not part, k == KC - 1 and part == 1)
                return last

            def freed(n, i):
                pe.wait_ge(s["item_ps"], n)
                pe.sem_inc(s[f"free{i % RING}"], 1)

            def w_in():
                b = BASE["w_in"]
                for n, it in enumerate(IN_ITEMS):
                    q = IB["in"] + n
                    bank = item(q)
                    if it[0] == "col":
                        last = col_block(bank, b, it[1])
                    elif it[0] in ("zw", "za", "g"):
                        if it == ("zw", 0):
                            pe.wait_ge(s["lora_in"], 3)
                        src = {"zw": "w2", "za": "a2", "g": "g2"}[it[0]]
                        last = mm(bank[:, 0:T], C(src, it[1] * P, (it[1] + 1) * P), tg if it[0] == "g" else td)
                    elif it[0] == "tok":
                        last = tok_block(bank, b + 7, it[1], P, 3 * P)
                    else:
                        w = C("gate_w").rearrange("p (k n) -> p k n", k=KC)
                        for k in range(KC):
                            last = mm(bank[0:24, 0:T], w[:, k, :], uT[:, k, :], k == 0, k == KC - 1)
                    last.then_inc(s["item_ps"], 1)
                    if (it[0] == "col" and it[1] % 3 == 2) or it == ("tok", 1):
                        freed(q + 1, b + 7 if it[0] == "tok" else b + it[1] // 3)
                    if it == ("g", 3):
                        pe.wait_ge(s["kk_sq"], 1)
                        for c in range(4):
                            last = mm(ps[c // 2][:, (c % 2) * T:(c % 2 + 1) * T], C("pair_ones"), tmp[:, c, :])
                        last.then_inc(s["n2_ps"], 1)
                    if it == ("col", 14):
                        pe.wait_ge(s["rk_ready"], 1)
                        for c in range(4):
                            last = mm(ps[2 + c // 2][:, (c % 2) * T:(c % 2 + 1) * T], C("pair_ones"), tmp[:, c, :])
                        last.then_inc(s["bon_ps"], 1)

            def rwkv_tok():
                pe.wait_ge(s["shift_ready"], 14)
                pe.wait_ge(s["item_ev"], IB["in"] + len(IN_ITEMS))
                srcs = [(pv, t) for t in range(TT)] + [(bT, 0), (kT_, 0)]
                for n, (src, t) in enumerate(srcs):
                    if n == 2:
                        pe.wait_ge(s["ab_ready"], 1)
                    for c in range(4):
                        last = pe.transpose(ps[(0, 1, 6, 7)[n]][:, c * P:(c + 1) * P], src[:, c, t * P:(t + 1) * P],
                                            ident)
                    last.then_inc(s["tok_ps"], 1)

            def rwkv():
                pe.wait_ge(s["bonus_read"], 1)
                pe.wait_ge(s["tok_ev"], 4)
                pe.wait_ge(s["cmp_row"], 2)
                for u in range(RWKV_UNITS):
                    t, c, r, k = u // 8, u % 8 // 2, HD * (u % 2), u // 4
                    if u >= 4:
                        pe.wait_ge(s["A_read"], u - 3)
                    if u % 4 == 0 and k >= 2:
                        pe.wait_ge(s["M_ready"], k - 1)
                    bank = ps[u % 4]
                    ar = arT[r:r + HD, c, t, :]
                    tk = slice(t * P, (t + 1) * P)
                    mm(ps[4 + 2 * (k % 2) + u % 2][:, (u % 4) // 2 * P:((u % 4) // 2 + 1) * P],
                       arT[r:r + HD, c, t, 0:P], bT[r:r + HD, c, tk])
                    mm(bank[:, 0:256], bT[r:r + HD, c, tk], ar)
                    mm(bank[:, 256:512], kT_[r:r + HD, c, tk], ar).then_inc(s["A_ps"], 1)
                pe.wait_ge(s["A_read"], RWKV_UNITS)
                n = (LEVELS - 1) * QUADS
                for q in range(n + 1):
                    if q == 2:
                        compress_T()
                    if q == 8:
                        compress_out()
                    if q < n:
                        k = q % QUADS
                        pe.wait_ge(s["M_ready"], q + 1)
                        for j in range(4):
                            last = mm(ps[q % 2][:, j * P:(j + 1) * P], AA4[k][:, j, 0:P], Mm[:, 4 * k + j, :])
                        last.then_inc(s["P_ps"], 1)
                    if q:
                        p = q - 1
                        k = p % QUADS
                        pe.wait_ge(s["P_ev"], p + 1)
                        pe.wait_ge(s["M_ready"], max(p + 3, QUADS))
                        for j in range(4):
                            pu = Pb[:, p % 2, j * P:(j + 1) * P]
                            last = mm(ps[4 + p % 2][:, j * P:(j + 1) * P], pu, Mt[:, 4 * k + j, :])
                            if p // QUADS < LEVELS - 2:
                                last = mm(ps[2 + p % 2][:, j * P:(j + 1) * P], Mt[:, 4 * k + j, :], pu)
                        last.then_inc(s["dM_ps"], 1)
                pe.wait_ge(s["M_ready"], LEVELS * QUADS)
                pe.wait_ge(s["gate_tok"], 2)
                for t in range(TT):
                    if t:
                        pe.wait_ge(s["s_ev"], 1)
                        pe.wait_ge(s["y_ev"], 1)
                    for c in range(4):
                        o = ps[6][:, c * P:(c + 1) * P]
                        if t:
                            mm(o, arT[:, c, 1, 0:P], Sst[:, c, :], True, False)
                        for h in (2 * c, 2 * c + 1):
                            last = mm(o[:, h % 2 * HD:(h % 2 + 1) * HD], AA4[2 * t + h // 4][:, h % 4, 256:384],
                                      vtok[:, t, h * HD:(h + 1) * HD], not t, True)
                    last.then_inc(s["rhs_ps"], 1)
                    pe.wait_ge(s["rhs_ev"], t + 1)
                    for h in range(8):
                        last = mm(ps[7][:, h * HD:(h + 1) * HD], Mt[:, 8 * t + h, :], RH[:, h * HD:(h + 1) * HD])
                    last.then_inc(s["sa_ps"], 1)
                    pe.wait_ge(s["sa_ev"], t + 1)
                    if not t:
                        for c in range(4):
                            o = ps[4][:, c * P:(c + 1) * P]
                            mm(o, bktok[:, 0, c * P:(c + 1) * P], SA[:, c * P:(c + 1) * P], True, False)
                            last = mm(o, bktok[:, 1, c * P:(c + 1) * P], vtok[:, 0, c * P:(c + 1) * P], False, True)
                        last.then_inc(s["s_ps"], 1)
                    for c in range(4):
                        o = ps[5][:, c * P:(c + 1) * P]
                        if t:
                            mm(o, arT[:, c, 1, P:2 * P], Sst[:, c, :], True, False)
                        for h in (2 * c, 2 * c + 1):
                            A, oh, hs = AA4[2 * t + h // 4], o[:, h % 2 * HD:(h % 2 + 1) * HD], slice(h * HD, (h + 1) * HD)
                            mm(oh, A[:, h % 4, 128:256], SA[:, hs], not t, False)
                            last = mm(oh, A[:, h % 4, 384:512], vtok[:, t, hs], False, True)
                    last.then_inc(s["y_ps"], 1)
                pe.wait_ge(s["y_ev"], 2)

            def rwkv_T(t):
                pe.wait_ge(s["yn_ready"], t + 1)
                if t:
                    pe.wait_ge(s["ynT_ev"], 1)
                for c in range(4):
                    last = pe.transpose(ps[7][:, c * P:(c + 1) * P], ytok[:, t, c * P:(c + 1) * P], ident)
                last.then_inc(s["ynT_ps"], 1)

            def tok_T(src, n0, chunks=4):
                for t in range(TT):
                    pe.wait_ge(s["yn_ready"], n0 + t + 1)
                    for c in range(chunks):
                        last = pe.transpose(ps[t][:, c * P:(c + 1) * P], src[:, t, c * P:(c + 1) * P], ident)
                    last.then_inc(s["ynT_ps"], 1)

            def compress():
                b = BASE["cmp_w1"]
                pe.wait_ge(s["cmp_z"], 2)
                pe.wait_ge(s["item_ev"], IB["in"] + len(IN_ITEMS))
                for n in range(2):
                    for m in range(16):
                        piece = 16 * n + m
                        i = b + piece // 12
                        if m == 0 or piece % 12 == 0:
                            land(i)
                        last = mm(ps[4 + n][0:47, 0:256], (zk, zv)[n][:].rearrange("p a n -> p (a n)")[:, m:m + 8 * 46 + 1:8],
                                  slot(i)[:, (piece % 12) * 256:(piece % 12 + 1) * 256], m == 0, m == 15)
                    last.then_inc(s["cmp_h"], 1)
                pe.wait_ge(s["cmp_h"], 2)
                for i in range(3):
                    pe.sem_inc(s[f"free{(b + i) % RING}"], 1)

            def compress_T():
                for n in range(2):
                    for half in range(2):
                        last = pe.transpose(ps[6 + n][:, half * 48:half * 48 + 47],
                                            hrow[0:47, n, half * P:(half + 1) * P], ident[0:47, 0:47])
                last.then_inc(s["cmp_hT"], 1)

            def compress_out():
                pe.wait_ge(s["cmp_hact"], 1)
                for half in range(2):
                    mm(ps[6][:, 0:30], C("ck2", half * P, (half + 1) * P), hid[:, 0, half, 0:30], half == 0, half == 1)
                for g in range(2):
                    for half in range(2):
                        last = mm(ps[6][0:NC_CMP, 64 + g * HD:64 + (g + 1) * HD],
                                  hid[:, 1, half, 15 * g:15 * g + 15], C("cv2", half * HD, (half + 1) * HD),
                                  half == 0, half == 1)
                last.then_inc(s["cmp_kv"], 1)
                pe.wait_ge(s["gates_ready"], 1)
                for t in range(TT):
                    last = pe.transpose(ps[7][:, t * 24:(t + 1) * 24], glT[0:24, t * P:(t + 1) * P], ident[0:24, 0:24])
                last.then_inc(s["gates_ps"], 1)

            def attention(kind, go, value, beside={}):
                units, b = UN[kind], UB[kind]
                n = len(units)
                if kind == "dsa":
                    pe.wait_ge(s["t5_in"], 16)
                pe.wait_ge(s[go], value)
                for i in range(n + 3):
                    if i in beside:
                        beside[i]()
                    if i < n:
                        u, a = b + i, units[i]
                        if u >= 3:
                            pe.wait_ge(s["max_ready"], u - 2)
                        o = ps[u % 3][:, 0:a["K"]]
                        if "head" in a:
                            h = a["head"]
                            mm(o, ident[0:8, h:h + 1].to_broadcast([8, P]), fneg[0:8, 0:a["K"]], True, False)
                            mm(o, fsum[0:8, a["tk"]], ident[0:8, h:h + 1].to_broadcast([8, a["K"]]), False, False)
                        if "t5" in a:
                            mm(o, C("reverse"), a["t5"], True, False)
                        mm(o, a["q"], a["k"], kind == "nsa", True).then_inc(s["S_ps"], 1)
                    if 2 <= i < n + 2:
                        u, a = b + i - 2, units[i - 2]
                        pe.wait_ge(s["p_ready"], u + 1)
                        if u >= 2:
                            pe.wait_ge(s["pT_ev"], u - 1)
                        for k in range(0, a["K"], P):
                            w = min(P, a["K"] - k)
                            last = pe.transpose(ps[3 + u % 2][0:w, k:k + P], Pp[:, u % 3, k:k + w], ident)
                        last.then_inc(s["pT_ps"], 1)
                    if i >= 3:
                        u, a = b + i - 3, units[i - 3]
                        pe.wait_ge(s["pT_ev"], u + 1)
                        if u % 8 == 0 and u >= 16:
                            pe.wait_ge(s["o_ready"], u // 8 - 1)
                        for k in range(0, a["K"], P):
                            w = min(P, a["K"] - k)
                            last = mm(ps[5 + u // 8 % 2][:, u % 8 * HD:(u % 8 + 1) * HD], PT[0:w, u % 2, k:k + P], a["v"][k // P],
                                      k == 0, k + P >= a["K"])
                        last.then_inc(s["o_ps"], 1)

            def even_in():
                b = BASE["even_in"]
                for n, it in enumerate(EVEN_ITEMS):
                    q = IB["even"] + n
                    bank = item(q)
                    if it[0] == "small":
                        pe.wait_ge(s["small_lo"], 1)
                        for k in range(KC):
                            for m, (a, b_) in enumerate(PASSES):
                                last = mm(bank[0:40, 0:T], w_small[a][:, 40 * k:40 * k + 40], uT_r[b_][:, k, :],
                                          k == 0 and m == 0, k == KC - 1 and m == 2)
                    elif it[0] == "gz":
                        if it[1] == 0:
                            pe.wait_ge(s["item_ev"], IB["even"] + 1)
                        last = mm(bank[:, 0:T], C("gla_gate", it[1] * P, (it[1] + 1) * P)[0:16, :], gsm[0:16, :])
                    elif it[0] == "col":
                        last = col_split("even", bank, it[1])
                    else:
                        _, t, w = it
                        last = tok_split("even", bank, 17 + 3 * w, t, 0 if w else P, 3 * P)
                    last.then_inc(s["item_ps"], 1)
                    if (it[0] == "col" and it[1] % 3 == 2) or (it[0] == "tok" and it[1] == 1):
                        freed(q + 1, b + 5 + it[2] if it[0] == "tok" else b + it[1] // 3)

            def gla():
                pe.wait_ge(s["gla_k"], 1)
                pe.wait_ge(s["item_ev"], IB["even"] + len(EVEN_ITEMS))
                for c in range(2):
                    last = pe.transpose(ps[2][:, c * P:(c + 1) * P], gkd[:, c, 0:P], ident)
                last.then_inc(s["tok_ps"], 1)
                for t in range(TT):
                    tk = slice(t * P, (t + 1) * P)
                    if t:
                        pe.wait_ge(s["A_read"], RWKV_UNITS + 1)
                    for h in range(4):
                        c, r = h // 2, HD * (h % 2)
                        last = mm(ps[4 + h % 2][:, c * P:(c + 1) * P], gkd[r:r + HD, c, tk], gqd[r:r + HD, c, tk])
                    last.then_inc(s["A_ps"], 1)
                    pe.wait_ge(s["A_read"], RWKV_UNITS + t + 1)
                    if t:
                        pe.wait_ge(s["s_ev"], 2)
                        pe.wait_ge(s["y_ev"], 3)
                    for h in range(4):
                        o = ps[1][:, h * P:(h + 1) * P]
                        if t:
                            r = HD * (h % 2)
                            mm(o, gqd[:, h // 2, tk], gS[:, h // 2, (h % 2) * P:(h % 2 + 1) * P], True, False)
                        last = mm(o, gA[:, h, :], evtok[:, t, h * P:(h + 1) * P], not t, True)
                    last.then_inc(s["y_ps"], 1)
                    if not t:
                        pe.wait_ge(s["tok_ev"], 5)
                        for c in range(2):
                            last = mm(ps[6][:, c * 256:(c + 1) * 256], gkt[:, c, :],
                                      evtok[:, 0, c * 256:(c + 1) * 256])
                        last.then_inc(s["s_ps"], 1)

            def odd_in():
                b = BASE["odd_in"]
                for n, it in enumerate(ODD_ITEMS):
                    q = IB["odd"] + n
                    bank = item(q)
                    if it[0] == "ki":
                        last = col_split("odd", bank, 0)
                    elif it[0] in ("qi", "q"):
                        blk = it[1] + (4 if it[0] == "q" else 0)
                        last = col_split("odd", bank, 3 + blk)
                    elif it[0] == "ckv":
                        last = tok_split("odd", bank, 2, it[1], P, 3 * P)
                    else:
                        w = C("odd_small").rearrange("p (k n) -> p k n", k=KC)
                        last = small_item(
                            bank[:, 0:8],
                            lambda k, part: uT_r[part][:, k, it[1] * P:(it[1] + 1) * P].bitcast(F32),
                            lambda k, part: w[:, k, :])
                    last.then_inc(s["item_ps"], 1)
                    if it == ("ckv", 1):
                        freed(q + 1, b)
                    if it[0] in ("qi", "q") and blk % 3 == 2:
                        freed(q + 1, b + 1 + blk // 3)
                    if it == ("qi", 3):
                        pe.wait_ge(s["c_n"], 1)
                        for c in range(2):
                            for t in range(TT):
                                last = pe.transpose(ps[3][:, c * T + t * P:c * T + (t + 1) * P],
                                                    ckv[:, t, c * P:(c + 1) * P], ident)
                        last.then_inc(s["c_ps"], 1)
                    if it[0] == "q":
                        for m in (2 * it[1], 2 * it[1] + 1):
                            t, h = m // 8, m % 8
                            if m >= 2:
                                pe.wait_ge(s["idx_relu"], m - 1)
                            if m == 0:
                                pe.wait_ge(s["item_ev"], q)
                            mm(ps[m % 2][:, 0:P * (t + 1)], qiT[:, h // 2, t * P:(t + 1) * P],
                               kiT[:, h % 2, 0:P * (t + 1)]).then_inc(s["idx_ps"], 1)
                pe.wait_ge(s["c_ev"], 1)
                b = BASE["uk_uv"]
                for n, it in enumerate(UKV_ITEMS):
                    q = IB["ukv"] + n
                    bank = item(q)
                    if it[0] == "kh":
                        if it[1] == 0:
                            land(b)
                        w = slot(b).rearrange("p (c n) -> p c n", c=3)
                        for c in range(2):
                            last = mm(bank[:, 0:T], w[:, c, it[1] * P:(it[1] + 1) * P], cT[:, c, :], c == 0, c == 1)
                    else:
                        _, t, half = it
                        if t == 0 and half == 0:
                            land(b + 1)
                        w = slot(b + 1).rearrange("p (c n) -> p c n", c=3)
                        for c in range(2):
                            last = mm(bank[:, :], cT[:, c, t * P:(t + 1) * P], w[:, c, half * 512:(half + 1) * 512],
                                      c == 0, c == 1)
                    last.then_inc(s["item_ps"], 1)
                    if it == ("kh", 7) or it == ("vh", 1, 1):
                        freed(q + 1, b if it[0] == "kh" else b + 1)

            def odd_oT():
                for t in range(TT):
                    pe.wait_ge(s["o_ready"], UB["dsa"] // 8 + 2 * (t + 1))
                    for half in range(2):
                        for c in range(4):
                            last = pe.transpose(ps[4 * t * 0 + 2 * t + half][:, c * P:(c + 1) * P],
                                                odsa[:, t, (4 * half + c) * P:(4 * half + c + 1) * P], ident)
                        last.then_inc(s["oT_ps"], 1)

            pe.wait_ge(s["first_loaded"], 16)
            norm_T(0)
            pe.wait_ge(s["consts_loaded"], 16)
            w_in()
            compress()
            rwkv_tok()
            rwkv()
            attention("nsa", "cmp_ready", 2, {6: lambda: rwkv_T(0), 18: lambda: rwkv_T(1)})
            for t in range(TT):
                pe.wait_ge(s["o_ready"], 3 * (t + 1))
                for c in range(4):
                    last = pe.transpose(ps[2 + t][:, c * P:(c + 1) * P], onsa[:, t, c * P:(c + 1) * P], ident)
                last.then_inc(s["oT_ps"], 1)
            out_proj(0, BASE["w_out"])
            norm_T(1)
            ffn(0)
            norm_T(3)
            ffn(1)
            norm_T(4)
            mm(ps[7][0:16, 0:384], C("t5")[0:32, :], C("t5_onehot")[0:32, :]).then_inc(s["t5_ps"], 1)
            pe.wait_ge(s["t5_sb"], 1)
            even_in()
            gla()
            tok_T(ogla, 2)
            attention("fox", "gla_ready", 2)
            for t in range(TT):
                pe.wait_ge(s["o_ready"], UB["fox"] // 8 + t + 1)
                for c in range(4):
                    last = pe.transpose(ps[2 + t][:, c * P:(c + 1) * P], ofox[:, t, c * P:(c + 1) * P], ident)
                last.then_inc(s["oT_ps"], 1)
            out_proj(1, BASE["even_out"])
            norm_T(5)
            ffn(2)
            norm_T(6)
            ffn(3)
            norm_T(7)
            odd_in()
            attention("dsa", "item_ev", IB["ukv"] + len(UKV_ITEMS))
            odd_oT()
            out_proj(2, BASE["odd_out"])
            norm_T(8)
            ffn(4)

        @block.scalar
        def _(act):
            cnt = {}
            ready = dict.fromkeys(names, 0)

            def A(ins, name="a_step", n=1):
                cnt[name] = cnt.get(name, 0) + n
                ins.then_inc(s[name], n)
                act.wait_ge(s[name], cnt[name])

            def gain(n):
                if n >= 2:
                    act.wait_ge(s["xn_ready"], 2 * (n - 1))
                act.dma_start(gb[:, n % 2, :], gains[:, n * D:(n + 1) * D]).then_inc(s[f"gain{n % 2}"], 16)

            def norm(n):
                for t in range(TT):
                    if n:
                        act.wait_ge(s["x_done"], 2 * (n - 1) + t + 1)
                    else:
                        act.wait_ge(s[f"x{t}_loaded"], 16)
                    A(act.activation(xn[:, t, :], x[:, t, :], ACT.Square, accum_out=ss[:, t:t + 1]), "ss_ready")
                if 1 <= n <= 8:
                    gain(n + 1)
                if n == 0:
                    for t in range(TT):
                        act.wait_ge(s["xT_ps"], 2 * t + 1)
                        A(act.copy(uT[:, 0:4, t * P:(t + 1) * P],
                                   ps[4 + 2 * t][:, :].rearrange("p (c n) -> p c n", c=4)), "uT_a")
                if n in SPLIT_OF:
                    k = TN[n]
                    if n in FFN_OF:
                        hi_a(FFN_OF[n], 0)
                    else:
                        hi_block(PROJ_OF[n], 0)
                    for i in range(4):
                        act.wait_ge(s["xT_ps"], 4 * k + i + 1)
                        c0, t = 4 * (i % 2), i // 2
                        act.copy(uT_r[0][:, c0:c0 + 4, t * P:(t + 1) * P],
                                 ps[4 + i][:, :].rearrange("p (c n) -> p c n", c=4)).then_inc(s["uT_hi"], 1)
                if n == 4:
                    act.copy(w_small[0][:, :], C("even_small")).then_inc(s["small_hi"], 1)
                if n in PROJ_OF:
                    for blk in range(1, 6):
                        hi_block(PROJ_OF[n], blk)

            def hi_block(kind, blk):
                i = BASE[kind + "_in"] + blk // 3
                act.wait_ge(s[f"land{i % RING}"], 16 * (i // RING + 1))
                f = blk % 3 * P
                act.copy(w_h[kind][blk // 3 % 2][:, :, f:f + P],
                         slot(i).rearrange("p (k f) -> p k f", k=KC)[:, :, f:f + P]).then_inc(s["hi_blk"], 1)

            def hi_after(kind, n):
                for blk in USED[kind][n]:
                    if blk + 6 < BLOCKS[kind]:
                        hi_block(kind, blk + 6)

            def hi_a(f, c, r=0, rr=0):
                q, i = FC * f, BASE[f"ffn{f}"] + c
                act.wait_ge(s[f"land{i % RING}"], rr + 16 * (i // RING + 1))
                if q + c >= 2:
                    act.wait_ge(s["gu_ps"], r + (q + c - 1))
                act.copy(w_gu[:, c % 2, 0, :], slot(i)[:, 0:2 * D]).then_inc(s["hi_a"], 1)

            def hi_b(f, c, r=0):
                q, i = FC * f, BASE[f"ffn{f}"] + c
                if q + c >= 2:
                    act.wait_ge(s["down_done"], r + (q + c - 1))
                act.copy(w_dn[:, c % 2, 0, :], slot(i)[:, 2 * D:3 * D]).then_inc(s["hi_b"], 1)

            def ffn(f):
                q = FC * f

                def step(c, r=0, rr=0):
                    act.wait_ge(s["gu_ps"], r + (q + c + 1))
                    if q + c >= 2:
                        act.wait_ge(s["h_ready"], r + (q + c - 1))
                    act.activation(sg[:, c % 2, :], ps[4 + c % 2][:, 0:T], ACT.Silu).then_inc(s["silu_ready"], 1)
                    if c + 2 < FC:
                        hi_a(f, c + 2, r, rr)
                    if c + 1 < FC:
                        hi_b(f, c + 1, r)
                hi_b(f, 0)
                hi_a(f, 1)
                step(0)
                step(1)
                with act.Fori(0, 4 * LOOPS, 4) as r:
                    for j in range(4):
                        step(2 + j, r, r * 4)
                for c in range(2 + 4 * LOOPS, FC):
                    step(c)

            def w_in():
                for n, it in enumerate(IN_ITEMS):
                    q = IB["in"] + n
                    act.wait_ge(s["item_ps"], q + 1)
                    bank = ps[4 + q % 4][:, 0:T]
                    name, j = it
                    if name == "col" and j < 14:
                        if j >= 4:
                            act.wait_ge(s["raw_free"], j - 3)
                        A(act.copy(raw[:, j % 4, 1:257], bank), "item_ev")
                        if j == 1:
                            act.wait_ge(s["shift_ready"], 2)
                            A(act.activation(td[0:64, :], lora[0:64, 0, :], ACT.Tanh), "lora_in")
                            A(act.copy(td[64:128, :], lora[64:128, 0, :]), "lora_in")
                            A(act.activation(tg, lora[:, 1, :], ACT.Sigmoid), "lora_in")
                    elif name == "zw":
                        A(act.activation(sgm[:, j, :], bank, ACT.Sigmoid, bias=C("w0", j, j + 1)), "item_ev")
                    elif name == "za":
                        A(act.activation(agm[:, j, :], bank, ACT.Sigmoid, bias=C("a0", j, j + 1)), "item_ev")
                    elif name == "g":
                        A(act.copy(gg[:, j, :], bank), "item_ev")
                    elif name == "col" and j < 18:
                        A(act.mul(qT[:, j - 14, :], bank, C("q_scale", j - 14, j - 13)), "item_ev")
                    elif name == "col" and j in (18, 19):
                        z = (zk, zv)[j - 18]
                        for g in range(2):
                            for par in range(2):
                                ins = act.copy(z[par * HD:(par + 1) * HD, g, :], bank[g * HD:(g + 1) * HD, par:T:2])
                                A(ins, "item_ev" if (g, par) == (1, 1) else "a_step")
                        act.copy(z[:, 2, 0:16], C(("pe_k", "pe_v")[j - 18])).then_inc(s["cmp_z"], 1)
                    elif name == "col" and j in (20, 21):
                        for g in range(2):
                            r = slice(g * HD, (g + 1) * HD)
                            A(act.copy((ksT, kwT)[j - 20][r, g, :], bank[r, :]), "item_ev" if g else "a_step")
                    elif name == "tok":
                        A(act.copy(vsw[:, j, :], bank), "item_ev")
                    else:
                        A(act.copy(glT[0:24, :], bank[0:24, :]), "item_ev")
                    if it == ("col", 7):
                        act.wait_ge(s["kk_clamped"], 1)
                        A(act.activation(tmp, tmp, ACT.Sqrt), "kk_sqrt")
                    if it == ("col", 14):
                        decays()
                        act.wait_ge(s["pads_ready"], 3)
                A(act.activation(glT[0:24, :], glT[0:24, :], ACT.Sigmoid), "gates_ready")

            def decays():
                act.wait_ge(s["csm_ready"], 1)
                for c in range(4):
                    for t in range(TT):
                        tk = slice(t * P, (t + 1) * P)
                        i = 2 * c + t
                        for o, src, sc, b0 in ((E1, cs, -DECAY, 32), (E2, cs, DECAY, 40), (E3, csp, -DECAY, 32)):
                            act.activation(o[:, c, tk], src[:, c, tk], ACT.Exp, scale=sc,
                                           bias=small[:, b0 + i:b0 + i + 1]).then_inc(s["e_ready"], 1)
                act.activation(small[:, 48:52], small[:, 52:56], ACT.Exp, scale=-DECAY).then_inc(s["e_ready"], 1)

            def rwkv():
                dsts = [vtok[:, 0, :], vtok[:, 1, :], bktok[:, 0, :], bktok[:, 1, :]]
                for n in range(2):
                    act.wait_ge(s["tok_ps"], n + 1)
                    A(act.copy(dsts[n], ps[n][:, :]), "tok_ev")
                act.wait_ge(s["ab_ready"], 1)
                for k in range(QUADS):
                    for M in (Mt, Mm):
                        A(act.copy(M[:, 4 * k:4 * k + 4, :], ident.unsqueeze(1).to_broadcast([P, 4, P])), "eye_ready")
                    if k < 2:
                        act.wait_ge(s["tok_ps"], 3 + k)
                        A(act.copy(dsts[2 + k], ps[6 + k][:, :]), "tok_ev")
                for q in range((LEVELS - 1) * QUADS):
                    act.wait_ge(s["P_ps"], q + 1)
                    A(act.copy(Pb[:, q % 2, :], ps[q % 2][:, :]), "P_ev")
                    if q == 4:
                        compress_act()
                    if q == 10:
                        compress_out()
                for t in range(TT):
                    act.wait_ge(s["rhs_ps"], t + 1)
                    A(act.copy(RH, ps[6][:, :]), "rhs_ev")
                    act.wait_ge(s["sa_ps"], t + 1)
                    A(act.copy(SA, ps[7][:, :]), "sa_ev")
                    act.wait_ge(s["y_ps"], t + 1)
                    A(act.copy(ytok[:, t, :], ps[5][:, :]), "y_ev")

            def compress():
                for n in range(2):
                    act.wait_ge(s["cmp_h"], n + 1)
                    A(act.copy(hrow[0:47, n, :], ps[4 + n][0:47, 0:T]), "cmp_row")

            def compress_act():
                act.wait_ge(s["cmp_hT"], 1)
                for n in range(2):
                    for half in range(2):
                        A(act.copy(small[:, 56:57], ps[6 + n][:, half * 48 + 32:half * 48 + 33]))
                        A(act.activation(hid[:, n, half, 0:30].rearrange("p (g c) -> p g c", g=2), ps[6 + n][:, half * 48:half * 48 + 32].rearrange("p (g c) -> p g c", g=2)[:, :, 0:15],
                                         ACT.Gelu_apprx_tanh, bias=small[:, 56:57]),
                          "cmp_hact" if (n, half) == (1, 1) else "a_step")

            def compress_out():
                act.wait_ge(s["cmp_kv"], 1)
                A(act.copy(kcT[0:64, 0, 0:15], ps[6][0:64, 0:15]))
                A(act.copy(kcT[64:128, 1, 0:15], ps[6][64:128, 15:30]))
                A(act.copy(vc[0:15, :, :], ps[6][0:15, 64:192].rearrange("p (g d) -> p g d", g=2)), "gate_tok")
                act.wait_ge(s["gates_ps"], 1)
                A(act.copy(gtok[:, :, :], ps[7][:, 0:48].rearrange("p (t n) -> p t n", t=2)), "gate_tok")

            def attention(kind):
                units, b = UN[kind], UB[kind]
                n = len(units)
                for i in range(n + 2):
                    if i < n:
                        u, a = b + i, units[i]
                        act.wait_ge(s["max_ready"], u + 1)
                        if u >= 3:
                            act.wait_ge(s["pT_ps"], u - 2)
                        if u % 8 == 0 and u >= 16:
                            act.wait_ge(s["o_ready"], u // 8 - 1)
                        act.activation(Pp[:, u % 3, 0:a["K"]], SS[:, u % 3, 0:a["K"]], ACT.Exp, scale=-1.0,
                                       bias=nmax[:, u % 4:u % 4 + 1],
                                       accum_out=den[:, u % 16:u % 16 + 1]).then_inc(s["p_ready"], 1)
                    if i >= 2:
                        u, a = b + i - 2, units[i - 2]
                        act.wait_ge(s["pT_ps"], u + 1)
                        if u >= 2:
                            act.wait_ge(s["o_ps"], u - 1)
                        w = min(P, a["K"])
                        nn = P * -(-a["K"] // P)
                        act.copy(PT[0:w, u % 2, 0:nn], ps[3 + u % 2][0:w, 0:nn]).then_inc(s["pT_ev"], 1)

            def even_in():
                for n, it in enumerate(EVEN_ITEMS):
                    q = IB["even"] + n
                    act.wait_ge(s["item_ps"], q + 1)
                    bk = ps[4 + q % 4]
                    bank = bk[:, 0:T]
                    if it[0] == "small":
                        A(act.copy(gsm[0:16, :], bk[0:16, 0:T]))
                        A(act.add(fz[0:8, :], bk[0:8, T:2 * T], C("fox_b")[0:8, :])
                          if False else act.activation(fz[0:8, :], bk[32:40, 0:T], ACT.Identity,
                                                       bias=C("fox_b")[0:8, :]), "item_ev")
                    elif it[0] == "gz":
                        A(act.activation(gz[:, it[1], :], bank, ACT.Identity, bias=C("gla_b", it[1], it[1] + 1)),
                          "item_ev")
                    elif it[0] == "col":
                        j = it[1]
                        if j < 2:
                            A(act.mul(gqT[:, j, :], bank, HD ** -0.5), "item_ev")
                        elif j < 4:
                            A(act.copy(gkT[:, j - 2, :], bank), "item_ev")
                        elif j < 8:
                            A(act.activation(goT[:, j - 4, :], bank, ACT.Silu), "item_ev")
                        elif j < 12:
                            A(act.mul(fqT[:, j - 8, :], bank, HD ** -0.5), "item_ev")
                        else:
                            if j == 12:
                                act.wait_ge(s["pads_ready"], 5)
                            for g in range(2):
                                r = slice(g * HD, (g + 1) * HD)
                                A(act.copy(fkT[(j - 12) // 2][r, j % 2, g, :], bank[r, :]), "item_ev" if g else "a_step")
                    else:
                        _, t, w = it
                        lo, nn = (0, 256) if w == 0 else (256 + 384 * (w - 1), 384)
                        A(act.copy(evtok[:, t, lo:lo + nn], bk[:, 0:nn]), "item_ev")
                    hi_after("even", n)
                    if it == ("gz", 1):
                        log_gates()
                    if it == ("col", 11):
                        gla_decays()

            def log_gates():
                A(act.activation(gab, gz, ACT.Abs))
                A(act.activation(fab[0:8, :], fz[0:8, :], ACT.Abs))
                A(act.activation(gab, gab, ACT.Exp, scale=-1.0))
                A(act.activation(fab[0:8, :], fab[0:8, :], ACT.Exp, scale=-1.0))
                A(act.activation(gab, gab, ACT.Ln, bias=1.0))
                A(act.activation(fab[0:8, :], fab[0:8, :], ACT.Ln, bias=1.0), "gk_ab")

            def gla_decays():
                act.wait_ge(s["gk_cs"], 1)
                for c in range(2):
                    for t in range(TT):
                        tk = slice(t * P, (t + 1) * P)
                        i = 2 * c + t
                        act.activation(gE1[:, c, tk], gcs[:, c, tk], ACT.Exp, scale=1 / 16.0,
                                       bias=small[:, 64 + i:65 + i]).then_inc(s["e_ready"], 1)
                        act.activation(gE2[:, c, tk], gcs[:, c, tk], ACT.Exp, scale=-1 / 16.0,
                                       bias=small[:, 72 + i:73 + i]).then_inc(s["e_ready"], 1)
                act.activation(small[:, 80:82], small[:, 84:86], ACT.Exp, scale=1 / 16.0).then_inc(s["e_ready"], 1)

            def gla():
                act.wait_ge(s["tok_ps"], 5)
                A(act.copy(gkt, ps[2][:, 0:256].rearrange("p (c n) -> p c n", c=2)), "tok_ev")
                for t in range(TT):
                    act.wait_ge(s["y_ps"], 2 + t + 1)
                    A(act.copy(ogla[:, t, :], ps[1][:, :]), "y_ev")

            def odd_in():
                for n, it in enumerate(ODD_ITEMS):
                    q = IB["odd"] + n
                    act.wait_ge(s["item_ps"], q + 1)
                    bk = ps[4 + q % 4]
                    bank = bk[:, 0:T]
                    j = it[1]
                    if it[0] == "q":
                        A(act.mul(oqT[:, j, :], bank, HD ** -0.5), "item_ev")
                        hi_after("odd", n)
                        for m in (2 * j, 2 * j + 1):
                            K = P * (m // 8 + 1)
                            act.wait_ge(s["idx_ps"], m + 1)
                            if m >= 2:
                                act.wait_ge(s["idx_acc"], m - 1)
                            act.activation(idxs[:, m % 2, 0:K], ps[m % 2][:, 0:K], ACT.Relu).then_inc(s["idx_relu"], 1)
                    elif it[0] == "qi":
                        A(act.mul(qiT[:, j, :], bank, HD ** -0.5), "item_ev")
                    elif it[0] == "ki":
                        act.wait_ge(s["pads_ready"], 6)
                        for g in range(2):
                            r = slice(g * HD, (g + 1) * HD)
                            A(act.copy(kiT[r, g, :], bank[r, :]), "item_ev" if g else "a_step")
                    elif it[0] == "ckv":
                        A(act.copy(ckv[:, j, :], bank), "item_ev")
                        A(act.activation(csc, ckv[:, j, :], ACT.Square, accum_out=small[:, 88 + j:89 + j]), "c_ss")
                    else:
                        A(act.mul(wtok[:, j, :], bk[:, 0:8], 8 ** -0.5), "item_ev")
                    if it[0] != "q":
                        hi_after("odd", n)
                act.wait_ge(s["c_ps"], 1)
                for c in range(2):
                    A(act.mul(cT[:, c, :], ps[3][:, c * T:(c + 1) * T], C("kv_norm", c, c + 1)),
                      "c_ev" if c else "a_step")
                act.wait_ge(s["pads_ready"], 8)
                for n, it in enumerate(UKV_ITEMS):
                    q = IB["ukv"] + n
                    act.wait_ge(s["item_ps"], q + 1)
                    bk = ps[4 + q % 4]
                    if it[0] == "kh":
                        for g in range(2):
                            r = slice(g * HD, (g + 1) * HD)
                            A(act.copy(khT[g][r, it[1], :], bk[r, 0:T]), "item_ev" if g else "a_step")
                    else:
                        A(act.copy(vh[:, it[1], it[2] * 512:(it[2] + 1) * 512], bk[:, :]), "item_ev")

            act.dma_start(cst[:, 0:FIRST], consts_in[:, 0:FIRST]).then_inc(s["first_loaded"], 16)
            gain(0)
            act.dma_start(cst[:, FIRST:NCONST], consts_in[:, FIRST:NCONST]).then_inc(s["consts_loaded"], 16)
            act.dma_start(W(5120, MASKS), masks_in).then_inc(s["masks_loaded"], 16)
            gain(1)
            act.wait_ge(s["first_loaded"], 16)
            norm(0)
            w_in()
            compress()
            rwkv()
            attention("nsa")
            norm(1)
            ffn(0)
            norm(2)
            norm(3)
            ffn(1)
            norm(4)
            act.wait_ge(s["t5_ps"], 1)
            A(act.copy(ffb[0:16, 0:2, :].rearrange("p a b -> p (a b)")[:, 0:384], ps[7][0:16, 0:384]), "t5_sb")
            act.dma_start(scratch, ffb[0:16, 0:2, :].rearrange("p a b -> p (a b)")[:, 0:384]).then_inc(s["t5_out"], 16)
            even_in()
            gla()
            attention("fox")
            act.wait_ge(s["t5_out"], 16)
            norm(5)
            ffn(2)
            norm(6)
            ffn(3)
            norm(7)
            act.dma_start(bias16, bass.AP(scratch.tensor, 0, [[1, P], [384, 16], [1, T]])).then_inc(s["t5_in"], 16)
            odd_in()
            attention("dsa")
            norm(8)
            ffn(4)
            norm(9)

        @block.gpsimd
        def _(gp):
            cnt = {}

            def G(ins, name="g_step"):
                cnt[name] = cnt.get(name, 0) + 1
                ins.then_inc(s[name], 1)
                gp.wait_ge(s[name], cnt[name])

            def rsqrt(o, i, scale, eps, name):
                n = i.shape[1]
                G(gp.tensor_scalar(o, i, scale, eps, ALU.mult, ALU.add))
                G(gp.tensor_tensor(o, o, C("neg_half", 0, n), ALU.pow), name)

            def norm(n):
                for t in range(TT):
                    gp.wait_ge(s["ss_ready"], 2 * n + t + 1)
                    rsqrt(rstd[:, t:t + 1], ss[:, t:t + 1], 1.0 / D, 1e-6, "rstd_ready")

            G(gp.memset(raw[:, :, 0:1], 0.0), "scan_in")
            G(gp.memset(zk[:, 2, :], 0.0), "scan_in")
            G(gp.memset(zv[:, 2, :], 0.0), "scan_in")
            gp.wait_ge(s["first_loaded"], 16)
            norm(0)
            gp.wait_ge(s["masks_loaded"], 16)
            G(gp.tensor_copy(msk[:], W(5120, MASKS)), "masks_ready")
            for k in (ksT, kwT, kcT[:]):
                G(gp.memset(k, 0.0), "pads_ready")
            G(gp.memset(Sst, 0.0))
            gp.wait_ge(s["item_ps"], IB["in"] + len(IN_ITEMS))
            G(gp.memset(AA4[3], 0.0))
            gp.wait_ge(s["ab_ready"], 1)
            for k in range(3):
                G(gp.memset(AA4[k], 0.0), "id_ready")
            for t in range(TT):
                gp.wait_ge(s["var_ready"], t + 1)
                rsqrt(small[:, 96 + 8 * t:104 + 8 * t], small[:, 112 + 8 * t:120 + 8 * t], 1.0 / HD, 64e-5, "grs_ready")
            norm(1)
            norm(2)
            norm(3)
            norm(4)
            for k in fkT:
                G(gp.memset(k, 0.0), "pads_ready")
            gp.wait_ge(s["item_ps"], IB["even"] + len(EVEN_ITEMS))
            G(gp.memset(gA, 0.0), "id_ready")
            G(gp.memset(gS, 0.0), "id_ready")
            for t in range(TT):
                gp.wait_ge(s["var_ready"], 2 + t + 1)
                rsqrt(small[:, 128 + 4 * t:132 + 4 * t], small[:, 136 + 4 * t:140 + 4 * t], 1.0 / P, 1e-6, "grs_ready")
            norm(5)
            norm(6)
            norm(7)
            G(gp.memset(kiT, 0.0), "pads_ready")
            G(gp.memset(khT[0], 0.0), "pads_ready")
            gp.wait_ge(s["xT_ps"], 4 * TN[7] + 4)
            G(gp.memset(khT[1], 0.0), "pads_ready")
            gp.wait_ge(s["c_ss"], 2)
            rsqrt(small[:, 90:92], small[:, 88:90], 1.0 / 256, 1e-6, "c_rs")
            norm(8)
            norm(9)

        @block.vector
        def _(v):
            cnt = {}

            def V(ins, name="v_step"):
                cnt[name] = cnt.get(name, 0) + 1
                ins.then_inc(s[name], 1)
                v.wait_ge(s[name], cnt[name])

            def norm(n, dst=None):
                v.wait_ge(s[f"gain{n % 2}"], 16 * (n // 2 + 1))
                for t in range(TT):
                    v.wait_ge(s["rstd_ready"], 2 * n + t + 1)
                    V(v.scalar_tensor_tensor((xn if dst is None else dst)[:, t, :], x[:, t, :], rstd[:, t:t + 1],
                                             gb[:, n % 2, :], ALU.mult, ALU.mult), "xn_ready")
                    if n == 2:
                        v.sem_inc(s["x_done"], 1)
                if n == 0:
                    for t in range(TT):
                        v.wait_ge(s["xT_ps"], 2 * t + 2)
                        V(v.tensor_copy(uT[:, 4:8, t * P:(t + 1) * P],
                                        ps[5 + 2 * t][:, :].rearrange("p (c n) -> p c n", c=4)), "uT_v")
                if n in SPLIT_OF:
                    f = SPLIT_OF[n]
                    if n in FFN_OF:
                        lo_a(FFN_OF[n], 0)
                    else:
                        lo_block(PROJ_OF[n], 0)
                    for i in range(4):
                        v.wait_ge(s["uT_hi"], 4 * f + i + 1)
                        c0, t = 4 * (i % 2), i // 2
                        v.tensor_tensor(uT_r[1][:, c0:c0 + 4, t * P:(t + 1) * P],
                                        ps[4 + i][:, :].rearrange("p (c n) -> p c n", c=4),
                                        uT_r[0][:, c0:c0 + 4, t * P:(t + 1) * P].bitcast(F32),
                                        ALU.subtract).then_inc(s["uT_lo"], 1)

                if n == 4:
                    v.wait_ge(s["small_hi"], 1)
                    v.tensor_tensor(w_small[1][:, :], C("even_small"), w_small[0][:, :].bitcast(F32),
                                    ALU.subtract).then_inc(s["small_lo"], 1)

            def lo_block(kind, blk):
                i = (BASE[kind + "_in"] + blk // 3) % RING
                v.wait_ge(s["hi_blk"], PB[kind] + blk + 1)
                f = blk % 3 * P
                view = lambda r: r[:, i, :].rearrange("p (k f) -> p k f", k=KC)[:, :, f:f + P]
                v.tensor_tensor(view(ring_r), view(ring), w_h[kind][blk // 3 % 2][:, :, f:f + P].bitcast(F32),
                                ALU.subtract).then_inc(s["lo_blk"], 1)

            def lo_a(f, c, r=0):
                q, i = FC * f, BASE[f"ffn{f}"] + c
                v.wait_ge(s["hi_a"], r + (q + c + 1))
                v.tensor_tensor(w_gu[:, c % 2, 1, :], slot(i)[:, 0:2 * D], w_gu[:, c % 2, 0, :].bitcast(F32),
                                ALU.subtract).then_inc(s["lo_a"], 1)

            def lo_b(f, c, r=0):
                q, i = FC * f, BASE[f"ffn{f}"] + c
                v.wait_ge(s["hi_b"], r + (q + c + 1))
                v.tensor_tensor(w_dn[:, c % 2, 1, :], slot(i)[:, 2 * D:3 * D], w_dn[:, c % 2, 0, :].bitcast(F32),
                                ALU.subtract).then_inc(s["lo_b"], 1)
                v.wait_ge(s["lo_b"], r + (q + c + 1))
                v.sem_inc(s[f"free{i % RING}"], 1)

            def residual(scale, first, n, last, m):
                for t, (sem, k) in enumerate(((first, n), (last, m))):
                    v.wait_ge(s[sem], k)
                    for half in range(2):
                        xs = x[:, t, half * 512:(half + 1) * 512]
                        V(v.scalar_tensor_tensor(xs, ps[2 * t + half][:, :], scale, xs, ALU.mult, ALU.add),
                          "x_done" if half else "v_step")

            def ffn(f, scale):
                q = FC * f

                def step(c, r=0):
                    n = q + c
                    v.wait_ge(s["silu_ready"], r + (n + 1))
                    h, hr = sg[:, c % 2, :], h_r[:, c % 2, :, :]
                    v.tensor_tensor(h, h, ps[4 + c % 2][:, T:2 * T], ALU.mult).then_inc(s["h_mul"], 1)
                    v.wait_ge(s["h_mul"], r + (n + 1))
                    if n >= 2:
                        v.wait_ge(s["down_done"], r + (n - 1))
                    v.tensor_copy(hr[:, 0, :], h).then_inc(s["h_hi"], 1)
                    v.wait_ge(s["h_hi"], r + (n + 1))
                    v.tensor_tensor(hr[:, 1, :], h, hr[:, 0, :].bitcast(F32), ALU.subtract).then_inc(s["h_ready"], 1)
                    if c + 2 < FC:
                        lo_a(f, c + 2, r)
                    if c + 1 < FC:
                        lo_b(f, c + 1, r)
                lo_b(f, 0)
                lo_a(f, 1)
                step(0)
                step(1)
                with v.Fori(0, 4 * LOOPS, 4) as r:
                    for j in range(4):
                        step(2 + j, r)
                for c in range(2 + 4 * LOOPS, FC):
                    step(c)
                residual(scale, "acc0_done", f + 1, "down_done", q + FC)

            def w_in():
                v.wait_ge(s["scan_in"], 3)
                order = {j: n for n, it in enumerate(IN_ITEMS) if it[0] == "col" for j in [it[1]]}
                dst = [lora[:, 0, :], lora[:, 1, :]] + [m[:, j, :] for m in (pk, pr, pv) for j in range(4)]

                def shift(js):
                    for j in js:
                        v.wait_ge(s["item_ev"], IB["in"] + order[j] + 1)
                        V(v.tensor_tensor(dst[j], raw[:, j % 4, 0:256], raw[:, j % 4, 1:257], ALU.subtract))
                        V(v.scalar_tensor_tensor(dst[j], dst[j], C("mu", j, j + 1), raw[:, j % 4, 1:257],
                                                 ALU.mult, ALU.add), "shift_ready")
                        v.sem_inc(s["raw_free"], 1)
                shift(range(0, 6))
                for c in range(4):
                    V(v.tensor_scalar(kk[:, c, :], pk[:, c, :], C("k_k", c, c + 1), None, ALU.mult))
                v.wait_ge(s["masks_ready"], 1)
                V(v.tensor_tensor(tmp, kk, kk, ALU.mult), "kk_sq")
                v.wait_ge(s["n2_ps"], 1)
                for c in range(2):
                    V(v.tensor_scalar(tmp[:, 2 * c:2 * c + 2, :], ps[c][:, :].rearrange("p (a b) -> p a b", a=2),
                                      1e-24, None, ALU.max), "kk_clamped" if c else "v_step")
                shift(range(6, 8))
                v.wait_ge(s["kk_sqrt"], 1)
                V(v.reciprocal(tmp, tmp))
                V(v.tensor_tensor(kk, kk, tmp, ALU.mult))
                for c in range(4):
                    V(v.tensor_scalar(tmp[:, c, :], agm[:, c, :], -1.0, C("k_a", c, c + 1), ALU.add, ALU.mult))
                V(v.scalar_tensor_tensor(kp, tmp, 1.0, pk, ALU.add, ALU.mult))
                shift(range(8, 10))
                for c in range(4):
                    V(v.scalar_tensor_tensor(tmp[:, c, :], pr[:, c, :], C("r_k", c, c + 1), kp[:, c, :],
                                             ALU.mult, ALU.mult), "rk_ready" if c == 3 else "v_step")
                shift(range(10, 12))
                for c in range(4):
                    for t in range(TT):
                        tk = slice(t * P, (t + 1) * P)
                        V(v.tensor_tensor_scan(cs[:, c, tk], C("ones"), sgm[:, c, tk], 0.0, ALU.mult, ALU.add))
                V(v.tensor_tensor(csp, cs, sgm, ALU.subtract))
                mid = cs.rearrange("p c (t n) -> p (c t) n", t=2)
                V(v.tensor_scalar(small[:, 32:40], mid[:, :, 63], DECAY, None, ALU.mult))
                V(v.tensor_scalar(small[:, 40:48], mid[:, :, 63], -DECAY, None, ALU.mult))
                V(v.tensor_tensor(small[:, 52:56], cs[:, :, 127], cs[:, :, 63], ALU.subtract))
                V(v.tensor_tensor(small[:, 52:56], small[:, 52:56], cs[:, :, 191], ALU.add), "csm_ready")
                shift(range(12, 14))
                v.wait_ge(s["e_ready"], 25)
                arv = arT.rearrange("p c t (w n) -> p c t w n", w=2)
                for c in range(4):
                    re = lambda a: a[:, c, :].rearrange("p (t n) -> p t n", t=2)
                    V(v.scalar_tensor_tensor(arv[:, c, :, 0, :], re(kk), -1.0, re(E3), ALU.mult, ALU.mult))
                    V(v.tensor_tensor(arv[:, c, :, 1, :], re(pr), re(E1), ALU.mult))
                V(v.tensor_tensor(bT, kk, agm, ALU.mult))
                V(v.tensor_tensor(bT, bT, E2, ALU.mult))
                V(v.tensor_tensor(kT_, kp, E2, ALU.mult), "ab_ready")

            def rwkv():
                v.wait_ge(s["bon_ps"], 1)
                v.wait_ge(s["tok_ps"], 2)
                for c in range(2):
                    V(v.tensor_tensor(pv[:, 2 * c:2 * c + 2, :], ps[2 + c][:, :].rearrange("p (a b) -> p a b", a=2),
                                      pv[:, 2 * c:2 * c + 2, :], ALU.mult), "bonus_read" if c else "v_step")
                for u in range(RWKV_UNITS):
                    k = u // 4
                    if u % 4 == 0:
                        v.wait_ge(s["id_ready"], min(k + 1, 3))
                        v.wait_ge(s["eye_ready"], 2 * (k + 1))
                    v.wait_ge(s["A_ps"], u + 1)
                    V(v.copy_predicated(Mt[:, u, :], mask(LEVELS), ps[u % 4][:, 0:P]))
                    V(v.copy_predicated(AA4[k][:, u % 4, :], msk[:, 0:512], ps[u % 4][:, :]), "A_read")
                    if u % 4 == 3:
                        for par in range(2):
                            V(v.copy_predicated(Mm[:, 4 * k + par:4 * k + 4:2, :],
                                                mask(0).unsqueeze(1).to_broadcast([P, 2, P]),
                                                ps[4 + 2 * (k % 2) + par][:, 0:256].rearrange("p (u n) -> p u n", u=2)),
                              "M_ready" if par else "v_step")
                for q in range((LEVELS - 1) * QUADS):
                    v.wait_ge(s["dM_ps"], q + 1)
                    lv, qs = q // QUADS + 1, slice(4 * (q % QUADS), 4 * (q % QUADS) + 4)
                    if lv < LEVELS - 1:
                        V(v.copy_predicated(Mm[:, qs, :], mask(lv).unsqueeze(1).to_broadcast([P, 4, P]),
                                            ps[2 + q % 2][:, :].rearrange("p (u n) -> p u n", u=4)))
                    V(v.copy_predicated(Mt[:, qs, :], mask(LEVELS + lv).unsqueeze(1).to_broadcast([P, 4, P]),
                                        ps[4 + q % 2][:, :].rearrange("p (u n) -> p u n", u=4)), "M_ready")
                v.wait_ge(s["s_ps"], 1)
                for hh in range(2):
                    r = slice(hh * HD, (hh + 1) * HD)
                    V(v.tensor_tensor(Sst[r, :, hh * HD:(hh + 1) * HD],
                                      ps[4][r, :].rearrange("p (c n) -> p c n", c=4)[:, :, hh * HD:(hh + 1) * HD],
                                      small[r, 48:52].unsqueeze(2).to_broadcast([HD, 4, HD]), ALU.mult),
                      "s_ev" if hh else "v_step")
                for t in range(TT):
                    v.wait_ge(s["y_ev"], t + 1)
                    yv = ytok[:, t, :].rearrange("p (h n) -> p h n", h=8)
                    sq = kk[:, 0:2, :].rearrange("p a (h n) -> p (a h) n", n=HD)
                    mean = small[:, 144:152]
                    V(v.tensor_reduce(mean, yv, AX.X, ALU.add))
                    V(v.tensor_scalar(mean, mean, 1.0 / HD, None, ALU.mult))
                    V(v.tensor_tensor(yv, yv, mean.unsqueeze(2).to_broadcast([P, 8, HD]), ALU.subtract))
                    V(v.tensor_tensor(sq, yv, yv, ALU.mult))
                    V(v.tensor_reduce(small[:, 112 + 8 * t:120 + 8 * t], sq, AX.X, ALU.add), "var_ready")
                    v.wait_ge(s["grs_ready"], t + 1)
                    V(v.tensor_tensor(yv, yv, small[:, 96 + 8 * t:104 + 8 * t].unsqueeze(2).to_broadcast([P, 8, HD]),
                                      ALU.mult), "yn_ready")

            def rwkv_out(t):
                v.wait_ge(s["ynT_ps"], t + 1)
                tk = slice(t * P, (t + 1) * P)
                for c in range(4):
                    V(v.tensor_scalar(yT[:, c, tk], ps[7][:, c * P:(c + 1) * P], C("lnx_w", c, c + 1),
                                      C("lnx_b", c, c + 1), ALU.mult, ALU.add), "ynT_ev" if c == 3 else "v_step")
                V(v.tensor_tensor(yT[:, 0:4, tk], yT[:, 0:4, tk], pv[:, :, tk], ALU.add))
                V(v.tensor_tensor(yT[:, 0:4, tk], yT[:, 0:4, tk], gg[:, :, tk], ALU.mult))

            def compress():
                v.wait_ge(s["gate_tok"], 2)
                for t in range(TT):
                    gv = gtok[:, t, :].rearrange("p (h b) -> p h b", b=3)[:, :, 0]
                    V(v.tensor_scalar(gv, gv, C("any_ok", t, t + 1), None, ALU.mult), "cmp_ready")

            def attention(kind, beside={}):
                units, b = UN[kind], UB[kind]
                n = len(units)

                def result(grp):
                    v.wait_ge(s["o_ps"], 8 * (grp + 1))
                    V(v.reciprocal(rden, den[:, grp % 2 * 8:grp % 2 * 8 + 8]))
                    g = grp - b // 8
                    o = ps[5 + grp % 2][:, :].rearrange("p (h n) -> p h n", h=8)
                    if kind == "nsa":
                        t, br = g // 3, g % 3
                        V(v.tensor_tensor(rden, rden, gtok[:, t, br:24:3], ALU.mult))
                        dst = onsa[:, t, :]
                    elif kind == "fox":
                        br, dst = 0, ofox[:, g, :]
                    else:
                        br, dst = 0, odsa[:, g // 2, g % 2 * 512:(g % 2 + 1) * 512]
                    dst = dst.rearrange("p (h n) -> p h n", h=8)
                    r = rden.unsqueeze(2).to_broadcast([P, 8, HD])
                    if br:
                        V(v.tensor_tensor(obr, o, r, ALU.mult))
                        V(v.tensor_tensor(dst, dst, obr, ALU.add), "o_ready")
                    else:
                        V(v.tensor_tensor(dst, o, r, ALU.mult), "o_ready")

                for i in range(n):
                    if i in beside:
                        beside[i]()
                    u, a = b + i, units[i]
                    K = a["K"]
                    v.wait_ge(s["S_ps"], u + 1)
                    if u >= 3:
                        v.wait_ge(s["p_ready"], u - 2)
                    V(v.tensor_tensor_reduce(SS[:, u % 3, 0:K], ps[u % 3][:, 0:K], a["dist"], -a["scale"], 3e38,
                                             ALU.add, ALU.min, nmax[:, u % 4:u % 4 + 1]), "max_ready")
                    if i % 8 == 4 and i > 8:
                        result(u // 8 - 1)
                result((b + n) // 8 - 1)

            def mix_T(n0, c0):
                for t in range(TT):
                    v.wait_ge(s["oT_ps"], n0 + t + 1)
                    V(v.tensor_copy(yT[:, c0:c0 + 4, t * P:(t + 1) * P],
                                    ps[2 + t][:, :].rearrange("p (c n) -> p c n", c=4)),
                      "mix_ready" if t else "v_step")

            def even_in():
                for blk in range(1, 10):
                    lo_block("even", blk)
                v.wait_ge(s["item_ev"], IB["even"] + EVEN_ITEMS.index(("gz", 1)) + 1)
                V(v.tensor_scalar(gmn, gz, 0.0, None, ALU.min))
                V(v.tensor_scalar(fmn[0:8, :], fz[0:8, :], 0.0, None, ALU.min))
                v.wait_ge(s["gk_ab"], 1)
                V(v.tensor_tensor(gmn, gmn, gab, ALU.subtract))
                V(v.tensor_tensor(fmn[0:8, :], fmn[0:8, :], fab[0:8, :], ALU.subtract))
                for t in range(TT):
                    V(v.tensor_tensor_scan(fsum[0:8, t * P:(t + 1) * P], C("ones")[0:8, :],
                                           fmn[0:8, t * P:(t + 1) * P],
                                           fsum[0:8, t * P - 1:t * P] if t else 0.0, ALU.mult, ALU.add),
                      "v_step")
                V(v.tensor_scalar(fneg[0:8, :], fsum[0:8, :], -1.0, None, ALU.mult))
                for c in range(2):
                    for t in range(TT):
                        tk = slice(t * P, (t + 1) * P)
                        V(v.tensor_tensor_scan(gcs[:, c, tk], C("ones"), gmn[:, c, tk], 0.0, ALU.mult, ALU.add))
                mid = gcs.rearrange("p c (t n) -> p (c t) n", t=2)
                V(v.tensor_scalar(small[:, 64:68], mid[:, :, 63], -1 / 16.0, None, ALU.mult))
                V(v.tensor_scalar(small[:, 72:76], mid[:, :, 63], 1 / 16.0, None, ALU.mult))
                V(v.tensor_tensor(small[:, 84:86], gcs[:, :, 127], gcs[:, :, 63], ALU.subtract))
                V(v.tensor_tensor(small[:, 84:86], small[:, 84:86], gcs[:, :, 191], ALU.add), "gk_cs")
                for blk in range(10, 18):
                    lo_block("even", blk)
                v.wait_ge(s["e_ready"], 25 + 9)
                V(v.tensor_tensor(gqd, gqT, gE1, ALU.mult))
                V(v.tensor_tensor(gkd, gkT, gE2, ALU.mult), "gla_k")
                for blk in range(18, BLOCKS["even"]):
                    lo_block("even", blk)

            def gla():
                v.wait_ge(s["id_ready"], 5)
                for t in range(TT):
                    v.wait_ge(s["A_ps"], RWKV_UNITS + t + 1)
                    if t:
                        v.wait_ge(s["y_ps"], 3)
                    for par in range(2):
                        V(v.copy_predicated(gA[:, par:4:2, :], msk[:, P:2 * P].unsqueeze(1).to_broadcast([P, 2, P]),
                                            ps[4 + par][:, 0:256].rearrange("p (h n) -> p h n", h=2)),
                          "A_read" if par else "v_step")
                    if not t:
                        v.wait_ge(s["s_ps"], 2)
                        for hh in range(2):
                            r = slice(hh * HD, (hh + 1) * HD)
                            for c in range(2):
                                V(v.tensor_scalar(gS[r, c, hh * P:(hh + 1) * P],
                                                  ps[6][r, c * 256 + hh * P:c * 256 + (hh + 1) * P],
                                                  small[r, 80 + c:81 + c], None, ALU.mult),
                                  "s_ev" if (hh, c) == (1, 1) else "v_step")
                for t in range(TT):
                    v.wait_ge(s["y_ev"], 3 + t)
                    yv = ogla[:, t, :].rearrange("p (h n) -> p h n", h=4)
                    sq = gsq.rearrange("p (h n) -> p h n", h=4)
                    V(v.tensor_tensor(sq, yv, yv, ALU.mult))
                    V(v.tensor_reduce(small[:, 136 + 4 * t:140 + 4 * t], sq, AX.X, ALU.add), "var_ready")
                    v.wait_ge(s["grs_ready"], 3 + t)
                    V(v.tensor_tensor(yv, yv, small[:, 128 + 4 * t:132 + 4 * t].unsqueeze(2).to_broadcast([P, 4, P]),
                                      ALU.mult), "yn_ready")
                for t in range(TT):
                    v.wait_ge(s["ynT_ps"], 3 + t)
                    tk = slice(t * P, (t + 1) * P)
                    V(v.scalar_tensor_tensor(yT[:, 0:4, tk], ps[t][:, :].rearrange("p (c n) -> p c n", c=4),
                                             C("gla_norm"), goT[:, :, tk], ALU.mult, ALU.mult), "gla_ready")

            def odd_in():
                for blk in range(1, 7):
                    lo_block("odd", blk)
                v.wait_ge(s["c_rs"], 1)
                for t in range(TT):
                    V(v.tensor_scalar(ckv[:, t, :], ckv[:, t, :], small[:, 90 + t:91 + t], None, ALU.mult),
                      "c_n" if t else "v_step")
                for t in range(TT):
                    K = P * (t + 1)
                    for h in range(8):
                        n = 8 * t + h
                        if n == 0:
                            for blk in range(7, 14):
                                lo_block("odd", blk)
                        if n == 2:
                            lo_block("odd", 14)
                        v.wait_ge(s["idx_relu"], n + 1)
                        rl, sc = idxs[:, n % 2, 0:K], score[:, 0:K]
                        if h:
                            V(v.scalar_tensor_tensor(sc, rl, wtok[:, t, h:h + 1], sc, ALU.mult, ALU.add), "idx_acc")
                        else:
                            V(v.tensor_scalar(sc, rl, wtok[:, t, h:h + 1], None, ALU.mult), "idx_acc")
                    causal = C("causal", P * (1 - t), P * (1 - t) + K)
                    V(v.tensor_tensor(sc, sc, causal, ALU.add))
                    for r in range(TOPK // 8):
                        V(v.max(small[:, 152:160], sc))
                        V(v.match_replace(sc, small[:, 152:160], sc, -3e38))
                    V(v.tensor_scalar(sc, sc, -2e38, NEG, ALU.is_gt, ALU.mult))
                    V(v.tensor_tensor(selm[:, t, 0:K], sc, causal, ALU.add), "sel_ready")

            norm(0)
            w_in()
            rwkv()
            compress()
            attention("nsa", {8: lambda: rwkv_out(0), 20: lambda: rwkv_out(1)})
            mix_T(0, 4)
            residual(1.0, "op_acc", 1, "op_acc", 2)
            norm(1)
            ffn(0, 1.0)
            norm(2, x)
            norm(3)
            ffn(1, 0.5)
            norm(4)
            even_in()
            gla()
            attention("fox")
            mix_T(2, 4)
            residual(1.0, "op_acc", 3, "op_acc", 4)
            norm(5)
            ffn(2, 0.5)
            norm(6)
            ffn(3, 0.5)
            norm(7)
            odd_in()
            attention("dsa")
            for t in range(TT):
                for half in range(2):
                    v.wait_ge(s["oT_ps"], 4 + 2 * t + half + 1)
                    V(v.tensor_copy(yT[:, 4 * half:4 * half + 4, t * P:(t + 1) * P],
                                    ps[2 * t + half][:, :].rearrange("p (c n) -> p c n", c=4)),
                      "mix_ready" if (t, half) == (1, 1) else "v_step")
            residual(1.0, "op_acc", 5, "op_acc", 6)
            norm(8)
            ffn(4, 0.5)
            norm(9, x)


def column_blocks(w, cols, width=3 * P):
    cols = np.concatenate([cols, np.full((-len(cols)) % width, -1)])
    w = np.concatenate([w, np.zeros((w.shape[0], 1), w.dtype)], axis=1)[:, cols]
    return [np.ascontiguousarray(w[:, i:i + width].reshape(KC, P, width).transpose(1, 0, 2)).reshape(P, SLOT)
            for i in range(0, len(cols), width)]


def row_blocks(w):
    w = np.concatenate([w, np.zeros((P, D), w.dtype)]).reshape(3, 3, P, D)
    return [np.ascontiguousarray(w[i].transpose(1, 0, 2)).reshape(P, SLOT) for i in range(3)]


def ffn_slots(gate, up, down):
    g, u = (m.reshape(KC, P, FC, P).transpose(2, 1, 0, 3).reshape(FC, P, D) for m in (gate, up))
    return list(np.concatenate([g, u, down.reshape(FC, P, D)], axis=2))


def padded(a, n=SLOT):
    return np.concatenate([a, np.zeros((P, n - a.shape[1]), a.dtype)], axis=1)


def rows(a):
    return np.concatenate([a, np.zeros((P - a.shape[0], a.shape[1]), a.dtype)])


def columns(vec):
    return np.ascontiguousarray(vec.reshape(-1, P).T)


def lay_out(i):
    r = np.arange
    w_in, od, ev = i["w_in"][0], i["odd_w_in_2"][0], i["even_w_in_2"][0]
    q0 = 1792
    rwkv = np.concatenate([r(1536, 1792), r(512, 1024), r(0, 512), r(1024, 1536)])
    q = np.concatenate([q0 + h * HD + r(HD) for j in range(4) for h in (j, j + 4)])
    kv = q0 + 512
    in_cols = np.concatenate([rwkv, q, kv + r(256), kv + 256 + r(128), kv + 512 + r(128), kv + 384 + r(128),
                              kv + 640 + r(128)])
    slots = column_blocks(w_in, in_cols)
    pieces = np.concatenate([i["nsa_cmp_k_w1"][0], i["nsa_cmp_v_w1"][0]]).reshape(32, P, 256)
    for a in range(0, 32, 12):
        slots.append(padded(pieces[a:a + 12].transpose(1, 0, 2).reshape(P, -1)))
    slots += row_blocks(i["w_out"][0])
    slots += ffn_slots(i["ffn_w_gate"][0], i["ffn_w_up"][0], i["ffn_w_down"][0])
    f_in, f_out = i["ffn_w_in_2"], i["ffn_w_out_2"]

    def ffn2(layer, n):
        return ffn_slots(f_in[layer, n][:, :F], f_in[layer, n][:, F:], f_out[layer, n])
    slots += ffn2(0, 0)
    e_cols = np.concatenate([r(0, 512), 1024 + r(512), 1552 + r(1024), 512 + r(512), 2576 + r(512)])
    slots += column_blocks(ev, e_cols)
    slots += row_blocks(i["even_w_out_2"][0])
    slots += ffn2(0, 1) + ffn2(1, 0)
    o_cols = np.concatenate([1792 + r(64), 1792 + r(64), 1024 + r(256), 1280 + r(512), r(1024)])
    slots += column_blocks(od, o_cols)
    uk = i["mla_w_uk_2"][0].transpose(2, 0, 1).reshape(2, P, D).transpose(1, 0, 2).reshape(P, 2 * D)
    uv = i["mla_w_uv_2"][0].transpose(1, 0, 2).reshape(2, P, D).transpose(1, 0, 2).reshape(P, 2 * D)
    slots += [padded(uk), padded(uv)]
    slots += row_blocks(i["odd_w_out_2"][0])
    slots += ffn2(1, 1)
    wstream = np.stack(slots)
    assert wstream.shape == (NSLOTS, P, SLOT)

    gains = [i["norm1_g"][0], i["norm2_g"][0], i["norm_f_g"]] + [i["norm_g_2"][a, b] for a in range(2) for b in range(3)]
    gains = np.concatenate(gains + [i["final_norm_g_2"]])
    gains = np.ascontiguousarray(np.broadcast_to(gains, (P, gains.size)))

    def small_w(w, cols):
        return w[:, cols].reshape(KC, P, len(cols)).transpose(1, 0, 2).reshape(P, -1)

    z64 = np.zeros((64, 512), np.float32)
    ck2 = i["nsa_cmp_k_w2"][0].reshape(2, P, HD).transpose(1, 0, 2)
    cv2 = i["nsa_cmp_v_w2"][0].reshape(2, P, HD).transpose(1, 0, 2).reshape(P, P)
    p_, c_ = np.arange(P)[:, None], np.arange(T)[None, :]
    dist = P + p_ - c_
    causal = np.where(dist >= 0, 0.0, NEG)
    end = np.arange(16)[None, :] * CMP_STRIDE + 31
    cmp_d = np.concatenate([np.where(end <= t * P + p_, -np.abs(t * P + p_ - end).astype(np.float64), NEG)
                            for t in range(TT)], axis=1)
    d = np.maximum(255 - np.arange(384), 0)
    large = 16 + (np.log(np.maximum(d, 1) / 16) / np.log(8.0) * 16 + 1e-9).astype(np.int64)
    bucket = np.where(d < 16, d, np.minimum(large, 31))
    c = {
        "ident": np.eye(P), "reverse": np.eye(P)[::-1], "pair_ones": np.kron(np.eye(2), np.ones((HD, HD))), "ones": np.ones((P, P)),
        "w2": np.concatenate([i["rwkv_w2"][0], z64]), "a2": np.concatenate([z64, i["rwkv_a2"][0]]),
        "g2": i["rwkv_g2"][0], "gate_w": small_w(w_in, q0 + 1280 + r(24)),
        "even_small": small_w(np.concatenate([ev, np.zeros((D, 1), ev.dtype)], axis=1),
                              np.concatenate([1536 + r(16), np.full(16, -1), 3088 + r(8)])), "odd_small": small_w(od, 1856 + r(8)),
        "gla_gate": rows(i["gla_w_gate_2"][0]), "ck2": np.concatenate([ck2, ck2], axis=2).reshape(P, 256), "cv2": cv2,
        "pe_k": i["nsa_pe_k"][0].reshape(16, P).T, "pe_v": i["nsa_pe_v"][0].reshape(16, P).T,
        "t5": rows(i["t5_table_2"]), "t5_onehot": rows((bucket[None, :] == np.arange(32)[:, None]).astype(np.float32)),
        "alibi": np.where(dist >= 0, -dist, NEG), "alibi_cmp": cmp_d,
        "any_ok": np.concatenate([(p_ + t * P >= 31).astype(np.float32) for t in range(TT)], axis=1),
        "causal": causal, "neg_half": np.full((P, 32), -0.5),
        "mu": columns(i["mu_shift"][0][rwkv]), "w0": columns(i["rwkv_w0"][0]), "a0": columns(i["rwkv_a0"][0]),
        "k_k": columns(i["rwkv_k_k"][0]), "k_a": columns(i["rwkv_k_a"][0]), "r_k": columns(i["rwkv_r_k"][0].reshape(-1)),
        "lnx_w": columns(i["rwkv_lnx_w"][0]), "lnx_b": columns(i["rwkv_lnx_b"][0]), "gla_b": columns(i["gla_b_gate_2"][0]),
        "gla_norm": columns(i["gla_norm_g_2"][0]), "fox_b": rows(i["fox_b_f_2"][0][:, None]),
        "q_scale": HD ** -0.5 * 2.0 ** (1 + np.arange(4)[None, :] + 4 * (p_ // HD)),
        "kv_norm": columns(i["mla_kv_norm_g_2"][0]),
    }
    for name, n in CONSTS:
        assert c[name].shape == (P, n), (name, c[name].shape)
    consts = np.concatenate([c[name].astype(np.float32) for name, _ in CONSTS], axis=1)
    strict, incl = (p_ < p_.T), (p_ <= p_.T)
    below = [((p_ // b) % 2 == 1) & (p_.T // b == p_ // b - 1) for b in (1 << lv for lv in range(LEVELS))]
    masks = np.concatenate([strict, incl, strict, incl] + below + [m.T for m in below], axis=1).astype(np.float32)
    return {"x_in": np.ascontiguousarray(i["x"][0]), "wstream": wstream, "gains": gains, "consts_in": consts,
            "masks_in": masks}


def kernel(**inputs):
    import concourse.bacc as bacc
    from concourse.bass_utils import run_bass_kernel_spmd
    arrays = lay_out({k: np.asarray(v) for k, v in inputs.items()})
    nc = bacc.Bacc("TRN2", target_bir_lowering=False, num_devices=1)
    args = {n: nc.dram_tensor(n, a.shape, F32, kind="ExternalInput").ap() for n, a in arrays.items()}
    scratch = nc.dram_tensor("t5_row", (16, 384), F32, kind="Internal").ap()
    out = nc.dram_tensor("out_dram", (T, D), F32, kind="ExternalOutput").ap()
    build(nc, **args, scratch=scratch, out=out)
    r = run_bass_kernel_spmd(nc, [arrays], core_ids=[0])
    return r.results[0]["out_dram"].reshape(1, T, D)
```

```python
from contextlib import ExitStack

import numpy as np

import concourse.bass as bass
from concourse import mybir

F32 = mybir.dt.float32
F32R = mybir.dt.float32r
U8 = mybir.dt.uint8
ALU = mybir.AluOpType
ACT = mybir.ActivationFunctionType
AX = mybir.AxisListType

P = 128
T, D = 256, 1024
TT, KC = T // P, D // P
F = 2816
FC = F // P
HD = 64
SLOT = 3 * 1024
RING = 4
NC_CMP, CMP_STRIDE = 15, 16
LEVELS = 7
DECAY = float(np.exp(-0.5))
NEG = -1e30
TOPK = 64

SLOTS = [("w_in", 8), ("cmp_w1", 3), ("w_out", 3), ("ffn0", FC), ("ffn1", FC), ("even_in", 8), ("even_out", 3),
         ("ffn2", FC), ("ffn3", FC), ("odd_in", 5), ("uk_uv", 2), ("odd_out", 3), ("ffn4", FC)]
BASE = {}
NSLOTS = 0
for _name, _n in SLOTS:
    BASE[_name] = NSLOTS
    NSLOTS += _n

CONSTS = [("ident", P), ("neg_half", 2 * 16),
          ("mu", 14), ("w0", 4), ("a0", 4), ("k_k", 4), ("k_a", 4), ("r_k", 4), ("lnx_w", 4), ("lnx_b", 4),
          ("gla_b", 2), ("gla_norm", 1), ("fox_b", 1), ("kv_norm", 2), ("q_scale", 4),
          ("reverse", P), ("pair_ones", P), ("ones", P), ("w2", 512), ("a2", 512), ("g2", 512), ("gate_w", KC * 24),
          ("even_small", KC * 40), ("odd_small", KC * 8), ("gla_gate", 256), ("ck2", 256), ("cv2", 128),
          ("pe_k", 16), ("pe_v", 16), ("t5", 16), ("t5_onehot", 384), ("alibi", 256), ("alibi_cmp", 2 * 16),
          ("any_ok", 2), ("causal", 256)]
COL = {}
NCONST = 0
for _name, _n in CONSTS:
    COL[_name] = (NCONST, _n)
    NCONST += _n

MASKS = 512 + 2 * LEVELS * P

IN_ITEMS = ([("col", 0), ("col", 1)] + [("col", b) for b in range(2, 6)] + [("zw", j) for j in range(4)]
            + [("za", j) for j in range(4)] + [("g", j) for j in range(4)] + [("col", b) for b in range(6, 22)]
            + [("tok", 0), ("tok", 1), ("gate", 0)])
EVEN_ITEMS = ([("small", 0)] + [("col", b) for b in range(4)] + [("gz", 0), ("gz", 1)]
              + [("col", b) for b in range(4, 16)]
              + [("tok", t, n) for n in range(3) for t in range(TT)])
ODD_ITEMS = ([("ki", 0)] + [("ckv", t) for t in range(TT)] + [("small", t) for t in range(TT)]
             + [("qi", j) for j in range(4)] + [("q", j) for j in range(8)])
UKV_ITEMS = [("kh", j) for j in range(8)] + [("vh", t, n) for t in range(TT) for n in range(2)]

FIRST = COL["reverse"][0]
RWKV_UNITS = 16
QUADS = RWKV_UNITS // 4


def build(nc, x_in, wstream, gains, consts_in, masks_in, scratch, out):
    ctx = ExitStack()
    with ctx:
        at = {}

        def sb(name, shape, dt=F32):
            at[name] = nc.sbuf_base
            return ctx.enter_context(nc.sbuf_tensor(name, shape, dt))

        def over(name, shape, under, skip=0):
            return nc.alloc_sbuf_tensor_at(name, shape, F32R, offset=at[under] + 4 * skip)

        names = ("x0_loaded x1_loaded first_loaded consts_loaded masks_loaded masks_ready gain0 gain1 land0 land1 "
                 "land2 land3 free0 free1 free2 free3 a_step v_step g_step ss_ready rstd_ready xn_ready x_done "
                 "xT_ps acc0_done gu_ps silu_ready h_mul h_hi h_ready down_done hi_a hi_b lo_a lo_b hi_blk lo_blk "
                 "small_hi small_lo gate_hi gate_lo uT_hi uT_lo rwkv_ready y_hi y_lo wo_hi wo_lo op_chunk op_acc "
                 "item_ps item_ev shift_ready lora_in raw_free kk_sq n2_ps kk_clamped kk_sqrt rk_ready bon_ps "
                 "bonus_read pads_ready eye_ready csm_ready e_ready scan_in ab_ready tok_ps tok_ev id_ready A_ps "
                 "A_read P_ps P_ev dM_ps M_ready rhs_ps rhs_ev sa_ps sa_ev y_ps s_ps y_ev s_ev var_ready "
                 "grs_ready yn_ready ynT_ps ynT_ev cmp_z cmp_h cmp_row cmp_hT cmp_hact cmp_kv cmp_ready "
                 "gates_ready gates_ps gate_tok S_ps max_ready p_ready pT_ps pT_ev0 pT_ev1 o_ps o_ready oT_ps gk_ab gk_cs "
                 "gla_k gla_ready c_ss c_rs c_n c_ps c_ev idx_ps idx_relu idx_acc sel_ready t5_ps t5_sb t5_out "
                 "t5_in stored").split()
        s = {n: ctx.enter_context(nc.semaphore(n)) for n in names}

        x = sb("x", [P, TT, D])
        xn = sb("xn", [P, TT, D])
        uT = sb("uT", [P, KC, T])
        yT = sb("yT", [P, KC, T])
        gb = sb("gb", [P, 2, D])
        ring = sb("ring", [P, RING, SLOT])
        ffb = sb("ffb", [P, 4, T])
        cst = sb("cst", [P, NCONST])
        msk = sb("msk", [P, MASKS], U8)
        small = sb("small", [P, 256])
        WK = 20480
        wk = sb("wk", [P, WK])
        ps = [ctx.enter_context(nc.psum_tensor(f"ps{i}", [P, 512], F32)) for i in range(8)]

        def C(name, lo=0, hi=None):
            o, n = COL[name]
            return cst[:, o + lo:o + (n if hi is None else hi)]

        def W(off, *shape):
            n = int(np.prod(shape))
            a = wk[:, off:off + n]
            if len(shape) == 2:
                a = a.rearrange("p (a b) -> p a b", b=shape[1])
            if len(shape) == 3:
                a = a.rearrange("p (a b c) -> p a b c", b=shape[1], c=shape[2])
            return a

        ident = C("ident")
        w_gu = over("w_gu", [P, 2, 2, 2 * D], "wk")
        w_dn = over("w_dn", [P, 2, 2, D], "wk", 8 * D)
        h_r = over("h_r", [P, 2, 2, T], "ffb")
        ring_r = over("ring_r", [P, RING, SLOT], "ring")
        w_h = {"even": [over(f"even_h{i}", [P, KC, 3 * P], "wk", o) for i, o in enumerate((17408, 9728))],
               "in": [over("in_h", [P, KC, 3 * P], "wk", 6144)] * 2,
               "odd": [over(f"odd_h{i}", [P, KC, 3 * P], "wk", o) for i, o in enumerate((4096, 9216))]}
        w_gate = [over(f"gate_w{i}", [P, KC * 24], "wk", 9216 + KC * 24 * i) for i in range(2)]
        w_small = [over(f"even_small{i}", [P, KC * 40], "wk", 14336 + KC * 40 * i) for i in range(2)]
        wo_h = [over(f"out_h{i}", [P, SLOT], "wk", o) for i, o in enumerate((13312, 12800, 12288))]
        uT_r = [over("uT_h", [P, KC, T], "uT"), over("uT_l", [P, KC, T], "yT")]
        sg = wk[:, 12 * D:12 * D + 2 * T].rearrange("p (a b) -> p a b", a=2)
        ss, rstd = small[:, 0:2], small[:, 2:4]
        den, nmax, rden = small[:, 160:176], small[:, 12:16], small[:, 16:24]

        pr, pk, pv = W(0, 4, T), W(1024, 4, T), W(2048, 4, T)
        gg, kk, kp = W(3072, 4, T), W(4096, 4, T), W(1024, 4, T)
        sgm, agm = xn[:, 0, :].rearrange("p (a b) -> p a b", b=T), xn[:, 1, :].rearrange("p (a b) -> p a b", b=T)
        ytok = W(5120, TT, 512)
        tmp = W(5120, 4, T)
        arT = W(6144, 4, TT, 2 * P)
        bT, kT_ = W(8192, 4, TT * P), W(9216, 4, TT * P)
        AA4 = [W(10240, 4, 512), W(12288, 4, 512), xn[:].rearrange("p t (u n) -> p (t u) n", n=512),
               uT[:].rearrange("p (u c) n -> p u (c n)", u=4)]
        E1, E2, E3, cs = W(10240, 4, T), W(11264, 4, T), W(12288, 4, T), W(13312, 4, T)
        Mm, Mt = W(14336, RWKV_UNITS, P), W(0, RWKV_UNITS, P)
        raw = W(14336, 4, 257)
        Pb = W(16384, 2, 512)
        csp = W(16384, 4, T)
        lora = W(17408, 2, T)
        td = W(17920, T)
        tg = W(18176, T)
        hrow = W(17408, 2, T)
        qT = W(18432, 4, T)
        ksT, kwT = W(19456, 2, T), W(19968, 2, T)
        vtok = yT[:, 0:4, :].rearrange("p (t c) n -> p t (c n)", t=2)
        bktok = yT[:, 4:8, :].rearrange("p (w c) n -> p w (c n)", w=2)
        Sst = ffb[:, 0:2, :].rearrange("p a (c n) -> p (a c) n", c=2)
        RH, SA = ffb[:, 2:4, :].rearrange("p a n -> p (a n)"), Pb[:, 0, :]
        glT = ffb[:, 3, :]

        zk = sb("zk", [P, 3, P])
        zv = sb("zv", [P, 3, P])
        vsw = sb("vsw", [P, TT, 256])
        hid = sb("hid", [P, 2, 2, 48])
        kcT = sb("kcT", [P, 2, 16])
        vc = sb("vc", [16, 2, HD])
        gtok = sb("gtok", [P, TT, 24])
        SS, Pp, PT = W(10240, 3, T), W(11008, 3, T), W(11776, 2, 2 * P)
        obr = W(12288, 512).rearrange("p (h n) -> p h n", h=8)
        onsa = W(0, TT, 512)

        block = ctx.enter_context(nc.Block())

        def mask(i, n=1):
            return msk[:, 512 + i * P:512 + (i + n) * P]

        def att_units(kind):
            units = []
            for t in range(TT):
                K, tk = P * (t + 1), slice(t * P, (t + 1) * P)
                if kind == "nsa":
                    for b in range(3):
                        for h in range(8):
                            g, slope = h // 4, 2.0 ** -(h + 1)
                            u = dict(q=qT[:, h % 4, tk], scale=slope)
                            if b == 0:
                                u.update(k=kcT[:, g, 0:NC_CMP], K=NC_CMP, v=[vc[0:NC_CMP, g, :]],
                                         dist=C("alibi_cmp", 16 * t, 16 * t + NC_CMP))
                            else:
                                kx, o = (ksT, kwT)[b - 1], (b - 1) * P + g * HD
                                u.update(k=kx[:, g, 0:K], K=K, v=[vsw[:, kt, o:o + HD] for kt in range(t + 1)],
                                         dist=C("alibi", P * (1 - t), P * (1 - t) + K))
                            units.append(u)
                if kind == "fox":
                    for h in range(8):
                        units.append(dict(q=fqT[:, h // 2, tk], k=fkT[h // 4][:, h // 2 % 2, h % 2, 0:K], K=K, scale=1.0,
                                          v=[evtok[:, kt, 512 + h * HD:512 + (h + 1) * HD] for kt in range(t + 1)],
                                          head=h, tk=tk, dist=C("causal", P * (1 - t), P * (1 - t) + K)))
                if kind == "dsa":
                    for h in range(16):
                        units.append(dict(q=oqT[:, h // 2, tk], k=khT[h % 2][:, h // 2, 0:K], K=K, scale=1.0,
                                          v=[vh[:, kt, h * HD:(h + 1) * HD] for kt in range(t + 1)],
                                          t5=bias16[:, h, P * (1 - t):P * (1 - t) + K], dist=selm[:, t, 0:K]))
            return units

        gqT, gkT = W(0, 2, T), W(512, 2, T)
        goT = W(1024, 4, T)
        fqT, fkT = W(2048, 4, T), [W(12800, 2, 2, T), W(16384, 2, 2, T)]
        evtok = W(4096, TT, 1024)
        gsm = W(6144, T)
        gz, gab, gmn, gcs = W(6400, 2, T), W(6912, 2, T), W(7424, 2, T), W(7936, 2, T)
        fz, fab, fmn, fneg = W(8448, T), W(8704, T), W(8960, T), W(9216, T)
        fsum = W(9472, T)
        gqd, gkd = W(14336, 2, T), W(14848, 2, T)
        gE1, gE2 = W(15360, 2, T), W(15872, 2, T)
        gkt = W(12288, 2, P)
        gA = W(9728, 4, P)
        gS = W(13824, 2, 256)
        ogla = W(17664, TT, 512)
        gsq = W(18688, 512)
        ofox = W(19200, 1, 1024)[:, 0, :].rearrange("p (t n) -> p t n", t=2)
        oqT = W(0, 8, T)
        khT = [W(2048, 8, T), xn[:].rearrange("p t (c n) -> p (t c) n", n=T)]
        vh = W(4096, TT, 1024)
        odsa = W(6144, TT, 1024)
        qiT = W(8192, 4, T)
        kiT = W(12288, 2, T)
        idxs = W(7168, 2, T)
        wtok = small[:, 208:224].rearrange("p (t h) -> p t h", t=2)
        selm = W(13568, 2, T)
        ckv = W(14080, 2, 256)
        cT = W(14592, 2, T)
        score = W(15104, T)
        bias16 = W(15360, 16, T)
        csc = W(7680, T)

        USED = {"in": [{"col": [it[1]], "tok": [22, 23] if it[1] else []}.get(it[0], []) for it in IN_ITEMS],
                "even": [[] for _ in EVEN_ITEMS], "odd": [[] for _ in ODD_ITEMS]}
        LOOK = {"in": 3, "even": 6, "odd": 6}
        for n, it in enumerate(EVEN_ITEMS):
            if it[0] == "col":
                USED["even"][n] = [it[1]]
            if it[0] == "tok" and it[1] == 1:
                USED["even"][n] = [[16, 17], [18, 19, 20], [21, 22, 23]][it[2]]
        for n, it in enumerate(ODD_ITEMS):
            USED["odd"][n] = {"ki": [0], "ckv": [1, 2] if it[1] else [], "qi": [3 + it[1]], "q": [7 + it[1]]}.get(it[0], [])
        BLOCKS = {k: sum(len(b) for b in u) for k, u in USED.items()}
        PB = {"in": 0, "even": BLOCKS["in"], "odd": BLOCKS["in"] + BLOCKS["even"]}

        UN = {k: att_units(k) for k in ("nsa", "fox", "dsa")}
        UB = {"nsa": 0, "fox": len(UN["nsa"]), "dsa": len(UN["nsa"]) + len(UN["fox"])}
        IB, n = {}, 0
        for k, items in (("in", IN_ITEMS), ("even", EVEN_ITEMS), ("odd", ODD_ITEMS), ("ukv", UKV_ITEMS)):
            IB[k] = n
            n += len(items)
        PIECES = [[(0, 1, 3, 7), None, (1, 1, 6, 4)], [(0, 1, 7, 7), None, (1, 1, 8, 4)],
                  [(0, 0, 9, 7), (0, 1, 10, 7), (1, 0, 11, 7), (1, 1, 12, 4)]]
        Y0, YT0 = [0, 3, 6], [0, 2, 4]
        MIX = [(onsa, 4), (ofox, 4), (odsa, 0)]
        TN = {n: i for i, n in enumerate([0, 1, 3, 4, 5, 6, 7, 8])}
        SPLIT_OF = TN
        PROJ_OF = {0: "in", 4: "even", 7: "odd"}
        FFN_OF = {1: 0, 3: 1, 5: 2, 6: 3, 8: 4}
        AHEAD = {1: 1, 2: 3, 4: 4, 5: 5, 6: 6, 8: 8}
        kind_slot = {"in": "w_in", "even": "even_in", "odd": "odd_in"}.get
        LOOPS = (FC - 6) // 4

        @block.sync
        def _(sp):
            for t in range(TT):
                sp.dma_start(x[:, t, :], x_in[t * P:(t + 1) * P, :]).then_inc(s[f"x{t}_loaded"], 16)
            for i in range(RING):
                sp.dma_start(ring[:, i, :], wstream[i]).then_inc(s[f"land{i}"], 16)
                if i == 1:
                    sp.dma_start(cst[:, FIRST:NCONST], consts_in[:, FIRST:NCONST]).then_inc(s["consts_loaded"], 16)
            sp.dma_start(W(10240, MASKS), masks_in).then_inc(s["masks_loaded"], 16)
            sp.dma_start(gb[:, 1, :], gains[:, D:2 * D]).then_inc(s["gain1"], 16)
            rounds = (NSLOTS - RING) // RING
            with sp.Fori(0, rounds) as r:
                for j in range(RING):
                    sp.wait_ge(s[f"free{j}"], r + 1)
                    sp.dma_start(ring[:, j, :],
                                 wstream[bass.ds(r * RING + (RING + j), 1)].rearrange("a p n -> p (a n)")
                                 ).then_inc(s[f"land{j}"], 16)
            for i in range(RING * (rounds + 1), NSLOTS):
                sp.wait_ge(s[f"free{i % RING}"], i // RING)
                sp.dma_start(ring[:, i % RING, :], wstream[i]).then_inc(s[f"land{i % RING}"], 16)
            for t in range(TT):
                sp.wait_ge(s["xn_ready"], 4 * 9 + 2 * t + 2)
                sp.dma_start(out[t * P:(t + 1) * P, :], x[:, t, :]).then_inc(s["stored"], 16)
            sp.wait_ge(s["stored"], 16 * TT)

        def slot(i):
            return ring[:, i % RING, :]

        @block.tensor
        def _(pe):
            def land(i):
                pe.wait_ge(s[f"land{i % RING}"], 16 * (i // RING + 1))

            def mm(o, l, r, start=True, stop=True):
                return pe.matmul(o, l, r, start=start, stop=stop, skip_group_check=True)

            def norm_T(n):
                k = TN[n]
                for t in range(TT):
                    for half in range(2):
                        pe.wait_ge(s["xn_ready"], 4 * n + 2 * t + half + 1)
                        for c in range(4):
                            last = pe.transpose(ps[4 + 2 * t + half][:, c * P:(c + 1) * P],
                                                xn[:, t, (4 * half + c) * P:(4 * half + c + 1) * P], ident)
                        last.then_inc(s["xT_ps"], 1)
                pe.wait_ge(s["uT_lo"], 4 * (SPLIT_OF[n] + 1))

            PASSES = [(0, 0), (1, 0), (0, 1)]

            def gate_up(j):
                for m in range(2):
                    for k in range(KC):
                        for n, (a, b) in enumerate(PASSES):
                            w = w_gu[:, j % 2, a, (m * KC + k) * P:(m * KC + k + 1) * P]
                            last = mm(ps[4 + j % 2][:, m * T:(m + 1) * T], w, uT_r[b][:, k, :],
                                      k == 0 and n == 0, k == KC - 1 and n == 2)
                last.then_inc(s["gu_ps"], 1)

            def down(j, start, stop):
                for t in range(TT):
                    for half in range(2):
                        for n, (a, b) in enumerate(PASSES):
                            last = mm(ps[2 * t + half][:, :], h_r[:, j % 2, a, t * P:(t + 1) * P],
                                      w_dn[:, j % 2, b, half * 512:(half + 1) * 512],
                                      start and n == 0, stop and n == 2)
                    if stop and t == 0:
                        last.then_inc(s["acc0_done"], 1)
                last.then_inc(s["down_done"], 1)

            def ffn(f):
                q = FC * f

                def step(c, r=0):
                    pe.wait_ge(s["lo_a"], r + (q + c + 1))
                    if q + c >= 2:
                        pe.wait_ge(s["h_ready"], r + (q + c - 1))
                    gate_up(c)
                    if c:
                        pe.wait_ge(s["lo_b"], r + (q + c))
                        pe.wait_ge(s["h_ready"], r + (q + c))
                        down(c - 1, c == 1, False)
                step(0)
                step(1)
                with pe.Fori(0, 4 * LOOPS, 4) as r:
                    for j in range(4):
                        step(2 + j, r)
                for c in range(2 + 4 * LOOPS, FC):
                    step(c)
                pe.wait_ge(s["lo_b"], q + FC)
                pe.wait_ge(s["h_ready"], q + FC)
                down(FC - 1, False, True)

            def piece(o, j):
                t, half, ready, bank = PIECES[o][j]
                src, c0 = MIX[o]
                pe.wait_ge(s["o_ready"], ready)
                if o < 2 and j == 0:
                    pe.wait_ge(s[("ynT_ev", "gla_ready")[o]], 2)
                if o == 2 and 0 < j < 3:
                    pe.wait_ge(s["y_lo"], Y0[o] + j)
                for c in range(4):
                    k = 4 * half - c0 + c
                    last = pe.transpose(ps[bank][:, c * P:(c + 1) * P], src[:, t, k * P:(k + 1) * P], ident)
                last.then_inc(s["oT_ps"], 1)

            def out_proj(o, b):
                def free_slot(i):
                    pe.wait_ge(s["op_chunk"], KC * o + min(3 * i + 3, KC))
                    pe.sem_inc(s[f"free{(b + i) % RING}"], 1)
                n = len(PIECES[o])
                if o == 2:
                    piece(o, 2)
                for c in range(KC):
                    if c == 2:
                        piece(o, n - 1)
                    if c in (0, 4):
                        pe.wait_ge(s["y_lo"], Y0[o] + (n if c else n - 1))
                    pe.wait_ge(s["wo_lo"], KC * o + c + 1)
                    f = c % 3 * D
                    for t in range(TT):
                        for half in range(2):
                            for m, (a, p) in enumerate(PASSES):
                                w = (wo_h[o][:, f + half * 512:f + (half + 1) * 512],
                                     ring_r[:, (b + c // 3) % RING, f + half * 512:f + (half + 1) * 512])[p]
                                last = mm(ps[2 * t + half][:, :], uT_r[a][:, c, t * P:(t + 1) * P], w,
                                          c == 0 and m == 0, c == KC - 1 and m == 2)
                        if c == KC - 1 and t == 0:
                            last.then_inc(s["op_acc"], 1)
                    last.then_inc(s["op_chunk"], 1)
                    if c in (3, 6):
                        free_slot(c // 3 - 1)
                free_slot(2)
                pe.sem_inc(s["op_acc"], 1)

            def item(q):
                if q >= 4:
                    pe.wait_ge(s["item_ev"], q - 3)
                return ps[4 + q % 4]

            def parts(kind, blk):
                pe.wait_ge(s["lo_blk"], PB[kind] + blk + 1)
                i = (BASE[kind_slot(kind)] + blk // 3) % RING
                return w_h[kind][blk // 3 % 2], ring_r[:, i, :].rearrange("p (k f) -> p k f", k=KC)

            def col_split(kind, bank, blk):
                w, f = parts(kind, blk), blk % 3 * P
                for k in range(KC):
                    for n, (a, b) in enumerate(PASSES):
                        last = mm(bank[:, 0:T], w[a][:, k, f:f + P], uT_r[b][:, k, :],
                                  k == 0 and n == 0, k == KC - 1 and n == 2)
                return last

            def tok_split(kind, bank, blk, t, lo, hi):
                w = parts(kind, blk)
                for k in range(KC):
                    for n, (a, b) in enumerate(PASSES):
                        last = mm(bank[:, 0:hi - lo], uT_r[b][:, k, t * P:(t + 1) * P], w[a][:, k, lo:hi],
                                  k == 0 and n == 0, k == KC - 1 and n == 2)
                return last

            def freed(n, i):
                pe.wait_ge(s["item_ps"], n)
                pe.sem_inc(s[f"free{i % RING}"], 1)

            def w_in():
                b = BASE["w_in"]
                for n, it in enumerate(IN_ITEMS):
                    q = IB["in"] + n
                    bank = item(q)
                    if it[0] == "col":
                        last = col_split("in", bank, it[1])
                    elif it[0] in ("zw", "za", "g"):
                        if it == ("zw", 0):
                            pe.wait_ge(s["consts_loaded"], 16)
                            pe.wait_ge(s["lora_in"], 3)
                        src = {"zw": "w2", "za": "a2", "g": "g2"}[it[0]]
                        last = mm(bank[:, 0:T], C(src, it[1] * P, (it[1] + 1) * P), tg if it[0] == "g" else td)
                    elif it[0] == "tok":
                        last = tok_split("in", bank, 23, it[1], P, 3 * P)
                    else:
                        pe.wait_ge(s["gate_lo"], 1)
                        for k in range(KC):
                            for m, (a, p) in enumerate(PASSES):
                                last = mm(bank[0:24, 0:T], w_gate[a][:, 24 * k:24 * k + 24], uT_r[p][:, k, :],
                                          k == 0 and m == 0, k == KC - 1 and m == 2)
                    last.then_inc(s["item_ps"], 1)
                    if (it[0] == "col" and it[1] % 3 == 2) or it == ("tok", 1):
                        freed(q + 1, b + 7 if it[0] == "tok" else b + it[1] // 3)
                    if it == ("g", 3):
                        pe.wait_ge(s["kk_sq"], 1)
                        for c in range(4):
                            last = mm(ps[c // 2][:, (c % 2) * T:(c % 2 + 1) * T], C("pair_ones"), tmp[:, c, :])
                        last.then_inc(s["n2_ps"], 1)
                    if it == ("col", 14):
                        pe.wait_ge(s["rk_ready"], 1)
                        for c in range(4):
                            last = mm(ps[2 + c // 2][:, (c % 2) * T:(c % 2 + 1) * T], C("pair_ones"), tmp[:, c, :])
                        last.then_inc(s["bon_ps"], 1)

            def rwkv_tok():
                pe.wait_ge(s["shift_ready"], 14)
                pe.wait_ge(s["item_ev"], IB["in"] + len(IN_ITEMS))
                srcs = [(pv, t) for t in range(TT)] + [(bT, 0), (kT_, 0)]
                for n, (src, t) in enumerate(srcs):
                    if n == 2:
                        pe.wait_ge(s["ab_ready"], 1)
                    for c in range(4):
                        last = pe.transpose(ps[(0, 1, 6, 7)[n]][:, c * P:(c + 1) * P], src[:, c, t * P:(t + 1) * P],
                                            ident)
                    last.then_inc(s["tok_ps"], 1)

            def rwkv():
                pe.wait_ge(s["bonus_read"], 1)
                pe.wait_ge(s["tok_ev"], 4)
                pe.wait_ge(s["cmp_row"], 2)
                for u in range(RWKV_UNITS):
                    t, c, r, k = u // 8, u % 8 // 2, HD * (u % 2), u // 4
                    if u >= 4:
                        pe.wait_ge(s["A_read"], u - 3)
                    if u % 4 == 0 and k >= 2:
                        pe.wait_ge(s["M_ready"], k - 1)
                    bank = ps[u % 4]
                    ar = arT[r:r + HD, c, t, :]
                    tk = slice(t * P, (t + 1) * P)
                    mm(ps[4 + 2 * (k % 2) + u % 2][:, (u % 4) // 2 * P:((u % 4) // 2 + 1) * P],
                       arT[r:r + HD, c, t, 0:P], bT[r:r + HD, c, tk])
                    mm(bank[:, 0:256], bT[r:r + HD, c, tk], ar)
                    mm(bank[:, 256:512], kT_[r:r + HD, c, tk], ar).then_inc(s["A_ps"], 1)
                pe.wait_ge(s["A_read"], RWKV_UNITS)
                n = (LEVELS - 1) * QUADS
                for q in range(n + 1):
                    if q == 2:
                        compress_T()
                    if q == 8:
                        compress_out()
                    if q < n:
                        k = q % QUADS
                        pe.wait_ge(s["M_ready"], q + 1)
                        for j in range(4):
                            last = mm(ps[q % 2][:, j * P:(j + 1) * P], AA4[k][:, j, 0:P], Mm[:, 4 * k + j, :])
                        last.then_inc(s["P_ps"], 1)
                    if q:
                        p = q - 1
                        k = p % QUADS
                        pe.wait_ge(s["P_ev"], p + 1)
                        pe.wait_ge(s["M_ready"], max(p + 3, QUADS))
                        for j in range(4):
                            pu = Pb[:, p % 2, j * P:(j + 1) * P]
                            last = mm(ps[4 + p % 2][:, j * P:(j + 1) * P], pu, Mt[:, 4 * k + j, :])
                            if p // QUADS < LEVELS - 2:
                                last = mm(ps[2 + p % 2][:, j * P:(j + 1) * P], Mt[:, 4 * k + j, :], pu)
                        last.then_inc(s["dM_ps"], 1)
                pe.wait_ge(s["M_ready"], LEVELS * QUADS)
                pe.wait_ge(s["gate_tok"], 2)
                for t in range(TT):
                    if t:
                        pe.wait_ge(s["s_ev"], 1)
                        pe.wait_ge(s["y_ev"], 1)
                    for c in range(4):
                        o = ps[6][:, c * P:(c + 1) * P]
                        if t:
                            mm(o, arT[:, c, 1, 0:P], Sst[:, c, :], True, False)
                        for h in (2 * c, 2 * c + 1):
                            last = mm(o[:, h % 2 * HD:(h % 2 + 1) * HD], AA4[2 * t + h // 4][:, h % 4, 256:384],
                                      vtok[:, t, h * HD:(h + 1) * HD], not t, True)
                    last.then_inc(s["rhs_ps"], 1)
                    pe.wait_ge(s["rhs_ev"], t + 1)
                    for h in range(8):
                        last = mm(ps[7][:, h * HD:(h + 1) * HD], Mt[:, 8 * t + h, :], RH[:, h * HD:(h + 1) * HD])
                    last.then_inc(s["sa_ps"], 1)
                    pe.wait_ge(s["sa_ev"], t + 1)
                    if not t:
                        for c in range(4):
                            o = ps[4][:, c * P:(c + 1) * P]
                            mm(o, bktok[:, 0, c * P:(c + 1) * P], SA[:, c * P:(c + 1) * P], True, False)
                            last = mm(o, bktok[:, 1, c * P:(c + 1) * P], vtok[:, 0, c * P:(c + 1) * P], False, True)
                        last.then_inc(s["s_ps"], 1)
                    for c in range(4):
                        o = ps[5][:, c * P:(c + 1) * P]
                        if t:
                            mm(o, arT[:, c, 1, P:2 * P], Sst[:, c, :], True, False)
                        for h in (2 * c, 2 * c + 1):
                            A, oh, hs = AA4[2 * t + h // 4], o[:, h % 2 * HD:(h % 2 + 1) * HD], slice(h * HD, (h + 1) * HD)
                            mm(oh, A[:, h % 4, 128:256], SA[:, hs], not t, False)
                            last = mm(oh, A[:, h % 4, 384:512], vtok[:, t, hs], False, True)
                    last.then_inc(s["y_ps"], 1)
                pe.wait_ge(s["y_ev"], 2)

            def rwkv_T(t):
                pe.wait_ge(s["yn_ready"], t + 1)
                if t:
                    pe.wait_ge(s["ynT_ev"], 1)
                for c in range(4):
                    last = pe.transpose(ps[7][:, c * P:(c + 1) * P], ytok[:, t, c * P:(c + 1) * P], ident)
                last.then_inc(s["ynT_ps"], 1)

            def gla_T(t):
                pe.wait_ge(s["yn_ready"], 2 + t + 1)
                if t:
                    pe.wait_ge(s["gla_ready"], 1)
                for c in range(4):
                    last = pe.transpose(ps[7][:, c * P:(c + 1) * P], ogla[:, t, c * P:(c + 1) * P], ident)
                last.then_inc(s["ynT_ps"], 1)

            def compress():
                b = BASE["cmp_w1"]
                pe.wait_ge(s["cmp_z"], 2)
                pe.wait_ge(s["item_ev"], IB["in"] + len(IN_ITEMS))
                for n in range(2):
                    for m in range(16):
                        piece = 16 * n + m
                        i = b + piece // 12
                        if m == 0 or piece % 12 == 0:
                            land(i)
                        last = mm(ps[4 + n][0:47, 0:256], (zk, zv)[n][:].rearrange("p a n -> p (a n)")[:, m:m + 8 * 46 + 1:8],
                                  slot(i)[:, (piece % 12) * 256:(piece % 12 + 1) * 256], m == 0, m == 15)
                    last.then_inc(s["cmp_h"], 1)
                pe.wait_ge(s["cmp_h"], 2)
                for i in range(3):
                    pe.sem_inc(s[f"free{(b + i) % RING}"], 1)

            def compress_T():
                for n in range(2):
                    for half in range(2):
                        last = pe.transpose(ps[6 + n][:, half * 48:half * 48 + 47],
                                            hrow[0:47, n, half * P:(half + 1) * P], ident[0:47, 0:47])
                last.then_inc(s["cmp_hT"], 1)

            def compress_out():
                pe.wait_ge(s["cmp_hact"], 1)
                for half in range(2):
                    mm(ps[6][:, 0:30], C("ck2", half * P, (half + 1) * P), hid[:, 0, half, 0:30], half == 0, half == 1)
                for g in range(2):
                    for half in range(2):
                        last = mm(ps[6][0:NC_CMP, 64 + g * HD:64 + (g + 1) * HD],
                                  hid[:, 1, half, 15 * g:15 * g + 15], C("cv2", half * HD, (half + 1) * HD),
                                  half == 0, half == 1)
                last.then_inc(s["cmp_kv"], 1)
                pe.wait_ge(s["gates_ready"], 1)
                for t in range(TT):
                    last = pe.transpose(ps[7][:, t * 24:(t + 1) * 24], glT[0:24, t * P:(t + 1) * P], ident[0:24, 0:24])
                last.then_inc(s["gates_ps"], 1)

            def attention(kind, go, value, beside={}):
                units, b = UN[kind], UB[kind]
                n = len(units)
                if kind == "dsa":
                    pe.wait_ge(s["t5_in"], 16)
                pe.wait_ge(s[go], value)
                for i in range(n + 3):
                    if i in beside:
                        beside[i]()
                    if i < n:
                        u, a = b + i, units[i]
                        if u >= 3:
                            pe.wait_ge(s["max_ready"], u - 2)
                        o = ps[u % 3][:, 0:a["K"]]
                        if "head" in a:
                            h = a["head"]
                            mm(o, ident[0:8, h:h + 1].to_broadcast([8, P]), fneg[0:8, 0:a["K"]], True, False)
                            mm(o, fsum[0:8, a["tk"]], ident[0:8, h:h + 1].to_broadcast([8, a["K"]]), False, False)
                        if "t5" in a:
                            mm(o, C("reverse"), a["t5"], True, False)
                        mm(o, a["q"], a["k"], kind == "nsa", True).then_inc(s["S_ps"], 1)
                    if 2 <= i < n + 2:
                        u, a = b + i - 2, units[i - 2]
                        pe.wait_ge(s["p_ready"], u + 1)
                        if u >= 2:
                            pe.wait_ge(s[f"pT_ev{u % 2}"], u // 2)
                        for k in range(0, a["K"], P):
                            w = min(P, a["K"] - k)
                            last = pe.transpose(ps[3 + u % 2][0:w, k:k + P], Pp[:, u % 3, k:k + w], ident)
                        last.then_inc(s["pT_ps"], 1)
                    if i >= 3:
                        u, a = b + i - 3, units[i - 3]
                        pe.wait_ge(s[f"pT_ev{u % 2}"], u // 2 + 1)
                        if u % 8 == 0 and u >= 16:
                            pe.wait_ge(s["o_ready"], u // 8 - 1)
                        for k in range(0, a["K"], P):
                            w = min(P, a["K"] - k)
                            last = mm(ps[5 + u // 8 % 2][:, u % 8 * HD:(u % 8 + 1) * HD], PT[0:w, u % 2, k:k + P], a["v"][k // P],
                                      k == 0, k + P >= a["K"])
                        last.then_inc(s["o_ps"], 1)

            def even_in():
                b = BASE["even_in"]
                for n, it in enumerate(EVEN_ITEMS):
                    q = IB["even"] + n
                    bank = item(q)
                    if it[0] == "small":
                        pe.wait_ge(s["small_lo"], 1)
                        for k in range(KC):
                            for m, (a, b_) in enumerate(PASSES):
                                last = mm(bank[0:40, 0:T], w_small[a][:, 40 * k:40 * k + 40], uT_r[b_][:, k, :],
                                          k == 0 and m == 0, k == KC - 1 and m == 2)
                    elif it[0] == "gz":
                        if it[1] == 0:
                            pe.wait_ge(s["item_ev"], IB["even"] + 1)
                        last = mm(bank[:, 0:T], C("gla_gate", it[1] * P, (it[1] + 1) * P)[0:16, :], gsm[0:16, :])
                    elif it[0] == "col":
                        last = col_split("even", bank, it[1])
                    else:
                        _, t, w = it
                        last = tok_split("even", bank, 17 + 3 * w, t, 0 if w else P, 3 * P)
                    last.then_inc(s["item_ps"], 1)
                    if (it[0] == "col" and it[1] % 3 == 2) or (it[0] == "tok" and it[1] == 1):
                        freed(q + 1, b + 5 + it[2] if it[0] == "tok" else b + it[1] // 3)

            def gla():
                pe.wait_ge(s["gla_k"], 1)
                pe.wait_ge(s["item_ev"], IB["even"] + len(EVEN_ITEMS))
                for c in range(2):
                    last = pe.transpose(ps[2][:, c * P:(c + 1) * P], gkd[:, c, 0:P], ident)
                last.then_inc(s["tok_ps"], 1)
                for t in range(TT):
                    tk = slice(t * P, (t + 1) * P)
                    if t:
                        pe.wait_ge(s["A_read"], RWKV_UNITS + 1)
                    for h in range(4):
                        c, r = h // 2, HD * (h % 2)
                        last = mm(ps[4 + h % 2][:, c * P:(c + 1) * P], gkd[r:r + HD, c, tk], gqd[r:r + HD, c, tk])
                    last.then_inc(s["A_ps"], 1)
                    pe.wait_ge(s["A_read"], RWKV_UNITS + t + 1)
                    if t:
                        pe.wait_ge(s["s_ev"], 2)
                        pe.wait_ge(s["y_ev"], 3)
                    for h in range(4):
                        o = ps[1][:, h * P:(h + 1) * P]
                        if t:
                            r = HD * (h % 2)
                            mm(o, gqd[:, h // 2, tk], gS[:, h // 2, (h % 2) * P:(h % 2 + 1) * P], True, False)
                        last = mm(o, gA[:, h, :], evtok[:, t, h * P:(h + 1) * P], not t, True)
                    last.then_inc(s["y_ps"], 1)
                    if not t:
                        pe.wait_ge(s["tok_ev"], 5)
                        for c in range(2):
                            last = mm(ps[6][:, c * 256:(c + 1) * 256], gkt[:, c, :],
                                      evtok[:, 0, c * 256:(c + 1) * 256])
                        last.then_inc(s["s_ps"], 1)

            def odd_in():
                b = BASE["odd_in"]
                for n, it in enumerate(ODD_ITEMS):
                    q = IB["odd"] + n
                    bank = item(q)
                    if it[0] == "ki":
                        last = col_split("odd", bank, 0)
                    elif it[0] in ("qi", "q"):
                        blk = it[1] + (4 if it[0] == "q" else 0)
                        last = col_split("odd", bank, 3 + blk)
                    elif it[0] == "ckv":
                        last = tok_split("odd", bank, 2, it[1], P, 3 * P)
                    else:
                        w = C("odd_small").rearrange("p (k n) -> p k n", k=KC)
                        for k in range(KC):
                            for part in range(2):
                                last = mm(bank[:, 0:8], uT_r[part][:, k, it[1] * P:(it[1] + 1) * P].bitcast(F32),
                                          w[:, k, :], k == 0 and not part, k == KC - 1 and part == 1)
                    last.then_inc(s["item_ps"], 1)
                    if it == ("ckv", 1):
                        freed(q + 1, b)
                    if it[0] in ("qi", "q") and blk % 3 == 2:
                        freed(q + 1, b + 1 + blk // 3)
                    if it == ("qi", 3):
                        pe.wait_ge(s["c_n"], 1)
                        for c in range(2):
                            for t in range(TT):
                                last = pe.transpose(ps[3][:, c * T + t * P:c * T + (t + 1) * P],
                                                    ckv[:, t, c * P:(c + 1) * P], ident)
                        last.then_inc(s["c_ps"], 1)
                    if it[0] == "q":
                        for m in (2 * it[1], 2 * it[1] + 1):
                            t, h = m // 8, m % 8
                            if m >= 2:
                                pe.wait_ge(s["idx_relu"], m - 1)
                            if m == 0:
                                pe.wait_ge(s["item_ev"], q)
                            mm(ps[m % 2][:, 0:P * (t + 1)], qiT[:, h // 2, t * P:(t + 1) * P],
                               kiT[:, h % 2, 0:P * (t + 1)]).then_inc(s["idx_ps"], 1)
                pe.wait_ge(s["c_ev"], 1)
                b = BASE["uk_uv"]
                for n, it in enumerate(UKV_ITEMS):
                    q = IB["ukv"] + n
                    bank = item(q)
                    if it[0] == "kh":
                        if it[1] == 0:
                            land(b)
                        w = slot(b).rearrange("p (c n) -> p c n", c=3)
                        for c in range(2):
                            last = mm(bank[:, 0:T], w[:, c, it[1] * P:(it[1] + 1) * P], cT[:, c, :], c == 0, c == 1)
                    else:
                        _, t, half = it
                        if t == 0 and half == 0:
                            land(b + 1)
                        w = slot(b + 1).rearrange("p (c n) -> p c n", c=3)
                        for c in range(2):
                            last = mm(bank[:, :], cT[:, c, t * P:(t + 1) * P], w[:, c, half * 512:(half + 1) * 512],
                                      c == 0, c == 1)
                    last.then_inc(s["item_ps"], 1)
                    if it == ("kh", 7) or it == ("vh", 1, 1):
                        freed(q + 1, b if it[0] == "kh" else b + 1)

            pe.wait_ge(s["first_loaded"], 16)
            norm_T(0)
            w_in()
            compress()
            rwkv_tok()
            rwkv()
            attention("nsa", "cmp_ready", 2, {6: lambda: rwkv_T(0), 18: lambda: rwkv_T(1), 32: lambda: piece(0, 0)})
            out_proj(0, BASE["w_out"])
            norm_T(1)
            ffn(0)
            norm_T(3)
            ffn(1)
            norm_T(4)
            mm(ps[7][0:16, 0:384], C("t5")[0:32, :], C("t5_onehot")[0:32, :]).then_inc(s["t5_ps"], 1)
            pe.wait_ge(s["t5_sb"], 1)
            even_in()
            gla()
            attention("fox", "y_ev", 4, {6: lambda: gla_T(0), 9: lambda: gla_T(1), 14: lambda: piece(1, 0)})
            out_proj(1, BASE["even_out"])
            norm_T(5)
            ffn(2)
            norm_T(6)
            ffn(3)
            norm_T(7)
            odd_in()
            attention("dsa", "item_ev", IB["ukv"] + len(UKV_ITEMS), {16: lambda: piece(2, 0), 24: lambda: piece(2, 1)})
            out_proj(2, BASE["odd_out"])
            norm_T(8)
            ffn(4)

        @block.scalar
        def _(act):
            cnt = {}

            def A(ins, name="a_step", n=1):
                cnt[name] = cnt.get(name, 0) + n
                ins.then_inc(s[name], n)
                act.wait_ge(s[name], cnt[name])

            def gain(n):
                if n >= 2:
                    act.wait_ge(s["xn_ready"], 4 * (n - 1))
                act.dma_start(gb[:, n % 2, :], gains[:, n * D:(n + 1) * D]).then_inc(s[f"gain{n % 2}"], 16)

            def norm(n):
                if n in AHEAD:
                    if AHEAD[n] == 4:
                        hi_block("even", 0)
                    else:
                        hi_a(FFN_OF[AHEAD[n]], 0)
                for t in range(TT):
                    if n:
                        act.wait_ge(s["x_done"], 2 * (n - 1) + t + 1)
                    else:
                        act.wait_ge(s[f"x{t}_loaded"], 16)
                    A(act.activation(xn[:, t, :], x[:, t, :], ACT.Square, scale=D ** -0.5, accum_out=ss[:, t:t + 1]),
                      "ss_ready")
                if 1 <= n <= 8:
                    gain(n + 1)
                if n in SPLIT_OF:
                    k = TN[n]
                    if n in (0, 7):
                        hi_block(PROJ_OF[n], 0)
                    for i in range(4):
                        act.wait_ge(s["xT_ps"], 4 * k + i + 1)
                        c0, t = 4 * (i % 2), i // 2
                        act.copy(uT_r[0][:, c0:c0 + 4, t * P:(t + 1) * P],
                                 ps[4 + i][:, :].rearrange("p (c n) -> p c n", c=4)).then_inc(s["uT_hi"], 1)
                if n == 4:
                    act.copy(w_small[0][:, :], C("even_small")).then_inc(s["small_hi"], 1)
                if n in PROJ_OF:
                    for blk in range(1, LOOK[PROJ_OF[n]]):
                        hi_block(PROJ_OF[n], blk)

            def hi_block(kind, blk):
                i = BASE[kind_slot(kind)] + blk // 3
                act.wait_ge(s[f"land{i % RING}"], 16 * (i // RING + 1))
                f = blk % 3 * P
                act.copy(w_h[kind][blk // 3 % 2][:, :, f:f + P],
                         slot(i).rearrange("p (k f) -> p k f", k=KC)[:, :, f:f + P]).then_inc(s["hi_blk"], 1)

            def hi_after(kind, n):
                for blk in USED[kind][n]:
                    if blk + LOOK[kind] < BLOCKS[kind]:
                        hi_block(kind, blk + LOOK[kind])

            def hi_a(f, c, r=0, rr=0):
                q, i = FC * f, BASE[f"ffn{f}"] + c
                act.wait_ge(s[f"land{i % RING}"], rr + 16 * (i // RING + 1))
                if q + c >= 2:
                    act.wait_ge(s["gu_ps"], r + (q + c - 1))
                act.copy(w_gu[:, c % 2, 0, :], slot(i)[:, 0:2 * D]).then_inc(s["hi_a"], 1)

            def hi_b(f, c, r=0):
                q, i = FC * f, BASE[f"ffn{f}"] + c
                if q + c >= 2:
                    act.wait_ge(s["down_done"], r + (q + c - 1))
                act.copy(w_dn[:, c % 2, 0, :], slot(i)[:, 2 * D:3 * D]).then_inc(s["hi_b"], 1)

            def ffn(f):
                q = FC * f

                def step(c, r=0, rr=0):
                    act.wait_ge(s["gu_ps"], r + (q + c + 1))
                    if q + c >= 2:
                        act.wait_ge(s["h_ready"], r + (q + c - 1))
                    act.activation(sg[:, c % 2, :], ps[4 + c % 2][:, 0:T], ACT.Silu).then_inc(s["silu_ready"], 1)
                    if c + 2 < FC:
                        hi_a(f, c + 2, r, rr)
                    if c + 1 < FC:
                        hi_b(f, c + 1, r)
                hi_b(f, 0)
                hi_a(f, 1)
                step(0)
                step(1)
                with act.Fori(0, 4 * LOOPS, 4) as r:
                    for j in range(4):
                        step(2 + j, r, r * 4)
                for c in range(2 + 4 * LOOPS, FC):
                    step(c)

            def w_in():
                for n, it in enumerate(IN_ITEMS):
                    q = IB["in"] + n
                    act.wait_ge(s["item_ps"], q + 1)
                    bank = ps[4 + q % 4][:, 0:T]
                    name, j = it
                    if name == "col" and j < 14:
                        if j >= 4:
                            act.wait_ge(s["raw_free"], j - 3)
                        A(act.copy(raw[:, j % 4, 1:257], bank), "item_ev")
                        if j == 5:
                            act.wait_ge(s["consts_loaded"], 16)
                            act.copy(w_gate[0][:, :], C("gate_w")).then_inc(s["gate_hi"], 1)
                        if j == 1:
                            act.wait_ge(s["shift_ready"], 2)
                            A(act.activation(td[0:64, :], lora[0:64, 0, :], ACT.Tanh), "lora_in")
                            A(act.copy(td[64:128, :], lora[64:128, 0, :]), "lora_in")
                            A(act.activation(tg, lora[:, 1, :], ACT.Sigmoid), "lora_in")
                    elif name == "zw":
                        A(act.activation(sgm[:, j, :], bank, ACT.Sigmoid, bias=C("w0", j, j + 1)), "item_ev")
                    elif name == "za":
                        A(act.activation(agm[:, j, :], bank, ACT.Sigmoid, bias=C("a0", j, j + 1)), "item_ev")
                    elif name == "g":
                        A(act.copy(gg[:, j, :], bank), "item_ev")
                    elif name == "col" and j < 18:
                        A(act.mul(qT[:, j - 14, :], bank, C("q_scale", j - 14, j - 13)), "item_ev")
                    elif name == "col" and j in (18, 19):
                        z = (zk, zv)[j - 18]
                        for g in range(2):
                            for par in range(2):
                                ins = act.copy(z[par * HD:(par + 1) * HD, g, :], bank[g * HD:(g + 1) * HD, par:T:2])
                                A(ins, "item_ev" if (g, par) == (1, 1) else "a_step")
                        act.copy(z[:, 2, 0:16], C(("pe_k", "pe_v")[j - 18])).then_inc(s["cmp_z"], 1)
                    elif name == "col" and j in (20, 21):
                        for g in range(2):
                            r = slice(g * HD, (g + 1) * HD)
                            A(act.copy((ksT, kwT)[j - 20][r, g, :], bank[r, :]), "item_ev" if g else "a_step")
                    elif name == "tok":
                        A(act.copy(vsw[:, j, :], bank), "item_ev")
                    else:
                        A(act.copy(glT[0:24, :], bank[0:24, :]), "item_ev")
                    if it == ("col", 7):
                        act.wait_ge(s["kk_clamped"], 1)
                        A(act.activation(tmp, tmp, ACT.Sqrt), "kk_sqrt")
                    hi_after("in", n)
                    if name == "col" and 14 <= j < 18:
                        if j == 14:
                            act.wait_ge(s["csm_ready"], 1)
                            act.wait_ge(s["masks_ready"], 1)
                            act.wait_ge(s["pads_ready"], 3)
                        decays(j - 14)
                A(act.activation(glT[0:24, :], glT[0:24, :], ACT.Sigmoid), "gates_ready")

            def decays(c):
                for t in range(TT):
                    tk = slice(t * P, (t + 1) * P)
                    i = 2 * c + t
                    for o, src, sc, b0 in ((E1, cs, -DECAY, 32), (E2, cs, DECAY, 40), (E3, csp, -DECAY, 32)):
                        act.activation(o[:, c, tk], src[:, c, tk], ACT.Exp, scale=sc,
                                       bias=small[:, b0 + i:b0 + i + 1]).then_inc(s["e_ready"], 1)
                if c == 3:
                    act.activation(small[:, 48:52], small[:, 52:56], ACT.Exp, scale=-DECAY).then_inc(s["e_ready"], 1)

            def rwkv():
                dsts = [vtok[:, 0, :], vtok[:, 1, :], bktok[:, 0, :], bktok[:, 1, :]]
                for n in range(2):
                    act.wait_ge(s["tok_ps"], n + 1)
                    A(act.copy(dsts[n], ps[n][:, :]), "tok_ev")
                act.wait_ge(s["ab_ready"], 1)
                for k in range(QUADS):
                    for M in (Mt, Mm):
                        A(act.copy(M[:, 4 * k:4 * k + 4, :], ident.unsqueeze(1).to_broadcast([P, 4, P])), "eye_ready")
                    if k < 2:
                        act.wait_ge(s["tok_ps"], 3 + k)
                        A(act.copy(dsts[2 + k], ps[6 + k][:, :]), "tok_ev")
                for q in range((LEVELS - 1) * QUADS):
                    act.wait_ge(s["P_ps"], q + 1)
                    A(act.copy(Pb[:, q % 2, :], ps[q % 2][:, :]), "P_ev")
                    if q == 4:
                        compress_act()
                    if q == 10:
                        compress_out()
                for t in range(TT):
                    act.wait_ge(s["rhs_ps"], t + 1)
                    A(act.copy(RH, ps[6][:, :]), "rhs_ev")
                    act.wait_ge(s["sa_ps"], t + 1)
                    A(act.copy(SA, ps[7][:, :]), "sa_ev")
                    act.wait_ge(s["y_ps"], t + 1)
                    A(act.copy(ytok[:, t, :], ps[5][:, :]), "y_ev")

            def compress():
                for n in range(2):
                    act.wait_ge(s["cmp_h"], n + 1)
                    A(act.copy(hrow[0:47, n, :], ps[4 + n][0:47, 0:T]), "cmp_row")

            def compress_act():
                act.wait_ge(s["cmp_hT"], 1)
                for n in range(2):
                    for half in range(2):
                        A(act.copy(small[:, 56:57], ps[6 + n][:, half * 48 + 32:half * 48 + 33]))
                        A(act.activation(hid[:, n, half, 0:30].rearrange("p (g c) -> p g c", g=2), ps[6 + n][:, half * 48:half * 48 + 32].rearrange("p (g c) -> p g c", g=2)[:, :, 0:15],
                                         ACT.Gelu_apprx_tanh, bias=small[:, 56:57]),
                          "cmp_hact" if (n, half) == (1, 1) else "a_step")

            def compress_out():
                act.wait_ge(s["cmp_kv"], 1)
                A(act.copy(kcT[0:64, 0, 0:15], ps[6][0:64, 0:15]))
                A(act.copy(kcT[64:128, 1, 0:15], ps[6][64:128, 15:30]))
                A(act.copy(vc[0:15, :, :], ps[6][0:15, 64:192].rearrange("p (g d) -> p g d", g=2)), "gate_tok")
                act.wait_ge(s["gates_ps"], 1)
                A(act.copy(gtok[:, :, :], ps[7][:, 0:48].rearrange("p (t n) -> p t n", t=2)), "gate_tok")

            def piece(o, j):
                if PIECES[o][j] is None:
                    act.wait_ge(s[("rwkv_ready", "gla_ready")[o]], 2)
                    ins = act.copy(uT_r[0][:, 0:4, :], yT[:, 0:4, :])
                else:
                    t, half, _, bank = PIECES[o][j]
                    act.wait_ge(s["oT_ps"], YT0[o] + sum(p is not None for p in PIECES[o][:j + 1]))
                    ins = act.copy(uT_r[0][:, 4 * half:4 * half + 4, t * P:(t + 1) * P],
                                   ps[bank][:, :].rearrange("p (c n) -> p c n", c=4))
                ins.then_inc(s["y_hi"], 1)

            def out_proj(o, b):
                def w_hi(c):
                    i = b + c // 3
                    act.wait_ge(s[f"land{i % RING}"], 16 * (i // RING + 1))
                    if c >= 3:
                        act.wait_ge(s["op_chunk"], KC * o + c - 2)
                    f = c % 3 * D
                    act.copy(wo_h[o][:, f:f + D], slot(i)[:, f:f + D]).then_inc(s["wo_hi"], 1)
                if o < 2:
                    piece(o, 1)
                w_hi(0)
                if o == 2:
                    piece(o, 2)
                w_hi(1)
                w_hi(2)
                piece(o, len(PIECES[o]) - 1)
                for c in range(3, KC):
                    w_hi(c)

            def attention(kind, beside={}):
                units, b = UN[kind], UB[kind]
                n = len(units)
                for i in range(n + 2):
                    if i in beside:
                        beside[i]()
                    if i < n:
                        u, a = b + i, units[i]
                        act.wait_ge(s["max_ready"], u + 1)
                        if u >= 3:
                            act.wait_ge(s["pT_ps"], u - 2)
                        if u % 8 == 0 and u >= 16:
                            act.wait_ge(s["o_ready"], u // 8 - 1)
                        act.activation(Pp[:, u % 3, 0:a["K"]], SS[:, u % 3, 0:a["K"]], ACT.Exp, scale=-1.0,
                                       bias=nmax[:, u % 4:u % 4 + 1],
                                       accum_out=den[:, u % 16:u % 16 + 1]).then_inc(s["p_ready"], 1)
                    if i >= 2 and i % 2 == 0:
                        u, a = b + i - 2, units[i - 2]
                        act.wait_ge(s["pT_ps"], u + 1)
                        if u >= 2:
                            act.wait_ge(s["o_ps"], u - 1)
                        w = min(P, a["K"])
                        nn = P * -(-a["K"] // P)
                        act.copy(PT[0:w, u % 2, 0:nn], ps[3 + u % 2][0:w, 0:nn]).then_inc(s["pT_ev0"], 1)

            def even_in():
                for n, it in enumerate(EVEN_ITEMS):
                    q = IB["even"] + n
                    act.wait_ge(s["item_ps"], q + 1)
                    bk = ps[4 + q % 4]
                    bank = bk[:, 0:T]
                    if it[0] == "small":
                        A(act.copy(gsm[0:16, :], bk[0:16, 0:T]))
                        A(act.activation(fz[0:8, :], bk[32:40, 0:T], ACT.Identity, bias=C("fox_b")[0:8, :]), "item_ev")
                    elif it[0] == "gz":
                        A(act.activation(gz[:, it[1], :], bank, ACT.Identity, bias=C("gla_b", it[1], it[1] + 1)),
                          "item_ev")
                    elif it[0] == "col":
                        j = it[1]
                        if j < 2:
                            A(act.mul(gqT[:, j, :], bank, HD ** -0.5), "item_ev")
                        elif j < 4:
                            A(act.copy(gkT[:, j - 2, :], bank), "item_ev")
                        elif j < 8:
                            A(act.activation(goT[:, j - 4, :], bank, ACT.Silu), "item_ev")
                        elif j < 12:
                            A(act.mul(fqT[:, j - 8, :], bank, HD ** -0.5), "item_ev")
                        else:
                            if j == 12:
                                act.wait_ge(s["pads_ready"], 5)
                            for g in range(2):
                                r = slice(g * HD, (g + 1) * HD)
                                A(act.copy(fkT[(j - 12) // 2][r, j % 2, g, :], bank[r, :]), "item_ev" if g else "a_step")
                    else:
                        _, t, w = it
                        lo, nn = (0, 256) if w == 0 else (256 + 384 * (w - 1), 384)
                        A(act.copy(evtok[:, t, lo:lo + nn], bk[:, 0:nn]), "item_ev")
                    hi_after("even", n)
                    if it == ("gz", 1):
                        log_gates()
                    if it == ("col", 11):
                        gla_decays()

            def log_gates():
                A(act.activation(gab, gz, ACT.Abs))
                A(act.activation(fab[0:8, :], fz[0:8, :], ACT.Abs))
                A(act.activation(gab, gab, ACT.Exp, scale=-1.0))
                A(act.activation(fab[0:8, :], fab[0:8, :], ACT.Exp, scale=-1.0))
                A(act.activation(gab, gab, ACT.Ln, bias=1.0))
                A(act.activation(fab[0:8, :], fab[0:8, :], ACT.Ln, bias=1.0), "gk_ab")

            def gla_decays():
                act.wait_ge(s["gk_cs"], 1)
                for c in range(2):
                    for t in range(TT):
                        tk = slice(t * P, (t + 1) * P)
                        i = 2 * c + t
                        act.activation(gE1[:, c, tk], gcs[:, c, tk], ACT.Exp, scale=1 / 16.0,
                                       bias=small[:, 64 + i:65 + i]).then_inc(s["e_ready"], 1)
                        act.activation(gE2[:, c, tk], gcs[:, c, tk], ACT.Exp, scale=-1 / 16.0,
                                       bias=small[:, 72 + i:73 + i]).then_inc(s["e_ready"], 1)
                act.activation(small[:, 80:82], small[:, 84:86], ACT.Exp, scale=1 / 16.0).then_inc(s["e_ready"], 1)

            def gla():
                act.wait_ge(s["tok_ps"], 5)
                A(act.copy(gkt, ps[2][:, 0:256].rearrange("p (c n) -> p c n", c=2)), "tok_ev")
                for t in range(TT):
                    act.wait_ge(s["y_ps"], 2 + t + 1)
                    A(act.copy(ogla[:, t, :], ps[1][:, :]), "y_ev")

            def odd_in():
                for n, it in enumerate(ODD_ITEMS):
                    q = IB["odd"] + n
                    act.wait_ge(s["item_ps"], q + 1)
                    bk = ps[4 + q % 4]
                    bank = bk[:, 0:T]
                    j = it[1]
                    if it[0] == "q":
                        A(act.mul(oqT[:, j, :], bank, HD ** -0.5), "item_ev")
                        hi_after("odd", n)
                        for m in (2 * j, 2 * j + 1):
                            K = P * (m // 8 + 1)
                            act.wait_ge(s["idx_ps"], m + 1)
                            if m >= 2:
                                act.wait_ge(s["idx_acc"], m - 1)
                            act.activation(idxs[:, m % 2, 0:K], ps[m % 2][:, 0:K], ACT.Relu).then_inc(s["idx_relu"], 1)
                    elif it[0] == "qi":
                        A(act.mul(qiT[:, j, :], bank, HD ** -0.5), "item_ev")
                    elif it[0] == "ki":
                        act.wait_ge(s["pads_ready"], 6)
                        for g in range(2):
                            r = slice(g * HD, (g + 1) * HD)
                            A(act.copy(kiT[r, g, :], bank[r, :]), "item_ev" if g else "a_step")
                    elif it[0] == "ckv":
                        A(act.copy(ckv[:, j, :], bank), "item_ev")
                        A(act.activation(csc, ckv[:, j, :], ACT.Square, accum_out=small[:, 88 + j:89 + j]), "c_ss")
                    else:
                        A(act.mul(wtok[:, j, :], bk[:, 0:8], 8 ** -0.5), "item_ev")
                    if it[0] != "q":
                        hi_after("odd", n)
                act.wait_ge(s["c_ps"], 1)
                for c in range(2):
                    A(act.mul(cT[:, c, :], ps[3][:, c * T:(c + 1) * T], C("kv_norm", c, c + 1)),
                      "c_ev" if c else "a_step")
                act.wait_ge(s["pads_ready"], 8)
                for n, it in enumerate(UKV_ITEMS):
                    q = IB["ukv"] + n
                    act.wait_ge(s["item_ps"], q + 1)
                    bk = ps[4 + q % 4]
                    if it[0] == "kh":
                        for g in range(2):
                            r = slice(g * HD, (g + 1) * HD)
                            A(act.copy(khT[g][r, it[1], :], bk[r, 0:T]), "item_ev" if g else "a_step")
                    else:
                        A(act.copy(vh[:, it[1], it[2] * 512:(it[2] + 1) * 512], bk[:, :]), "item_ev")

            act.dma_start(cst[:, 0:FIRST], consts_in[:, 0:FIRST]).then_inc(s["first_loaded"], 16)
            gain(0)
            act.wait_ge(s["first_loaded"], 16)
            norm(0)
            w_in()
            compress()
            rwkv()
            attention("nsa", {34: lambda: piece(0, 0)})
            out_proj(0, BASE["w_out"])
            norm(1)
            ffn(0)
            norm(2)
            norm(3)
            ffn(1)
            norm(4)
            act.wait_ge(s["t5_ps"], 1)
            A(act.copy(ffb[0:16, 0:2, :].rearrange("p a b -> p (a b)")[:, 0:384], ps[7][0:16, 0:384]), "t5_sb")
            act.dma_start(scratch, ffb[0:16, 0:2, :].rearrange("p a b -> p (a b)")[:, 0:384]).then_inc(s["t5_out"], 16)
            even_in()
            gla()
            attention("fox", {15: lambda: piece(1, 0)})
            out_proj(1, BASE["even_out"])
            act.wait_ge(s["t5_out"], 16)
            norm(5)
            ffn(2)
            norm(6)
            ffn(3)
            norm(7)
            act.dma_start(bias16, bass.AP(scratch.tensor, 0, [[1, P], [384, 16], [1, T]])).then_inc(s["t5_in"], 16)
            odd_in()
            attention("dsa", {18: lambda: piece(2, 0), 26: lambda: piece(2, 1)})
            out_proj(2, BASE["odd_out"])
            norm(8)
            ffn(4)
            norm(9)

        @block.gpsimd
        def _(gp):
            cnt = {}

            def G(ins, name="g_step"):
                cnt[name] = cnt.get(name, 0) + 1
                ins.then_inc(s[name], 1)
                gp.wait_ge(s[name], cnt[name])

            def rsqrt(o, i, scale, eps, name):
                n = i.shape[1]
                G(gp.tensor_scalar(o, i, scale, eps, ALU.mult, ALU.add))
                G(gp.tensor_tensor(o, o, C("neg_half", 0, n), ALU.pow), name)

            def norm(n):
                for t in range(TT):
                    gp.wait_ge(s["ss_ready"], 2 * n + t + 1)
                    rsqrt(rstd[:, t:t + 1], ss[:, t:t + 1], 1.0, 1e-6, "rstd_ready")

            G(gp.memset(raw[:, :, 0:1], 0.0), "scan_in")
            G(gp.memset(zk[:, 2, :], 0.0), "scan_in")
            G(gp.memset(zv[:, 2, :], 0.0), "scan_in")
            gp.wait_ge(s["first_loaded"], 16)
            norm(0)
            gp.wait_ge(s["masks_loaded"], 16)
            G(gp.tensor_copy(msk[:], W(10240, MASKS)), "masks_ready")
            for k in (ksT, kwT, kcT[:]):
                G(gp.memset(k, 0.0), "pads_ready")
            G(gp.memset(Sst, 0.0))
            gp.wait_ge(s["item_ps"], IB["in"] + len(IN_ITEMS))
            G(gp.memset(AA4[3], 0.0))
            gp.wait_ge(s["ab_ready"], 1)
            for k in range(3):
                G(gp.memset(AA4[k], 0.0), "id_ready")
            for t in range(TT):
                gp.wait_ge(s["var_ready"], t + 1)
                rsqrt(small[:, 96 + 8 * t:104 + 8 * t], small[:, 112 + 8 * t:120 + 8 * t], 1.0 / HD, 64e-5, "grs_ready")
            norm(1)
            norm(2)
            norm(3)
            norm(4)
            for k in fkT:
                G(gp.memset(k, 0.0), "pads_ready")
            gp.wait_ge(s["item_ps"], IB["even"] + len(EVEN_ITEMS))
            G(gp.memset(gA, 0.0), "id_ready")
            G(gp.memset(gS, 0.0), "id_ready")
            for t in range(TT):
                gp.wait_ge(s["var_ready"], 2 + t + 1)
                rsqrt(small[:, 128 + 4 * t:132 + 4 * t], small[:, 136 + 4 * t:140 + 4 * t], 1.0 / P, 1e-6, "grs_ready")
            norm(5)
            norm(6)
            norm(7)
            G(gp.memset(kiT, 0.0), "pads_ready")
            G(gp.memset(khT[0], 0.0), "pads_ready")
            gp.wait_ge(s["xT_ps"], 4 * TN[7] + 4)
            G(gp.memset(khT[1], 0.0), "pads_ready")
            gp.wait_ge(s["c_ss"], 2)
            rsqrt(small[:, 90:92], small[:, 88:90], 1.0 / 256, 1e-6, "c_rs")
            norm(8)
            norm(9)

        @block.vector
        def _(v):
            cnt = {}

            def V(ins, name="v_step"):
                cnt[name] = cnt.get(name, 0) + 1
                ins.then_inc(s[name], 1)
                v.wait_ge(s[name], cnt[name])

            def norm(n, dst=None):
                v.wait_ge(s[f"gain{n % 2}"], 16 * (n // 2 + 1))
                for t in range(TT):
                    v.wait_ge(s["rstd_ready"], 2 * n + t + 1)
                    for half in range(2):
                        hs = slice(half * 512, (half + 1) * 512)
                        V(v.scalar_tensor_tensor((xn if dst is None else dst)[:, t, hs], x[:, t, hs], rstd[:, t:t + 1],
                                                 gb[:, n % 2, hs], ALU.mult, ALU.mult), "xn_ready")
                    if n == 2:
                        v.sem_inc(s["x_done"], 1)
                if n in SPLIT_OF:
                    f = SPLIT_OF[n]
                    if n in (0, 7):
                        lo_block(PROJ_OF[n], 0)
                    for i in range(4):
                        v.wait_ge(s["uT_hi"], 4 * f + i + 1)
                        c0, t = 4 * (i % 2), i // 2
                        v.tensor_tensor(uT_r[1][:, c0:c0 + 4, t * P:(t + 1) * P],
                                        ps[4 + i][:, :].rearrange("p (c n) -> p c n", c=4),
                                        uT_r[0][:, c0:c0 + 4, t * P:(t + 1) * P].bitcast(F32),
                                        ALU.subtract).then_inc(s["uT_lo"], 1)

                if n == 4:
                    v.wait_ge(s["small_hi"], 1)
                    v.tensor_tensor(w_small[1][:, :], C("even_small"), w_small[0][:, :].bitcast(F32),
                                    ALU.subtract).then_inc(s["small_lo"], 1)

            def lo_block(kind, blk):
                i = (BASE[kind_slot(kind)] + blk // 3) % RING
                v.wait_ge(s["hi_blk"], PB[kind] + blk + 1)
                f = blk % 3 * P
                view = lambda r: r[:, i, :].rearrange("p (k f) -> p k f", k=KC)[:, :, f:f + P]
                v.tensor_tensor(view(ring_r), view(ring), w_h[kind][blk // 3 % 2][:, :, f:f + P].bitcast(F32),
                                ALU.subtract).then_inc(s["lo_blk"], 1)

            def lo_a(f, c, r=0):
                q, i = FC * f, BASE[f"ffn{f}"] + c
                v.wait_ge(s["hi_a"], r + (q + c + 1))
                v.tensor_tensor(w_gu[:, c % 2, 1, :], slot(i)[:, 0:2 * D], w_gu[:, c % 2, 0, :].bitcast(F32),
                                ALU.subtract).then_inc(s["lo_a"], 1)

            def lo_b(f, c, r=0):
                q, i = FC * f, BASE[f"ffn{f}"] + c
                v.wait_ge(s["hi_b"], r + (q + c + 1))
                v.tensor_tensor(w_dn[:, c % 2, 1, :], slot(i)[:, 2 * D:3 * D], w_dn[:, c % 2, 0, :].bitcast(F32),
                                ALU.subtract).then_inc(s["lo_b"], 1)
                v.wait_ge(s["lo_b"], r + (q + c + 1))
                v.sem_inc(s[f"free{i % RING}"], 1)

            def residual(scale, first, n, last, m, norm_next):
                if norm_next in AHEAD:
                    if AHEAD[norm_next] == 4:
                        lo_block("even", 0)
                    else:
                        lo_a(FFN_OF[AHEAD[norm_next]], 0)
                for t, (sem, k) in enumerate(((first, n), (last, m))):
                    v.wait_ge(s[sem], k)
                    for half in range(2):
                        xs = x[:, t, half * 512:(half + 1) * 512]
                        V(v.scalar_tensor_tensor(xs, ps[2 * t + half][:, :], scale, xs, ALU.mult, ALU.add),
                          "x_done" if half else "v_step")

            def ffn(f, scale):
                q = FC * f

                def step(c, r=0):
                    n = q + c
                    v.wait_ge(s["silu_ready"], r + (n + 1))
                    h, hr = sg[:, c % 2, :], h_r[:, c % 2, :, :]
                    v.tensor_tensor(h, h, ps[4 + c % 2][:, T:2 * T], ALU.mult).then_inc(s["h_mul"], 1)
                    v.wait_ge(s["h_mul"], r + (n + 1))
                    if n >= 2:
                        v.wait_ge(s["down_done"], r + (n - 1))
                    v.tensor_copy(hr[:, 0, :], h).then_inc(s["h_hi"], 1)
                    v.wait_ge(s["h_hi"], r + (n + 1))
                    v.tensor_tensor(hr[:, 1, :], h, hr[:, 0, :].bitcast(F32), ALU.subtract).then_inc(s["h_ready"], 1)
                    if c + 2 < FC:
                        lo_a(f, c + 2, r)
                    if c + 1 < FC:
                        lo_b(f, c + 1, r)
                lo_b(f, 0)
                lo_a(f, 1)
                step(0)
                step(1)
                with v.Fori(0, 4 * LOOPS, 4) as r:
                    for j in range(4):
                        step(2 + j, r)
                for c in range(2 + 4 * LOOPS, FC):
                    step(c)
                residual(scale, "acc0_done", f + 1, "down_done", q + FC, (2, 4, 6, 7, 9)[f])

            def w_in():
                v.wait_ge(s["scan_in"], 3)
                order = {j: n for n, it in enumerate(IN_ITEMS) if it[0] == "col" for j in [it[1]]}
                dst = [lora[:, 0, :], lora[:, 1, :]] + [m[:, j, :] for m in (pk, pr, pv) for j in range(4)]

                def shift(js):
                    for j in js:
                        v.wait_ge(s["item_ev"], IB["in"] + order[j] + 1)
                        V(v.tensor_tensor(dst[j], raw[:, j % 4, 0:256], raw[:, j % 4, 1:257], ALU.subtract))
                        V(v.scalar_tensor_tensor(dst[j], dst[j], C("mu", j, j + 1), raw[:, j % 4, 1:257],
                                                 ALU.mult, ALU.add), "shift_ready")
                        v.sem_inc(s["raw_free"], 1)
                        if j == 10:
                            v.wait_ge(s["gate_hi"], 1)
                            v.tensor_tensor(w_gate[1][:, :], C("gate_w"), w_gate[0][:, :].bitcast(F32),
                                            ALU.subtract).then_inc(s["gate_lo"], 1)
                lo_block("in", 1)
                lo_block("in", 2)
                for j in range(6):
                    shift([j])
                    lo_block("in", j + 3)
                for c in range(4):
                    V(v.tensor_scalar(kk[:, c, :], pk[:, c, :], C("k_k", c, c + 1), None, ALU.mult))
                V(v.tensor_tensor(tmp, kk, kk, ALU.mult), "kk_sq")
                lo_block("in", 9)
                v.wait_ge(s["n2_ps"], 1)
                for c in range(2):
                    V(v.tensor_scalar(tmp[:, 2 * c:2 * c + 2, :], ps[c][:, :].rearrange("p (a b) -> p a b", a=2),
                                      1e-24, None, ALU.max), "kk_clamped" if c else "v_step")
                shift([6])
                lo_block("in", 10)
                shift([7])
                v.wait_ge(s["kk_sqrt"], 1)
                for c in range(4):
                    V(v.reciprocal(tmp[:, c, :], tmp[:, c, :]))
                    if c == 1:
                        lo_block("in", 11)
                V(v.tensor_tensor(kk, kk, tmp, ALU.mult))
                shift([8])
                lo_block("in", 12)
                for c in range(4):
                    V(v.tensor_scalar(tmp[:, c, :], agm[:, c, :], -1.0, C("k_a", c, c + 1), ALU.add, ALU.mult))
                V(v.scalar_tensor_tensor(kp, tmp, 1.0, pk, ALU.add, ALU.mult))
                shift([9])
                lo_block("in", 13)
                for c in range(4):
                    V(v.scalar_tensor_tensor(tmp[:, c, :], pr[:, c, :], C("r_k", c, c + 1), kp[:, c, :],
                                             ALU.mult, ALU.mult), "rk_ready" if c == 3 else "v_step")
                shift([10])
                lo_block("in", 14)
                shift([11])
                lo_block("in", 15)
                for c in range(4):
                    for t in range(TT):
                        tk = slice(t * P, (t + 1) * P)
                        V(v.tensor_tensor_scan(cs[:, c, tk], C("ones"), sgm[:, c, tk], 0.0, ALU.mult, ALU.add))
                V(v.tensor_tensor(csp, cs, sgm, ALU.subtract))
                mid = cs.rearrange("p c (t n) -> p (c t) n", t=2)
                V(v.tensor_scalar(small[:, 32:40], mid[:, :, 63], DECAY, None, ALU.mult))
                V(v.tensor_scalar(small[:, 40:48], mid[:, :, 63], -DECAY, None, ALU.mult))
                V(v.tensor_tensor(small[:, 52:56], cs[:, :, 127], cs[:, :, 63], ALU.subtract))
                V(v.tensor_tensor(small[:, 52:56], small[:, 52:56], cs[:, :, 191], ALU.add), "csm_ready")
                for j in range(12, 14):
                    shift([j])
                    lo_block("in", j + 4)
                for blk in range(18, BLOCKS["in"]):
                    lo_block("in", blk)
                v.wait_ge(s["item_ps"], IB["in"] + len(IN_ITEMS))
                v.wait_ge(s["e_ready"], 25)
                arv = arT.rearrange("p c t (w n) -> p c t w n", w=2)
                for c in range(4):
                    re = lambda a: a[:, c, :].rearrange("p (t n) -> p t n", t=2)
                    V(v.scalar_tensor_tensor(arv[:, c, :, 0, :], re(kk), -1.0, re(E3), ALU.mult, ALU.mult))
                    V(v.tensor_tensor(arv[:, c, :, 1, :], re(pr), re(E1), ALU.mult))
                V(v.tensor_tensor(bT, kk, agm, ALU.mult))
                V(v.tensor_tensor(bT, bT, E2, ALU.mult))
                V(v.tensor_tensor(kT_, kp, E2, ALU.mult), "ab_ready")

            def rwkv():
                v.wait_ge(s["bon_ps"], 1)
                v.wait_ge(s["tok_ps"], 2)
                for c in range(2):
                    V(v.tensor_tensor(pv[:, 2 * c:2 * c + 2, :], ps[2 + c][:, :].rearrange("p (a b) -> p a b", a=2),
                                      pv[:, 2 * c:2 * c + 2, :], ALU.mult), "bonus_read" if c else "v_step")
                for u in range(RWKV_UNITS):
                    k = u // 4
                    if u % 4 == 0:
                        v.wait_ge(s["id_ready"], min(k + 1, 3))
                        v.wait_ge(s["eye_ready"], 2 * (k + 1))
                    v.wait_ge(s["A_ps"], u + 1)
                    V(v.copy_predicated(Mt[:, u, :], mask(LEVELS), ps[u % 4][:, 0:P]))
                    V(v.copy_predicated(AA4[k][:, u % 4, :], msk[:, 0:512], ps[u % 4][:, :]), "A_read")
                    if u % 4 == 3:
                        for par in range(2):
                            V(v.copy_predicated(Mm[:, 4 * k + par:4 * k + 4:2, :],
                                                mask(0).unsqueeze(1).to_broadcast([P, 2, P]),
                                                ps[4 + 2 * (k % 2) + par][:, 0:256].rearrange("p (u n) -> p u n", u=2)),
                              "M_ready" if par else "v_step")
                for q in range((LEVELS - 1) * QUADS):
                    v.wait_ge(s["dM_ps"], q + 1)
                    lv, qs = q // QUADS + 1, slice(4 * (q % QUADS), 4 * (q % QUADS) + 4)
                    if lv < LEVELS - 1:
                        V(v.copy_predicated(Mm[:, qs, :], mask(lv).unsqueeze(1).to_broadcast([P, 4, P]),
                                            ps[2 + q % 2][:, :].rearrange("p (u n) -> p u n", u=4)))
                    V(v.copy_predicated(Mt[:, qs, :], mask(LEVELS + lv).unsqueeze(1).to_broadcast([P, 4, P]),
                                        ps[4 + q % 2][:, :].rearrange("p (u n) -> p u n", u=4)), "M_ready")
                v.wait_ge(s["s_ps"], 1)
                for hh in range(2):
                    r = slice(hh * HD, (hh + 1) * HD)
                    V(v.tensor_tensor(Sst[r, :, hh * HD:(hh + 1) * HD],
                                      ps[4][r, :].rearrange("p (c n) -> p c n", c=4)[:, :, hh * HD:(hh + 1) * HD],
                                      small[r, 48:52].unsqueeze(2).to_broadcast([HD, 4, HD]), ALU.mult),
                      "s_ev" if hh else "v_step")

            def rwkv_var(t):
                v.wait_ge(s["y_ev"], t + 1)
                yv = ytok[:, t, :].rearrange("p (h n) -> p h n", h=8)
                sq = kk[:, 0:2, :].rearrange("p a (h n) -> p (a h) n", n=HD)
                mean = small[:, 144:152]
                V(v.tensor_reduce(mean, yv, AX.X, ALU.add))
                V(v.tensor_scalar(mean, mean, 1.0 / HD, None, ALU.mult))
                V(v.tensor_tensor(yv, yv, mean.unsqueeze(2).to_broadcast([P, 8, HD]), ALU.subtract))
                V(v.tensor_tensor(sq, yv, yv, ALU.mult))
                V(v.tensor_reduce(small[:, 112 + 8 * t:120 + 8 * t], sq, AX.X, ALU.add), "var_ready")

            def rwkv_norm(t):
                v.wait_ge(s["grs_ready"], t + 1)
                yv = ytok[:, t, :].rearrange("p (h n) -> p h n", h=8)
                V(v.tensor_tensor(yv, yv, small[:, 96 + 8 * t:104 + 8 * t].unsqueeze(2).to_broadcast([P, 8, HD]),
                                  ALU.mult), "yn_ready")

            def rwkv_out(t):
                v.wait_ge(s["ynT_ps"], t + 1)
                tk = slice(t * P, (t + 1) * P)
                for c in range(4):
                    V(v.tensor_scalar(yT[:, c, tk], ps[7][:, c * P:(c + 1) * P], C("lnx_w", c, c + 1),
                                      C("lnx_b", c, c + 1), ALU.mult, ALU.add), "ynT_ev" if c == 3 else "v_step")
                V(v.tensor_tensor(yT[:, 0:4, tk], yT[:, 0:4, tk], pv[:, :, tk], ALU.add))
                V(v.tensor_tensor(yT[:, 0:4, tk], yT[:, 0:4, tk], gg[:, :, tk], ALU.mult), "rwkv_ready")

            def compress():
                v.wait_ge(s["gate_tok"], 2)
                for t in range(TT):
                    gv = gtok[:, t, :].rearrange("p (h b) -> p h b", b=3)[:, :, 0]
                    V(v.tensor_scalar(gv, gv, C("any_ok", t, t + 1), None, ALU.mult), "cmp_ready")

            def attention(kind, beside, before_last):
                units, b = UN[kind], UB[kind]
                n = len(units)

                def result(grp):
                    v.wait_ge(s["o_ps"], 8 * (grp + 1))
                    V(v.reciprocal(rden, den[:, grp % 2 * 8:grp % 2 * 8 + 8]))
                    g = grp - b // 8
                    o = ps[5 + grp % 2][:, :].rearrange("p (h n) -> p h n", h=8)
                    if kind == "nsa":
                        t, br = g // 3, g % 3
                        V(v.tensor_tensor(rden, rden, gtok[:, t, br:24:3], ALU.mult))
                        dst = onsa[:, t, :]
                    elif kind == "fox":
                        br, dst = 0, ofox[:, g, :]
                    else:
                        br, dst = 0, odsa[:, g // 2, g % 2 * 512:(g % 2 + 1) * 512]
                    dst = dst.rearrange("p (h n) -> p h n", h=8)
                    r = rden.unsqueeze(2).to_broadcast([P, 8, HD])
                    if br:
                        V(v.tensor_tensor(obr, o, r, ALU.mult))
                        V(v.tensor_tensor(dst, dst, obr, ALU.add), "o_ready")
                    else:
                        V(v.tensor_tensor(dst, o, r, ALU.mult), "o_ready")

                def transposed(i):
                    u, a = b + i, units[i]
                    v.wait_ge(s["pT_ps"], u + 1)
                    if u >= 2:
                        v.wait_ge(s["o_ps"], u - 1)
                    w = min(P, a["K"])
                    nn = P * -(-a["K"] // P)
                    V(v.tensor_copy(PT[0:w, u % 2, 0:nn], ps[3 + u % 2][0:w, 0:nn]), "pT_ev1")

                for i in range(n):
                    if i in beside:
                        beside[i]()
                    u, a = b + i, units[i]
                    K = a["K"]
                    v.wait_ge(s["S_ps"], u + 1)
                    if u >= 3:
                        v.wait_ge(s["p_ready"], u - 2)
                    V(v.tensor_tensor_reduce(SS[:, u % 3, 0:K], ps[u % 3][:, 0:K], a["dist"], -a["scale"], 3e38,
                                             ALU.add, ALU.min, nmax[:, u % 4:u % 4 + 1]), "max_ready")
                    if i >= 2 and i % 2:
                        transposed(i - 2)
                    if i % 8 == 4 and i > 8:
                        result(u // 8 - 1)
                transposed(n - 1)
                before_last()
                result((b + n) // 8 - 1)

            def piece(o, j):
                v.wait_ge(s["y_hi"], Y0[o] + j + 1)
                if PIECES[o][j] is None:
                    ins = v.tensor_tensor(uT_r[1][:, 0:4, :], yT[:, 0:4, :], uT_r[0][:, 0:4, :].bitcast(F32),
                                          ALU.subtract)
                else:
                    t, half, _, bank = PIECES[o][j]
                    at_ = (slice(None), slice(4 * half, 4 * half + 4), slice(t * P, (t + 1) * P))
                    ins = v.tensor_tensor(uT_r[1][at_], ps[bank][:, :].rearrange("p (c n) -> p c n", c=4),
                                          uT_r[0][at_].bitcast(F32), ALU.subtract)
                ins.then_inc(s["y_lo"], 1)

            def w_lo(o, b, c):
                v.wait_ge(s["wo_hi"], KC * o + c + 1)
                i, f = (b + c // 3) % RING, c % 3 * D
                v.tensor_tensor(ring_r[:, i, f:f + D], ring[:, i, f:f + D], wo_h[o][:, f:f + D].bitcast(F32),
                                ALU.subtract).then_inc(s["wo_lo"], 1)

            def first_parts(o, b):
                if o < 2:
                    piece(o, 1)
                w_lo(o, b, 0)
                w_lo(o, b, 1)

            def out_proj(o, b):
                if o == 2:
                    piece(o, 2)
                w_lo(o, b, 2)
                piece(o, len(PIECES[o]) - 1)
                for c in range(3, KC):
                    w_lo(o, b, c)
                residual(1.0, "op_acc", 2 * o + 1, "op_acc", 2 * o + 2, (1, 5, 8)[o])

            def even_in():
                for blk in range(1, 10):
                    lo_block("even", blk)
                v.wait_ge(s["item_ev"], IB["even"] + EVEN_ITEMS.index(("gz", 1)) + 1)
                V(v.tensor_scalar(gmn, gz, 0.0, None, ALU.min))
                V(v.tensor_scalar(fmn[0:8, :], fz[0:8, :], 0.0, None, ALU.min))
                v.wait_ge(s["gk_ab"], 1)
                V(v.tensor_tensor(gmn, gmn, gab, ALU.subtract))
                V(v.tensor_tensor(fmn[0:8, :], fmn[0:8, :], fab[0:8, :], ALU.subtract))
                for t in range(TT):
                    V(v.tensor_tensor_scan(fsum[0:8, t * P:(t + 1) * P], C("ones")[0:8, :],
                                           fmn[0:8, t * P:(t + 1) * P],
                                           fsum[0:8, t * P - 1:t * P] if t else 0.0, ALU.mult, ALU.add),
                      "v_step")
                V(v.tensor_scalar(fneg[0:8, :], fsum[0:8, :], -1.0, None, ALU.mult))
                for c in range(2):
                    for t in range(TT):
                        tk = slice(t * P, (t + 1) * P)
                        V(v.tensor_tensor_scan(gcs[:, c, tk], C("ones"), gmn[:, c, tk], 0.0, ALU.mult, ALU.add))
                mid = gcs.rearrange("p c (t n) -> p (c t) n", t=2)
                V(v.tensor_scalar(small[:, 64:68], mid[:, :, 63], -1 / 16.0, None, ALU.mult))
                V(v.tensor_scalar(small[:, 72:76], mid[:, :, 63], 1 / 16.0, None, ALU.mult))
                V(v.tensor_tensor(small[:, 84:86], gcs[:, :, 127], gcs[:, :, 63], ALU.subtract))
                V(v.tensor_tensor(small[:, 84:86], small[:, 84:86], gcs[:, :, 191], ALU.add), "gk_cs")
                for blk in range(10, 18):
                    lo_block("even", blk)
                v.wait_ge(s["e_ready"], 25 + 9)
                V(v.tensor_tensor(gqd, gqT, gE1, ALU.mult))
                V(v.tensor_tensor(gkd, gkT, gE2, ALU.mult), "gla_k")
                for blk in range(18, BLOCKS["even"]):
                    lo_block("even", blk)

            def gla():
                v.wait_ge(s["id_ready"], 5)
                for t in range(TT):
                    v.wait_ge(s["A_ps"], RWKV_UNITS + t + 1)
                    if t:
                        v.wait_ge(s["y_ps"], 3)
                    for par in range(2):
                        V(v.copy_predicated(gA[:, par:4:2, :], msk[:, P:2 * P].unsqueeze(1).to_broadcast([P, 2, P]),
                                            ps[4 + par][:, 0:256].rearrange("p (h n) -> p h n", h=2)),
                          "A_read" if par else "v_step")
                    if not t:
                        v.wait_ge(s["s_ps"], 2)
                        for hh in range(2):
                            r = slice(hh * HD, (hh + 1) * HD)
                            for c in range(2):
                                V(v.tensor_scalar(gS[r, c, hh * P:(hh + 1) * P],
                                                  ps[6][r, c * 256 + hh * P:c * 256 + (hh + 1) * P],
                                                  small[r, 80 + c:81 + c], None, ALU.mult),
                                  "s_ev" if (hh, c) == (1, 1) else "v_step")

            def gla_var(t):
                v.wait_ge(s["y_ev"], 3 + t)
                yv = ogla[:, t, :].rearrange("p (h n) -> p h n", h=4)
                sq = gsq.rearrange("p (h n) -> p h n", h=4)
                V(v.tensor_tensor(sq, yv, yv, ALU.mult))
                V(v.tensor_reduce(small[:, 136 + 4 * t:140 + 4 * t], sq, AX.X, ALU.add), "var_ready")

            def gla_norm(t):
                v.wait_ge(s["grs_ready"], 3 + t)
                yv = ogla[:, t, :].rearrange("p (h n) -> p h n", h=4)
                V(v.tensor_tensor(yv, yv, small[:, 128 + 4 * t:132 + 4 * t].unsqueeze(2).to_broadcast([P, 4, P]),
                                  ALU.mult), "yn_ready")

            def gla_out(t):
                v.wait_ge(s["ynT_ps"], 3 + t)
                tk = slice(t * P, (t + 1) * P)
                V(v.scalar_tensor_tensor(yT[:, 0:4, tk], ps[7][:, :].rearrange("p (c n) -> p c n", c=4),
                                         C("gla_norm"), goT[:, :, tk], ALU.mult, ALU.mult), "gla_ready")

            def odd_in():
                for blk in range(1, 7):
                    lo_block("odd", blk)
                v.wait_ge(s["c_rs"], 1)
                for t in range(TT):
                    V(v.tensor_scalar(ckv[:, t, :], ckv[:, t, :], small[:, 90 + t:91 + t], None, ALU.mult),
                      "c_n" if t else "v_step")
                for t in range(TT):
                    K = P * (t + 1)
                    for h in range(8):
                        n = 8 * t + h
                        if n == 0:
                            for blk in range(7, 14):
                                lo_block("odd", blk)
                        if n == 2:
                            lo_block("odd", 14)
                        v.wait_ge(s["idx_relu"], n + 1)
                        rl, sc = idxs[:, n % 2, 0:K], score[:, 0:K]
                        if h:
                            V(v.scalar_tensor_tensor(sc, rl, wtok[:, t, h:h + 1], sc, ALU.mult, ALU.add), "idx_acc")
                        else:
                            V(v.tensor_scalar(sc, rl, wtok[:, t, h:h + 1], None, ALU.mult), "idx_acc")
                    causal = C("causal", P * (1 - t), P * (1 - t) + K)
                    V(v.tensor_tensor(sc, sc, causal, ALU.add))
                    for r in range(TOPK // 8):
                        V(v.max(small[:, 152:160], sc))
                        V(v.match_replace(sc, small[:, 152:160], sc, -3e38))
                    V(v.tensor_scalar(sc, sc, -2e38, NEG, ALU.is_gt, ALU.mult))
                    V(v.tensor_tensor(selm[:, t, 0:K], sc, causal, ALU.add), "sel_ready")

            norm(0)
            w_in()
            rwkv()
            compress()
            rwkv_var(0)
            attention("nsa", {1: lambda: rwkv_norm(0), 3: lambda: rwkv_var(1), 5: lambda: rwkv_norm(1),
                              9: lambda: rwkv_out(0), 20: lambda: rwkv_out(1), 35: lambda: piece(0, 0)},
                      lambda: first_parts(0, BASE["w_out"]))
            out_proj(0, BASE["w_out"])
            norm(1)
            ffn(0, 1.0)
            norm(2, x)
            norm(3)
            ffn(1, 0.5)
            norm(4)
            even_in()
            gla()
            attention("fox", {0: lambda: gla_var(0), 1: lambda: gla_var(1), 3: lambda: gla_norm(0),
                              4: lambda: gla_norm(1), 8: lambda: gla_out(0), 11: lambda: gla_out(1),
                              15: lambda: piece(1, 0)}, lambda: first_parts(1, BASE["even_out"]))
            out_proj(1, BASE["even_out"])
            norm(5)
            ffn(2, 0.5)
            norm(6)
            ffn(3, 0.5)
            norm(7)
            odd_in()
            attention("dsa", {19: lambda: piece(2, 0), 27: lambda: piece(2, 1)}, lambda: first_parts(2, BASE["odd_out"]))
            out_proj(2, BASE["odd_out"])
            norm(8)
            ffn(4, 0.5)
            norm(9, x)


def column_blocks(w, cols, width=3 * P):
    cols = np.concatenate([cols, np.full((-len(cols)) % width, -1)])
    w = np.concatenate([w, np.zeros((w.shape[0], 1), w.dtype)], axis=1)[:, cols]
    return [np.ascontiguousarray(w[:, i:i + width].reshape(KC, P, width).transpose(1, 0, 2)).reshape(P, SLOT)
            for i in range(0, len(cols), width)]


def row_blocks(w):
    w = np.concatenate([w, np.zeros((P, D), w.dtype)]).reshape(3, 3, P, D)
    return [np.ascontiguousarray(w[i].transpose(1, 0, 2)).reshape(P, SLOT) for i in range(3)]


def ffn_slots(gate, up, down):
    g, u = (m.reshape(KC, P, FC, P).transpose(2, 1, 0, 3).reshape(FC, P, D) for m in (gate, up))
    return list(np.concatenate([g, u, down.reshape(FC, P, D)], axis=2))


def padded(a, n=SLOT):
    return np.concatenate([a, np.zeros((P, n - a.shape[1]), a.dtype)], axis=1)


def rows(a):
    return np.concatenate([a, np.zeros((P - a.shape[0], a.shape[1]), a.dtype)])


def columns(vec):
    return np.ascontiguousarray(vec.reshape(-1, P).T)


def lay_out(i):
    r = np.arange
    w_in, od, ev = i["w_in"][0], i["odd_w_in_2"][0], i["even_w_in_2"][0]
    q0 = 1792
    rwkv = np.concatenate([r(1536, 1792), r(512, 1024), r(0, 512), r(1024, 1536)])
    q = np.concatenate([q0 + h * HD + r(HD) for j in range(4) for h in (j, j + 4)])
    kv = q0 + 512
    in_cols = np.concatenate([rwkv, q, kv + r(256), kv + 256 + r(128), kv + 512 + r(128), kv + 384 + r(128),
                              kv + 640 + r(128)])
    slots = column_blocks(w_in, in_cols)
    pieces = np.concatenate([i["nsa_cmp_k_w1"][0], i["nsa_cmp_v_w1"][0]]).reshape(32, P, 256)
    for a in range(0, 32, 12):
        slots.append(padded(pieces[a:a + 12].transpose(1, 0, 2).reshape(P, -1)))
    slots += row_blocks(i["w_out"][0])
    slots += ffn_slots(i["ffn_w_gate"][0], i["ffn_w_up"][0], i["ffn_w_down"][0])
    f_in, f_out = i["ffn_w_in_2"], i["ffn_w_out_2"]

    def ffn2(layer, n):
        return ffn_slots(f_in[layer, n][:, :F], f_in[layer, n][:, F:], f_out[layer, n])
    slots += ffn2(0, 0)
    e_cols = np.concatenate([r(0, 512), 1024 + r(512), 1552 + r(1024), 512 + r(512), 2576 + r(512)])
    slots += column_blocks(ev, e_cols)
    slots += row_blocks(i["even_w_out_2"][0])
    slots += ffn2(0, 1) + ffn2(1, 0)
    o_cols = np.concatenate([1792 + r(64), 1792 + r(64), 1024 + r(256), 1280 + r(512), r(1024)])
    slots += column_blocks(od, o_cols)
    uk = i["mla_w_uk_2"][0].transpose(2, 0, 1).reshape(2, P, D).transpose(1, 0, 2).reshape(P, 2 * D)
    uv = i["mla_w_uv_2"][0].transpose(1, 0, 2).reshape(2, P, D).transpose(1, 0, 2).reshape(P, 2 * D)
    slots += [padded(uk), padded(uv)]
    slots += row_blocks(i["odd_w_out_2"][0])
    slots += ffn2(1, 1)
    wstream = np.stack(slots)
    assert wstream.shape == (NSLOTS, P, SLOT)

    gains = [i["norm1_g"][0], i["norm2_g"][0], i["norm_f_g"]] + [i["norm_g_2"][a, b] for a in range(2) for b in range(3)]
    gains = np.concatenate(gains + [i["final_norm_g_2"]])
    gains = np.ascontiguousarray(np.broadcast_to(gains, (P, gains.size)))

    def small_w(w, cols):
        return w[:, cols].reshape(KC, P, len(cols)).transpose(1, 0, 2).reshape(P, -1)

    z64 = np.zeros((64, 512), np.float32)
    ck2 = i["nsa_cmp_k_w2"][0].reshape(2, P, HD).transpose(1, 0, 2)
    cv2 = i["nsa_cmp_v_w2"][0].reshape(2, P, HD).transpose(1, 0, 2).reshape(P, P)
    p_, c_ = np.arange(P)[:, None], np.arange(T)[None, :]
    dist = P + p_ - c_
    causal = np.where(dist >= 0, 0.0, NEG)
    end = np.arange(16)[None, :] * CMP_STRIDE + 31
    cmp_d = np.concatenate([np.where(end <= t * P + p_, -np.abs(t * P + p_ - end).astype(np.float64), NEG)
                            for t in range(TT)], axis=1)
    d = np.maximum(255 - np.arange(384), 0)
    large = 16 + (np.log(np.maximum(d, 1) / 16) / np.log(8.0) * 16 + 1e-9).astype(np.int64)
    bucket = np.where(d < 16, d, np.minimum(large, 31))
    c = {
        "ident": np.eye(P), "reverse": np.eye(P)[::-1], "pair_ones": np.kron(np.eye(2), np.ones((HD, HD))), "ones": np.ones((P, P)),
        "w2": np.concatenate([i["rwkv_w2"][0], z64]), "a2": np.concatenate([z64, i["rwkv_a2"][0]]),
        "g2": i["rwkv_g2"][0], "gate_w": small_w(w_in, q0 + 1280 + r(24)),
        "even_small": small_w(np.concatenate([ev, np.zeros((D, 1), ev.dtype)], axis=1),
                              np.concatenate([1536 + r(16), np.full(16, -1), 3088 + r(8)])), "odd_small": small_w(od, 1856 + r(8)),
        "gla_gate": rows(i["gla_w_gate_2"][0]), "ck2": np.concatenate([ck2, ck2], axis=2).reshape(P, 256), "cv2": cv2,
        "pe_k": i["nsa_pe_k"][0].reshape(16, P).T, "pe_v": i["nsa_pe_v"][0].reshape(16, P).T,
        "t5": rows(i["t5_table_2"]), "t5_onehot": rows((bucket[None, :] == np.arange(32)[:, None]).astype(np.float32)),
        "alibi": np.where(dist >= 0, -dist, NEG), "alibi_cmp": cmp_d,
        "any_ok": np.concatenate([(p_ + t * P >= 31).astype(np.float32) for t in range(TT)], axis=1),
        "causal": causal, "neg_half": np.full((P, 32), -0.5),
        "mu": columns(i["mu_shift"][0][rwkv]), "w0": columns(i["rwkv_w0"][0]), "a0": columns(i["rwkv_a0"][0]),
        "k_k": columns(i["rwkv_k_k"][0]), "k_a": columns(i["rwkv_k_a"][0]), "r_k": columns(i["rwkv_r_k"][0].reshape(-1)),
        "lnx_w": columns(i["rwkv_lnx_w"][0]), "lnx_b": columns(i["rwkv_lnx_b"][0]), "gla_b": columns(i["gla_b_gate_2"][0]),
        "gla_norm": columns(i["gla_norm_g_2"][0]), "fox_b": rows(i["fox_b_f_2"][0][:, None]),
        "q_scale": HD ** -0.5 * 2.0 ** (1 + np.arange(4)[None, :] + 4 * (p_ // HD)),
        "kv_norm": columns(i["mla_kv_norm_g_2"][0]),
    }
    for name, n in CONSTS:
        assert c[name].shape == (P, n), (name, c[name].shape)
    consts = np.concatenate([c[name].astype(np.float32) for name, _ in CONSTS], axis=1)
    strict, incl = (p_ < p_.T), (p_ <= p_.T)
    below = [((p_ // b) % 2 == 1) & (p_.T // b == p_ // b - 1) for b in (1 << lv for lv in range(LEVELS))]
    masks = np.concatenate([strict, incl, strict, incl] + below + [m.T for m in below], axis=1).astype(np.float32)
    return {"x_in": np.ascontiguousarray(i["x"][0]), "wstream": wstream, "gains": gains, "consts_in": consts,
            "masks_in": masks}


def kernel(**inputs):
    import concourse.bacc as bacc
    from concourse.bass_utils import run_bass_kernel_spmd
    arrays = lay_out({k: np.asarray(v) for k, v in inputs.items()})
    nc = bacc.Bacc("TRN2", target_bir_lowering=False, num_devices=1)
    args = {n: nc.dram_tensor(n, a.shape, F32, kind="ExternalInput").ap() for n, a in arrays.items()}
    scratch = nc.dram_tensor("t5_row", (16, 384), F32, kind="Internal").ap()
    out = nc.dram_tensor("out_dram", (T, D), F32, kind="ExternalOutput").ap()
    build(nc, **args, scratch=scratch, out=out)
    r = run_bass_kernel_spmd(nc, [arrays], core_ids=[0])
    return r.results[0]["out_dram"].reshape(1, T, D)
```
